# Optimizing a Trainium2 kernel written in Bass

```python
import jax, jax.numpy as jnp
from jax import lax
import numpy as np

D_MODEL = 1024
BATCH = 1
SEQ = 1024
DEPTH = 2

N_A_LAYERS = DEPTH // 2
N_B_LAYERS = DEPTH - N_A_LAYERS
POOL_WINDOWS = (2, 4, 8, 16)
N_POOL_GROUPS = len(POOL_WINDOWS)
POOL_GROUP = D_MODEL // N_POOL_GROUPS
HEAD_DIM = 64
N_HEADS = D_MODEL // HEAD_DIM
N_KV_HEADS = 4
GQA_GROUP = N_HEADS // N_KV_HEADS
WINDOW = 128
BLOCK = 128
ROPE_THETA = 10000.0
D_FF = ((8 * D_MODEL + 3 * 256 - 1) // (3 * 256)) * 256
PLE_DIM = 256
RMS_EPS = 1e-6
NEG_INF = -1e30

kernel_name = "yoco_pool_swa_sink_hybrid"

def rms_norm(x, g):
    xf = x.astype(jnp.float32)
    y = xf * lax.rsqrt(jnp.mean(xf * xf, axis=-1, keepdims=True) + RMS_EPS)
    return (y * g.astype(jnp.float32)).astype(x.dtype)

def rope_tables(seq):
    inv = 1.0 / (ROPE_THETA ** (jnp.arange(0, HEAD_DIM, 2, dtype=jnp.float32) / HEAD_DIM))
    ang = jnp.arange(seq, dtype=jnp.float32)[:, None] * inv[None, :]
    return jnp.cos(ang), jnp.sin(ang)

def apply_rope(x, cos, sin):
    xf = x.astype(jnp.float32)
    half = HEAD_DIM // 2
    x1, x2 = xf[..., :half], xf[..., half:]
    c = cos[None, :, None, :]
    s = sin[None, :, None, :]
    return jnp.concatenate([x1 * c - x2 * s, x2 * c + x1 * s], axis=-1).astype(x.dtype)

def multiscale_pool(x, w_pool, pool_scale):
    b, s, _ = x.shape
    xf = x.astype(jnp.float32).reshape(b, s, N_POOL_GROUPS, POOL_GROUP)
    cs = jnp.cumsum(xf, axis=1)
    t = jnp.arange(s)
    pooled = []
    for g, w in enumerate(POOL_WINDOWS):
        csg = cs[:, :, g]
        lower = jnp.concatenate([jnp.zeros((b, w, POOL_GROUP), jnp.float32), csg[:, :s - w]], axis=1)
        cnt = jnp.minimum(t + 1, w).astype(jnp.float32)[None, :, None]
        pooled.append((csg - lower) / cnt - xf[:, :, g])
    pooled = jnp.stack(pooled, axis=2).astype(x.dtype)
    y = jnp.einsum('bsgc,gcd->bsgd', pooled, w_pool).reshape(b, s, D_MODEL)
    return y * pool_scale

def sliding_window_sink_attention(q, k, v, sinks):
    b, s = q.shape[0], q.shape[1]
    nb = s // BLOCK
    qb = q.reshape(b, nb, BLOCK, N_KV_HEADS, GQA_GROUP, HEAD_DIM)

    def band(t):
        tb = t.reshape(b, nb, BLOCK, N_KV_HEADS, HEAD_DIM)
        prev = jnp.concatenate([jnp.zeros_like(tb[:, :1]), tb[:, :-1]], axis=1)
        return jnp.concatenate([prev, tb], axis=2)

    kb, vb = band(k), band(v)
    scores = jnp.einsum('bnqkgd,bnskd->bnkgqs', qb, kb).astype(jnp.float32) * (HEAD_DIM ** -0.5)
    blk = jnp.arange(nb)[:, None, None] * BLOCK
    qpos = blk + jnp.arange(BLOCK)[None, :, None]
    kpos = blk - BLOCK + jnp.arange(2 * BLOCK)[None, None, :]
    diff = qpos - kpos
    valid = (diff >= 0) & (diff < WINDOW) & (kpos >= 0)
    scores = jnp.where(valid[None, :, None, None], scores, NEG_INF)
    sink = sinks.astype(jnp.float32).reshape(N_KV_HEADS, GQA_GROUP)[None, None, :, :, None, None]
    sink = jnp.broadcast_to(sink, scores.shape[:-1] + (1,))
    probs = jax.nn.softmax(jnp.concatenate([scores, sink], axis=-1), axis=-1)[..., :-1]
    out = jnp.einsum('bnkgqs,bnskd->bnqkgd', probs.astype(v.dtype), vb)
    return out.reshape(b, s, N_HEADS * HEAD_DIM)

def swiglu(x, w_gate, w_up, w_down):
    return (jax.nn.silu(x @ w_gate) * (x @ w_up)) @ w_down

def setup_inputs(seed: int = 0) -> dict:
    key = jax.random.key(seed)
    ks = jax.random.split(key, 20)
    f32 = jnp.float32

    def nrm(k, shape, fan_in):
        return jax.random.normal(k, shape, f32) * (fan_in ** -0.5)

    def gain(k, shape):
        return 1.0 + 0.05 * jax.random.normal(k, shape, f32)

    return {
        "x": jax.random.normal(ks[0], (BATCH, SEQ, D_MODEL), f32),
        "p": jax.random.normal(ks[1], (DEPTH, BATCH, SEQ, PLE_DIM), f32),
        "mix_pre_g": gain(ks[2], (DEPTH, D_MODEL)),
        "mix_post_g": gain(ks[3], (DEPTH, D_MODEL)),
        "ffn_pre_g": gain(ks[4], (DEPTH, D_MODEL)),
        "ffn_post_g": gain(ks[5], (DEPTH, D_MODEL)),
        "pool_w": nrm(ks[6], (N_A_LAYERS, N_POOL_GROUPS, POOL_GROUP, POOL_GROUP), POOL_GROUP),
        "pool_scale": 1.0 + 0.1 * jax.random.normal(ks[7], (N_A_LAYERS, D_MODEL), f32),
        "kv_norm_g": gain(ks[8], (D_MODEL,)),
        "w_k": nrm(ks[9], (D_MODEL, N_KV_HEADS * HEAD_DIM), D_MODEL),
        "w_v": nrm(ks[10], (D_MODEL, N_KV_HEADS * HEAD_DIM), D_MODEL),
        "w_q": nrm(ks[11], (N_B_LAYERS, D_MODEL, N_HEADS * HEAD_DIM), D_MODEL),
        "w_o": nrm(ks[12], (N_B_LAYERS, N_HEADS * HEAD_DIM, D_MODEL), N_HEADS * HEAD_DIM),
        "sinks": 0.5 * jax.random.normal(ks[13], (N_B_LAYERS, N_HEADS), f32),
        "w_ff_gate": nrm(ks[14], (DEPTH, D_MODEL, D_FF), D_MODEL),
        "w_ff_up": nrm(ks[15], (DEPTH, D_MODEL, D_FF), D_MODEL),
        "w_ff_down": nrm(ks[16], (DEPTH, D_FF, D_MODEL), D_FF),
        "ple_norm_g": gain(ks[17], (DEPTH, D_MODEL)),
        "w_ple_gate": nrm(ks[18], (DEPTH, D_MODEL, D_MODEL), D_MODEL),
        "w_ple_proj": nrm(ks[19], (DEPTH, PLE_DIM, D_MODEL), PLE_DIM),
    }

def reference(x, p, mix_pre_g, mix_post_g, ffn_pre_g, ffn_post_g, pool_w, pool_scale,
              kv_norm_g, w_k, w_v, w_q, w_o, sinks, w_ff_gate, w_ff_up, w_ff_down,
              ple_norm_g, w_ple_gate, w_ple_proj):
    b, s, _ = x.shape
    cos, sin = rope_tables(s)
    h = x
    k_shared = None
    v_shared = None
    for i in range(DEPTH):
        hn = rms_norm(h, mix_pre_g[i])
        if i < N_A_LAYERS:
            m = multiscale_pool(hn, pool_w[i], pool_scale[i])
        else:
            j = i - N_A_LAYERS
            q = apply_rope((hn @ w_q[j]).reshape(b, s, N_HEADS, HEAD_DIM), cos, sin)
            m = sliding_window_sink_attention(q, k_shared, v_shared, sinks[j]) @ w_o[j]
        h = h + rms_norm(m, mix_post_g[i])
        f = swiglu(rms_norm(h, ffn_pre_g[i]), w_ff_gate[i], w_ff_up[i], w_ff_down[i])
        h = h + rms_norm(f, ffn_post_g[i])
        gate = jax.nn.sigmoid(rms_norm(h, ple_norm_g[i]) @ w_ple_gate[i])
        h = h + (p[i] @ w_ple_proj[i]) * gate
        if i == N_A_LAYERS - 1:
            hk = rms_norm(h, kv_norm_g)
            k_shared = apply_rope((hk @ w_k).reshape(b, s, N_KV_HEADS, HEAD_DIM), cos, sin)
            v_shared = (hk @ w_v).reshape(b, s, N_KV_HEADS, HEAD_DIM)
    return h


_drawn_inputs = setup_inputs


def setup_inputs(seed=0):
    import zlib

    import numpy as np

    out = dict(_drawn_inputs(seed))
    spreads = {}
    factors = {'sinks': 8.0, 'ple_norm_g': 6.444}
    for name, (base, spread) in spreads.items():
        noise = np.random.default_rng([zlib.crc32(name.encode()), seed]).standard_normal(out[name].shape)
        drawn = base * np.exp(spread * noise) if base else spread * noise
        out[name] = __import__('jax').numpy.asarray(drawn.astype(out[name].dtype))
    for name, factor in factors.items():
        out[name] = (out[name] * factor).astype(out[name].dtype)
    return out
```

```python
from contextlib import ExitStack

import numpy as np
import concourse.bass as bass
from concourse import mybir

P = 128
F32 = mybir.dt.float32
F32R = mybir.dt.float32r
BF16 = mybir.dt.bfloat16
ALU = mybir.AluOpType
ACT = mybir.ActivationFunctionType
AX = mybir.AxisListType

D = 1024
SEQ = 1024
TILES = SEQ // P
PAIRS = TILES // 2
KD = D // P
HALF = 512
HEAD = 64
HEADS = D // HEAD
KV_HEADS = 4
GQA = HEADS // KV_HEADS
WINDOWS = (2, 4, 8, 16)
LONGEST = max(WINDOWS)
D_FF = 2816
GROUP = 256
GROUPS = D_FF // GROUP
PLE = 256
EPS = 1e-6
NEG = -1e30
SLOTS = 6
STEPS = [(0, 0), (1, 0), (0, 1), (1, 1)]


def constants():
    s, t = np.arange(P)[:, None], np.arange(P)[None, :]
    first, inner, before = [], [], []
    for w in WINDOWS:
        near = (t >= s) & (t - s < w)
        first.append(near / np.minimum(t + 1, w).astype(np.float32) - (s == t))
        inner.append(near / np.float32(w) - (s == t))
        before.append(((t + P - s < w) / np.float32(w))[:, :LONGEST])
    inv = (1.0 / (10000.0 ** (np.arange(0, HEAD, 2, dtype=np.float32) / np.float32(HEAD)))).astype(np.float32)
    angle = np.arange(SEQ, dtype=np.float32)[:, None] * inv[None, :]
    angle = angle.reshape(TILES, P, HEAD // 2).transpose(1, 0, 2)
    q, k = np.arange(P)[:, None], np.arange(-P, P)[None, :]
    valid = (q - k >= 0) & (q - k < P)
    mask = np.stack([np.where(valid & (k >= 0), 0.0, NEG), np.where(valid, 0.0, NEG)], axis=1)
    out = {
        "identity": np.eye(P),
        "band_first": np.stack(first, 1), "band_inner": np.stack(inner, 1), "band_before": np.stack(before, 1),
        "rope_cos": np.cos(angle), "rope_sin": np.sin(angle), "mask": mask,
    }
    return {k: np.ascontiguousarray(v, dtype=np.float32) for k, v in out.items()}


def done(i):
    return i + 2


def free(i):
    return i + 1


def trunk(nc, I, out):
    ctx = ExitStack()
    with ctx:
        credited = []

        def sem(name):
            return ctx.enter_context(nc.semaphore(name))

        def sem_c(name):
            s = sem(name)
            credited.append(s)
            return s

        families, rounds = {}, {}

        class Phase:

            def __init__(self, *events, count=PAIRS):
                self.base = {}
                for e in events:
                    if e not in families:
                        families[e], rounds[e] = [sem_c(f"{e}{p}") for p in range(2)], 0
                    self.base[e] = rounds[e]
                    rounds[e] += count

            def __getitem__(self, e):
                return families[e]

            def done(self, e, i):
                return done(self.base[e] + i)

            def free(self, e, i):
                return free(self.base[e] + i)

        def sb(name, shape, dt=F32):
            return ctx.enter_context(nc.sbuf_tensor(name, shape, dt))

        def region(name, elements, *uses):
            views = {}
            for use in uses:
                with ExitStack() as inner:
                    for n, shape, dt in use:
                        views[n] = inner.enter_context(nc.sbuf_tensor(n, shape, dt))
            sb(name, [P, elements])
            return views

        H = sb("H", [P, TILES * D])
        raw = [sb(f"raw{i}", [P, D]) for i in range(SLOTS)]
        xn = [sb(f"xn{p}", [P, D]) for p in range(2)]
        tmp = sb("tmp", [P, D])
        gain = sb("gain", [P, D])
        ident = sb("ident", [P, P])
        small = sb("small", [P, 64])
        sinks = sb("sinks_row", [P, HEADS])

        def weights(name, shape):
            return [(name + "_hi", shape, F32R), (name + "_lo", shape, F32R)]

        A = region("A", 16 * D,
                   weights("xT", [P, KD, SEQ]),
                   weights("w_ple_gate0", [P, KD, D]), weights("w_ple_gate1", [P, KD, D]),
                   weights("w_q", [P, KD, D]), weights("w_o", [P, KD, D]), [("pool_squares", [P, 2, D], F32)])
        B = region("B", 8 * D,
                   weights("wg", [P, KD, GROUP]) + weights("wu", [P, KD, GROUP]),
                   weights("w_kv", [P, KD, 2 * GROUP]),
                   [("pool_m0", [P, D], F32), ("pool_m1", [P, D], F32)],
                   [("qo", [P, TILES, D], F32)])
        C = region("C", 8 * D,
                   weights("wd", [P, 2, D]) + weights("a", [P, 2, SEQ]),
                   weights("w_ple_proj", [P, 2, D]) + weights("pT0", [P, 2, P]) + weights("pT1", [P, 2, P])
                   + [("p_raw0", [P, 2, P], F32), ("p_raw1", [P, 2, P], F32)],
                   weights("w_pool", [P, KD, GROUP])
                   + [("band_first", [P, 4, P], F32), ("band_inner", [P, 4, P], F32),
                      ("band_before", [P, 4, LONGEST], F32), ("scale_row", [P, D], F32)],
                   [("kT", [P, TILES + 1, KV_HEADS, P], F32), ("V", [P, TILES + 1, GROUP], F32),
                    ("mask0", [P, 2 * P], F32), ("mask1", [P, 2 * P], F32),
                    ("cos", [P, TILES, 32], F32), ("sin", [P, TILES, 32], F32)],
                   [("o_squares", [P, 2, D], F32)])
        DD = region("DD", 4 * D,
                    weights("xt0", [P, KD, P]) + weights("xt1", [P, KD, P]),
                    [("sig", [P, 2, HALF], F32), ("act0", [P, HALF], F32),
                     ("act1", [P, HALF], F32), ("back0", [P, D], F32), ("back1", [P, D], F32)],
                    [("q_tile0", [P, HEADS, P], F32), ("q_tile1", [P, HEADS, P], F32)])
        E = region("E", D,
                   [("post_gain", [P, D], F32)], [("ple_sig", [P, 2, HALF], F32)],
                   [("k_rot", [P, KV_HEADS, 2, HEAD], F32), ("rope_a", [P, 256], F32), ("rope_b", [P, 256], F32)],
                   [("pt1", [P, KD, P], F32)])
        xt_hi, xt_lo = [DD["xt0_hi"], DD["xt1_hi"]], [DD["xt0_lo"], DD["xt1_lo"]]
        post_gain = E["post_gain"]
        kT, V = C["kT"], C["V"]
        qo = B["qo"]
        pool_m = [B["pool_m0"], B["pool_m1"]]

        ssum, mean, rstd = [[small[:, 2 * n + p:2 * n + p + 1] for p in range(2)] for n in range(3)]
        ssum2, mean2, rstd2 = [[small[:, 6 + 2 * n + p:7 + 2 * n + p] for p in range(2)] for n in range(3)]
        minus_half, eps = small[:, 12:13], small[:, 13:14]
        row_max = [small[:, 16 + 4 * p:20 + 4 * p] for p in range(2)]
        neg_max = [small[:, 24 + 4 * p:28 + 4 * p] for p in range(2)]
        sink_gap = [small[:, 32 + 4 * p:36 + 4 * p] for p in range(2)]
        sums = [sb(f"sums{p}", [P, HEADS]) for p in range(2)]
        sink_exp = [sb(f"sink_exp{p}", [P, HEADS]) for p in range(2)]
        recip = sb("recip", [P, HEADS])

        ps = ctx.enter_context(nc.psum_tensor("ps", [P, 8, HALF], F32))

        def banks(b, n=2):
            return ps[:, b:b + n, :].rearrange("p b c -> p (b c)")

        spill = nc.dram_tensor("residual_spill", (2, P, TILES * D), F32, kind="Internal").ap()

        units = []

        def rows(w, k):
            return w[k * P:(k + 1) * P, :]

        def quarter(w, j):
            return w.rearrange("(k p) n -> p k n", p=P)[:, 4 * j:4 * j + 4, :]

        BASE, n = {}, 0
        for name, count in (("pool", 2), ("ffn0", 6 * GROUPS), ("ple0", 10), ("kv", 4), ("q", 8), ("o", 8),
                            ("ffn1", 6 * GROUPS), ("ple1", 10)):
            BASE[name] = n
            n += count
        raw_loaded = [sem(f"raw_loaded{i}") for i in range(SLOTS)]
        hi_done = sem("weight_hi_done")
        w_ready = sem("weights_ready")

        def loaded(base, j, g=0):
            return raw_loaded[(base + j) % SLOTS], 16 * ((base + j) // SLOTS + 1 + g)

        def shape_of(dst, src):
            free_dims = dst.shape[1:]
            if len(free_dims) == 1:
                return src[:, :]
            return src[:, :].rearrange("p (k n) -> p k n", k=free_dims[0])

        def load_unit(sp, base, j, src, g=0):
            if not isinstance(g, int) or base + j + 6 * g >= SLOTS:
                sp.wait_ge(w_ready, base + j + 6 * g - SLOTS + 1)
            slot = raw[(base + j) % SLOTS]
            sp.dma_start(shape_of(src, slot), src).then_inc(loaded(base, j)[0], 16)

        def cut_hi(act, base, j, dst, g=0):
            s, value = loaded(base, j, g)
            act.wait_ge(s, value)
            act.activation(dst, shape_of(dst, raw[(base + j) % SLOTS]), ACT.Copy).then_inc(hi_done, 1)

        def cut_lo(dve, base, j, dst_hi, dst_lo, g=0):
            dve.wait_ge(hi_done, base + j + 6 * g + 1)
            dve.tensor_tensor(dst_lo, shape_of(dst_lo, raw[(base + j) % SLOTS]), dst_hi.bitcast(F32),
                              ALU.subtract).then_inc(w_ready, 1)

        def product(pe, out_, lhs, rhs, first, last):
            pe.matmul(out_, lhs[0], rhs[0], start=first, stop=False)
            pe.matmul(out_, lhs[0], rhs[1], start=False, stop=False)
            return pe.matmul(out_, lhs[1], rhs[0], start=False, stop=last)

        consts_loaded = sem("consts_loaded")
        pool_consts_loaded = sem("pool_consts_loaded")
        x_loaded = [sem(f"x_loaded{t}") for t in range(TILES)]
        gain_loaded = sem("gain_loaded")
        post_gain_loaded = sem("post_gain_loaded")
        consts_set = sem("consts_set")
        TURN = ("xn", "turned", "hi", "lo")
        MEAN = ("ssum", "mean", "rstd")
        POST = ("ssum2", "mean2", "rstd2", "scaled", "added")
        EMBED = ("p_hi", "p_lo")
        S = {}
        S["pool"] = Phase(*TURN, *MEAN, "used", *POST, "out_scaled")
        S["ffn0"] = Phase(*TURN, *MEAN)
        S["ple0"] = Phase(*TURN, *MEAN, "used", *EMBED)
        S["kv"] = Phase(*TURN, *MEAN, "used", "rotated", "k_turned")
        S["q"] = Phase(*TURN, *MEAN, "used")
        S["att"] = Phase("q_tile")
        S["o"] = Phase(*TURN, "used", *POST)
        S["ffn1"] = Phase(*TURN, *MEAN)
        S["ple1"] = Phase(*TURN, *MEAN, "used", *EMBED)
        att = Phase("scores", "masked", "max", "neg_max", "probs", "p_turned", "pt_act", "pt_dve", "pv", count=TILES * 2)
        p_loaded = [[sem(f"p_loaded{L}{p}") for p in range(2)] for L in range(2)]
        stored = sem("stored")

        def tile(i, p):
            return bass.ds((2 * i + p) * D, D)

        def square_sum(act, s, i, p, ready=None):
            act.wait_ge(s["turned"][p], s.free("turned", i))
            if ready:
                ready(act, i, p)
            act.activation(xn[p][:, :], H[:, tile(i, p)], ACT.Square, scale=D ** -0.5, accum_out=ssum[p]).then_inc(s["ssum"][p], 1)

        def inv_rms(pool, s, i, p, sums_, mean_, rstd_, names=("ssum", "mean", "rstd")):
            pool.wait_ge(s[names[0]][p], s.done(names[0], i))
            pool.tensor_tensor(mean_, sums_, eps, ALU.add).then_inc(s[names[1]][p], 1)
            pool.wait_ge(s[names[1]][p], s.done(names[1], i))
            pool.tensor_tensor(rstd_, mean_, minus_half, ALU.pow).then_inc(s[names[2]][p], 1)

        def normed(dve, s, i, p):
            dve.wait_ge(s["rstd"][p], s.done("rstd", i))
            dve.scalar_tensor_tensor(out=xn[p][:, :], in0=H[:, tile(i, p)], scalar=rstd[p], in1=gain[:, :],
                                     op0=ALU.mult, op1=ALU.mult).then_inc(s["xn"][p], 1)

        def turn(pe, s, i, p):
            pe.wait_ge(s["xn"][p], s.done("xn", i))
            pe.wait_ge(s["lo"][p], s.free("lo", i))
            for k in range(KD):
                last = pe.transpose(banks(2 * p)[:, k * P:(k + 1) * P], xn[p][:, k * P:(k + 1) * P], ident[:, :])
            last.then_inc(s["turned"][p], 1)

        def turned_hi(act, s, i, p, dst):
            act.wait_ge(s["turned"][p], s.done("turned", i))
            if "used" in s.base:
                act.wait_ge(s["used"][p], s.free("used", i))
            act.activation(dst, banks(2 * p).rearrange("p (k c) -> p k c", k=KD), ACT.Copy).then_inc(s["hi"][p], 1)

        def turned_lo(dve, s, i, p, hi, lo):
            dve.wait_ge(s["hi"][p], s.done("hi", i))
            dve.tensor_tensor(lo, banks(2 * p).rearrange("p (k c) -> p k c", k=KD), hi.bitcast(F32),
                              ALU.subtract).then_inc(s["lo"][p], 1)

        def slot_hi(act, s, i, p):
            turned_hi(act, s, i, p, xt_hi[p][:, :, :])

        def slot_lo(dve, s, i, p):
            turned_lo(dve, s, i, p, xt_hi[p][:, :, :], xt_lo[p][:, :, :])

        def over_pairs(eng, body):
            with eng.Fori(0, PAIRS - 1) as i:
                body(i, False)
            body(PAIRS - 1, True)

        def add_post(dve, s, i, p, src):
            dve.wait_ge(s["rstd2"][p], s.done("rstd2", i))
            dve.wait_ge(s["added"][1 - p], s.done("added", i) if p else s.free("added", i))
            dve.scalar_tensor_tensor(out=tmp[:, :], in0=src, scalar=rstd2[p], in1=post_gain[:, :],
                                     op0=ALU.mult, op1=ALU.mult).then_inc(s["scaled"][p], 1)
            dve.wait_ge(s["scaled"][p], s.done("scaled", i))
            dve.tensor_tensor(H[:, tile(i, p)], H[:, tile(i, p)], tmp[:, :], ALU.add).then_inc(s["added"][p], 1)

        ple_added = [sem_c(f"ple{n}_added") for n in range(2)]
        post_added = [sem_c(f"ffn{n}_post_added") for n in range(2)]

        def after_x(eng, i, p):
            pass

        def after_phase(name):
            def ready(eng, i, p):
                eng.wait_ge(S[name]["added"][p], done(PAIRS - 1))
            return ready

        def after_count(s, per_tile):
            def ready(eng, i, p):
                eng.wait_ge(s, 1 + per_tile * TILES)
            return ready

        def row_load(eng, dst, src, s):
            eng.dma_start(dst[:, :], src.partition_broadcast(P)).then_inc(s, 16)

        GAIN = {"pool": 1, "ffn0": 2, "ple0": 3, "kv": 4, "q": 5, "ffn1": 6, "ple1": 7}
        POSTG = {"pool": 1, "ffn0": 2, "o": 3, "ffn1": 4}

        w_pool = (C["w_pool_hi"], C["w_pool_lo"])
        s_pool = S["pool"]
        xn_pool_ready = s_pool["xn"]
        pool_junk = DD["xt0_hi"]

        def pool_band(pe, i, p, first=False):
            s = s_pool
            pe.wait_ge(s["xn"][p], s.done("xn", i))
            pe.wait_ge(s["lo"][p], s.free("lo", i))
            for c in range(KD):
                w = c // 2
                band = C["band_first"] if first else C["band_inner"]
                o = banks(2 * p)[:, c * P:(c + 1) * P]
                last = pe.matmul(o, xn[p][:, c * P:(c + 1) * P], band[:, w, :], start=True, stop=first)
                if not first:
                    last = pe.matmul(o[:, 0:LONGEST], xn[1 - p][:, c * P:(c + 1) * P], C["band_before"][:, w, :],
                                     start=False, stop=True)
            last.then_inc(s["turned"][p], 1)

        def pool_square_sum(act, i, p):
            s = s_pool
            if p == 0:
                act.wait_ge(s["turned"][1], s.free("turned", i))
            else:
                act.wait_ge(s["turned"][0], s.done("turned", i))
            act.activation(xn[p][:, :], H[:, tile(i, p)], ACT.Square, scale=D ** -0.5, accum_out=ssum[p]).then_inc(s["ssum"][p], 1)

        xT = (A["xT_hi"], A["xT_lo"])
        wg, wu, wd = (B["wg_hi"], B["wg_lo"]), (B["wu_hi"], B["wu_lo"]), (C["wd_hi"], C["wd_lo"])
        a = (C["a_hi"], C["a_lo"])
        sig, act32 = DD["sig"], [DD["act0"], DD["act1"]]
        back = [DD["back0"], DD["back1"]]
        F = {
            "gate": sem_c("ffn_gate_ready"), "up": sem_c("ffn_up_ready"),
            "sig": sem_c("ffn_sigmoid_done"), "prod": sem_c("ffn_silu_done"),
            "act": [sem_c(f"ffn_act_done{p}") for p in range(2)],
            "a_hi": sem_c("ffn_a_hi_done"), "a_lo": sem_c("ffn_a_ready"),
            "down": sem_c("ffn_down_ready"), "summed": [sem_c(f"ffn_summed{b}") for b in range(4)],
            "spilled": sem("ffn_spilled"), "cleared": sem("ffn_cleared"),
            "back": [sem(f"ffn_back_loaded{p}") for p in range(2)],
            "ssum2": sem("ffn_out_ssum"), "mean2": sem("ffn_out_mean"), "rstd2": sem("ffn_out_rstd"),
            "scaled": sem("ffn_out_scaled"),
        }

        def gu_dst(j):
            w = wg if j < 2 else wu
            k = 4 * (j % 2)
            return w[0][:, k:k + 4, :], w[1][:, k:k + 4, :]

        def ffn_pe(pe, L, g):
            f, base, r = F, BASE[f"ffn{L}"], GROUPS * L + g
            for n, (t, h) in enumerate(STEPS):
                b = 2 * (n % 2)
                pe.wait_ge(f["act"][n % 2], free(2 * r + n // 2))
                for m, (w, ready) in enumerate(((wg, "gate"), (wu, "up"))):
                    for k in range(KD):
                        if n == 0 and k % 4 == 0:
                            pe.wait_ge(w_ready, base + 6 * g + 2 * m + k // 4 + 1)
                        last = product(pe, ps[:, b + m, :],
                                       [x[:, k, t * P:(t + 1) * P] for x in w],
                                       [x[:, k, h * HALF:(h + 1) * HALF] for x in xT], k == 0, k == KD - 1)
                    last.then_inc(f[ready], 1)
            for n in range(2 * TILES):
                j, c = n // 2, n % 2
                if n == 0:
                    pe.wait_ge(w_ready, base + 6 * g + 6)
                    pe.wait_ge(f["a_lo"], 1 + 4 * r + 2)
                if n == TILES:
                    pe.wait_ge(f["a_lo"], 1 + 4 * r + 4)
                pe.wait_ge(f["summed"][n % 4], free(4 * r + n // 4))
                for t in range(2):
                    last = product(pe, ps[:, 4 + n % 4, :], [x[:, t, j * P:(j + 1) * P] for x in a],
                                   [x[:, t, c * HALF:(c + 1) * HALF] for x in wd], t == 0, t == 1)
                last.then_inc(f["down"], 1)

        def ffn_act(act, L, g, last_group):
            f, base, r = F, BASE[f"ffn{L}"], GROUPS * L + g
            act.wait_ge(f["down"], 1 + 16 * r)
            for t in range(2):
                cut_hi(act, base, 4 + t, wd[0][:, t, :], g)
            for n, (t, h) in enumerate(STEPS):
                act.wait_ge(f["gate"], 1 + 4 * r + n + 1)
                act.wait_ge(f["act"][n % 2], free(2 * r + n // 2))
                act.activation(sig[:, n % 2, :], ps[:, 2 * (n % 2), :], ACT.Sigmoid).then_inc(f["sig"], 1)
                act.wait_ge(f["act"][n % 2], done(2 * r + n // 2))
                act.activation(a[0][:, t, h * HALF:(h + 1) * HALF], act32[n % 2][:, :], ACT.Copy).then_inc(f["a_hi"], 1)
            if not last_group:
                act.wait_ge(f["up"], 1 + 4 * r + 4)
                for j in range(4):
                    cut_hi(act, base, j, gu_dst(j)[0], g + 1)

        def ffn_dve(dve, L, g, last_group, between=None):
            f, base, r = F, BASE[f"ffn{L}"], GROUPS * L + g
            for t in range(2):
                cut_lo(dve, base, 4 + t, wd[0][:, t, :], wd[1][:, t, :], g)
            for n, (t, h) in enumerate(STEPS):
                dve.wait_ge(f["sig"], 1 + 4 * r + n + 1)
                dve.tensor_tensor(sig[:, n % 2, :], ps[:, 2 * (n % 2), :], sig[:, n % 2, :], ALU.mult).then_inc(f["prod"], 1)
                dve.wait_ge(f["prod"], 1 + 4 * r + n + 1)
                dve.wait_ge(f["up"], 1 + 4 * r + n + 1)
                dve.tensor_tensor(act32[n % 2][:, :], ps[:, 2 * (n % 2) + 1, :], sig[:, n % 2, :],
                                  ALU.mult).then_inc(f["act"][n % 2], 1)
                dve.wait_ge(f["a_hi"], 1 + 4 * r + n + 1)
                hs = slice(h * HALF, (h + 1) * HALF)
                dve.tensor_tensor(a[1][:, t, hs], act32[n % 2][:, :], a[0][:, t, hs].bitcast(F32),
                                  ALU.subtract).then_inc(f["a_lo"], 1)
            for n in range(2 * TILES):
                j, c = n // 2, n % 2
                dve.wait_ge(f["down"], 1 + 16 * r + n + 1)
                dst = H[:, j * D + c * HALF:j * D + (c + 1) * HALF]
                dve.tensor_tensor(dst, dst, ps[:, 4 + n % 4, :], ALU.add).then_inc(f["summed"][n % 4], 1)
                if not last_group and n in (4, 7, 10, 13):
                    u = (n - 4) // 3
                    cut_lo(dve, base, u, *gu_dst(u), g + 1)
                if last_group and between:
                    between(n)

        def ffn_post_act(act, L):
            f, n0 = F, TILES * L
            for j in range(TILES):
                for n in (2 * j, 2 * j + 1):
                    act.wait_ge(f["summed"][n % 4], 1 + 4 * (GROUPS * (L + 1) - 1) + n // 4 + 1)
                if n0 + j >= 1:
                    act.wait_ge(f["mean2"], n0 + j)
                act.activation(sig[:, :, :].rearrange("p a b -> p (a b)"), H[:, j * D:(j + 1) * D], ACT.Square, scale=D ** -0.5,
                               accum_out=ssum2[0]).then_inc(f["ssum2"], 1)

        def ffn_post_pool(pool, L):
            f, n0 = F, TILES * L
            for j in range(TILES):
                pool.wait_ge(f["ssum2"], n0 + j + 1)
                if n0 + j >= 1:
                    pool.wait_ge(f["rstd2"], n0 + j)
                pool.tensor_tensor(mean2[0], ssum2[0], eps, ALU.add).then_inc(f["mean2"], 1)
                pool.wait_ge(f["mean2"], n0 + j + 1)
                if n0 + j >= 1:
                    pool.wait_ge(f["scaled"], n0 + j)
                pool.tensor_tensor(rstd2[0], mean2[0], minus_half, ALU.pow).then_inc(f["rstd2"], 1)

        def ffn_post_dve(dve, L, j):
            f, n0 = F, TILES * L
            dve.wait_ge(f["rstd2"], n0 + j + 1)
            dve.wait_ge(post_gain_loaded, 16 * POSTG[f"ffn{L}"])
            Hj = H[:, j * D:(j + 1) * D]
            dve.scalar_tensor_tensor(out=Hj, in0=Hj, scalar=rstd2[0], in1=post_gain[:, :],
                                     op0=ALU.mult, op1=ALU.mult).then_inc(f["scaled"], 1)
            dve.wait_ge(f["scaled"], n0 + j + 1)
            dve.wait_ge(f["back"][j % 2], 16 * (PAIRS * L + j // 2 + 1))
            dve.tensor_tensor(Hj, Hj, back[j % 2][:, :], ALU.add).then_inc(post_added[L], 1)

        w_pg = [(A[f"w_ple_gate{L}_hi"], A[f"w_ple_gate{L}_lo"]) for L in range(2)]
        w_pp = (C["w_ple_proj_hi"], C["w_ple_proj_lo"])
        pT = [(C[f"pT{p}_hi"], C[f"pT{p}_lo"]) for p in range(2)]
        p_raw = [C["p_raw0"], C["p_raw1"]]
        ple_sig = E["ple_sig"]
        G = {
            "gate": [sem_c(f"ple_gate_ready{c}") for c in range(2)],
            "proj": sem_c("ple_proj_ready0"),
            "sig": [sem_c(f"ple_sigmoid_done{c}") for c in range(2)],
            "prod": [sem_c(f"ple_gated{c}") for c in range(2)],
        }

        def ple_pe(pe, L, i, p):
            g, s, t = G, S[f"ple{L}"], TILES * L + 2 * i + p
            pe.wait_ge(s["lo"][p], s.done("lo", i))
            for c in range(2):
                pe.wait_ge(g["sig"][c], free(t))
                for k in range(KD):
                    if isinstance(i, int) or p == 0:
                        pe.wait_ge(w_ready, BASE[f"ple{L}"] + k + 1)
                    last = product(pe, ps[:, 4 + c, :], [x[p][:, k, :] for x in (xt_hi, xt_lo)],
                                   [x[:, k, c * HALF:(c + 1) * HALF] for x in w_pg[L]], k == 0, k == KD - 1)
                last.then_inc(g["gate"][c], 1)
            pe.wait_ge(s["p_lo"][p], s.done("p_lo", i))
            pe.wait_ge(w_ready, BASE[f"ple{L}"] + 10)
            for c in range(2):
                pe.wait_ge(g["prod"][c], free(t))
                for k in range(2):
                    last = product(pe, ps[:, 6 + c, :], [x[:, k, :] for x in pT[p]],
                                   [x[:, k, c * HALF:(c + 1) * HALF] for x in w_pp], k == 0, k == 1)
                last.then_inc(g["proj"] if c == 0 else s["used"][p], 1)

        def ple_act(act, L, i, p):
            g, t = G, TILES * L + 2 * i + p
            for c in range(2):
                act.wait_ge(g["gate"][c], done(t))
                act.wait_ge(g["prod"][c], free(t))
                act.activation(ple_sig[:, c, :], ps[:, 4 + c, :], ACT.Sigmoid).then_inc(g["sig"][c], 1)

        def ple_dve(dve, L, i, p):
            g, s, t = G, S[f"ple{L}"], TILES * L + 2 * i + p
            dve.wait_ge(ple_added[L], 1 + 2 * (2 * i + p))
            for c in range(2):
                dve.wait_ge(g["sig"][c], done(t))
                if c == 0:
                    dve.wait_ge(g["proj"], done(t))
                else:
                    dve.wait_ge(s["used"][p], s.done("used", i))
                dve.tensor_tensor(tmp[:, c * HALF:(c + 1) * HALF], ps[:, 6 + c, :], ple_sig[:, c, :],
                                  ALU.mult).then_inc(g["prod"][c], 1)
            for c in range(2):
                dve.wait_ge(g["prod"][c], done(t))
                dst = H[:, bass.ds((2 * i + p) * D + c * HALF, HALF)]
                dve.tensor_tensor(dst, dst, tmp[:, c * HALF:(c + 1) * HALF], ALU.add).then_inc(ple_added[L], 1)

        def p_load(sp, L, i, p):
            s = S[f"ple{L}"]
            sp.wait_ge(s["p_lo"][p], s.free("p_lo", i))
            sp.dma_start(p_raw[p][:, :, :], I["pT"][L].rearrange("(k c) t -> c k t", c=P)[:, :, bass.ds((2 * i + p) * P, P)]
                         ).then_inc(p_loaded[L][p], 16)

        def p_hi(act, L, i, p):
            s = S[f"ple{L}"]
            act.wait_ge(p_loaded[L][p], 16 * i + 16)
            act.wait_ge(s["used"][p], s.free("used", i))
            act.activation(pT[p][0][:, :, :], p_raw[p][:, :, :], ACT.Copy).then_inc(s["p_hi"][p], 1)

        def p_lo(dve, L, i, p):
            s = S[f"ple{L}"]
            dve.wait_ge(s["p_hi"][p], s.done("p_hi", i))
            dve.tensor_tensor(pT[p][1][:, :, :], p_raw[p][:, :, :], pT[p][0][:, :, :].bitcast(F32),
                              ALU.subtract).then_inc(s["p_lo"][p], 1)

        w_kv = (B["w_kv_hi"], B["w_kv_lo"])
        k_rot, rope_a, rope_b = E["k_rot"], E["rope_a"], E["rope_b"]
        s_kv = S["kv"]
        k_copied = [sem_c(f"kv_k_copied{p}") for p in range(2)]
        v_copied = sem("v_copied")
        rope_step = sem("rope_step")
        kv_zeroed = sem("kv_zeroed")
        q_zeroed = sem("q_zeroed")

        def kv_dst(j):
            k, c = 4 * (j % 2), GROUP * (j // 2)
            return [w[:, k:k + 4, c:c + GROUP] for w in w_kv]

        def kv_pe(pe, i, p):
            s = s_kv
            pe.wait_ge(s["lo"][p], s.done("lo", i))
            pe.wait_ge(s["rotated"][p], s.free("rotated", i))
            for k in range(KD):
                last = product(pe, ps[:, 4 + p, :], [x[p][:, k, :] for x in (xt_hi, xt_lo)],
                               [x[:, k, :] for x in w_kv], k == 0, k == KD - 1)
            last.then_inc(s["used"][p], 1)

        def kv_turn(pe, i, p):
            s = s_kv
            pe.wait_ge(s["rotated"][p], s.done("rotated", i))
            pe.wait_ge(k_copied[p], free(i))
            for n in range(KV_HEADS):
                last = pe.transpose(ps[:, 6 + p, n * P:(n + 1) * P], k_rot[:, n, :, :].rearrange("p a b -> p (a b)"),
                                    ident[:, :])
            last.then_inc(s["k_turned"][p], 1)

        def kv_act(act, i, p):
            act.wait_ge(s_kv["k_turned"][p], s_kv.done("k_turned", i))
            act.activation(kT[:, bass.ds(2 * i + p + 1, 1), :, :].rearrange("p a b c -> p (a b c)"),
                           ps[:, 6 + p, :], ACT.Copy).then_inc(k_copied[p], 1)

        def rope(dve, base, src1, src2, c, s, dst1, dst2, ta, tb, bank_read, n=1):
            dve.tensor_tensor(ta, src1, c, ALU.mult).then_inc(rope_step, 1)
            dve.tensor_tensor(tb, src2, s, ALU.mult).then_inc(rope_step, 1)
            dve.wait_ge(rope_step, base + 2)
            dve.tensor_tensor(dst1[0], dst1[1](ta), dst1[1](tb), ALU.subtract).then_inc(rope_step, 1)
            dve.wait_ge(rope_step, base + 3)
            dve.tensor_tensor(ta, src2, c, ALU.mult).then_inc(rope_step, 1)
            dve.tensor_tensor(tb, src1, s, ALU.mult).then_inc(rope_step, 1)
            dve.wait_ge(rope_step, base + 5)
            dve.tensor_tensor(dst2[0], dst2[1](ta), dst2[1](tb), ALU.add).then_inc(bank_read, 1)

        def table(name, i, p, heads):
            return C[name][:, bass.ds(2 * i + p, 1), :].to_broadcast([P, heads, 32])

        def kv_dve(dve, i, p):
            s = s_kv
            dve.wait_ge(s["used"][p], s.done("used", i))
            dve.tensor_copy(V[:, bass.ds(2 * i + p + 1, 1), :].rearrange("p a b -> p (a b)"),
                            ps[:, 4 + p, GROUP:2 * GROUP]).then_inc(v_copied, 1)
            dve.wait_ge(s["k_turned"][1 - p], s.done("k_turned", i) if p else s.free("k_turned", i))
            k4 = ps[:, 4 + p, 0:GROUP].rearrange("p (h d) -> p h d", d=HEAD)
            ta = rope_a[:, 0:128].rearrange("p (h d) -> p h d", d=32)
            tb = rope_b[:, 0:128].rearrange("p (h d) -> p h d", d=32)
            dve.wait_ge(s["rotated"][1 - p], s.done("rotated", i) if p else s.free("rotated", i))
            twice = lambda x: x.unsqueeze(2).to_broadcast([P, KV_HEADS, 2, 32])
            rope(dve, (2 * i + p) * 5, k4[:, :, 0:32], k4[:, :, 32:64], table("cos", i, p, KV_HEADS),
                 table("sin", i, p, KV_HEADS), (k_rot[:, :, :, 0:32], twice), (k_rot[:, :, :, 32:64], twice),
                 ta, tb, s["rotated"][p])

        w_q = (A["w_q_hi"], A["w_q_lo"])
        s_q = S["q"]
        q_out = [sem_c(f"q_out_ready{c}") for c in range(2)]
        q_rot = [sem_c(f"q_rotated{c}") for c in range(2)]
        q_turned, q_copied = sem_c("q_turned"), sem_c("q_copied")

        def q_pe(pe, i, p):
            t = 2 * i + p
            pe.wait_ge(s_q["lo"][p], s_q.done("lo", i))
            for c in range(2):
                pe.wait_ge(q_rot[c], free(t))
                for k in range(KD):
                    if isinstance(i, int) or p == 0:
                        pe.wait_ge(w_ready, BASE["q"] + k + 1)
                    last = product(pe, ps[:, 4 + c, :], [x[p][:, k, :] for x in (xt_hi, xt_lo)],
                                   [x[:, k, c * HALF:(c + 1) * HALF] for x in w_q], k == 0, k == KD - 1)
                last.then_inc(q_out[c] if c == 0 else s_q["used"][p], 1)

        def q_turn(pe, i, p):
            t = 2 * i + p
            for c in range(2):
                pe.wait_ge(q_rot[c], done(t))
            pe.wait_ge(q_copied, free(t))
            for k in range(KD):
                last = pe.transpose(banks(6)[:, k * P:(k + 1) * P], tmp[:, k * P:(k + 1) * P], ident[:, :])
            last.then_inc(q_turned, 1)

        def q_act(act, i, p):
            t = 2 * i + p
            act.wait_ge(q_turned, done(t))
            act.activation(qo[:, bass.ds(t, 1), :].rearrange("p a b -> p (a b)"), banks(6), ACT.Copy).then_inc(q_copied, 1)

        def q_dve(dve, i, p):
            t = 2 * i + p
            for c in range(2):
                if c == 0:
                    dve.wait_ge(q_out[0], done(t))
                    dve.wait_ge(q_turned, free(t))
                    dve.wait_ge(q_rot[1], free(t))
                else:
                    dve.wait_ge(s_q["used"][p], s_q.done("used", i))
                    dve.wait_ge(q_rot[0], done(t))
                h8 = ps[:, 4 + c, :].rearrange("p (h d) -> p h d", d=HEAD)
                o8 = tmp[:, c * HALF:(c + 1) * HALF].rearrange("p (h d) -> p h d", d=HEAD)
                ta, tb = [x[:, :].rearrange("p (h d) -> p h d", d=32) for x in (rope_a, rope_b)]
                same = lambda x: x
                rope(dve, 5 * TILES + (2 * t + c) * 5, h8[:, :, 0:32], h8[:, :, 32:64], table("cos", i, p, 8),
                     table("sin", i, p, 8), (o8[:, :, 0:32], same), (o8[:, :, 32:64], same), ta, tb, q_rot[c])

        s_a = S["att"]
        q_tile = [DD["q_tile0"], DD["q_tile1"]]
        pt = [tmp[:, :].rearrange("p (k c) -> p k c", k=KD), E["pt1"]]
        mask = [C["mask0"], C["mask1"]]
        o_ready, o_out = sem_c("o_ready"), sem_c("o_read_out")
        sink_dve, sink_act = sem_c("sink_gap_done"), sem_c("sink_exp_done")
        mask_set = sem("mask0_set")
        sums_read = [sem_c(f"sums_read{p}") for p in range(2)]
        recip_done = sem("recip_done")
        att_max1 = [sem_c(f"att_row_max{p}") for p in range(2)]

        def scores(pe, i, p, g):
            par, r = g % 2, 4 * i + 2 * p + g // 2
            if g == 0:
                pe.wait_ge(s_a["q_tile"][p], s_a.done("q_tile", i))
            pe.wait_ge(att["masked"][par], att.free("masked", r))
            for m in range(GQA):
                h = GQA * g + m
                last = pe.matmul(banks(2 * par)[:, m * 256:(m + 1) * 256].rearrange("p (b c) -> p b c", b=2),
                                 q_tile[p][:, h, :], kT[:, bass.ds(2 * i + p, 2), g, :], start=True, stop=True)
            last.then_inc(att["scores"][par], 1)

        def softmax_dve(dve, i, p, g):
            par, r = g % 2, 4 * i + 2 * p + g // 2
            dve.wait_ge(att["scores"][par], att.done("scores", r))
            dve.wait_ge(att["p_turned"][par], att.free("p_turned", r))
            if g == 0 and p == 0 and not (isinstance(i, int) and i == 0):
                dve.tensor_copy(mask[0][:, :], mask[1][:, :]).then_inc(mask_set, 1)
                dve.wait_ge(mask_set, i)
            S3 = xn[par][:, :].rearrange("p (h k) -> p h k", h=GQA)
            m3 = mask[p][:, :].unsqueeze(1).to_broadcast([P, GQA, 2 * P])
            dve.scalar_tensor_tensor(out=S3, in0=banks(2 * par).rearrange("p (h k) -> p h k", h=GQA),
                                     scalar=HEAD ** -0.5, in1=m3, op0=ALU.mult, op1=ALU.add
                                     ).then_inc(att["masked"][par], 1)
            dve.wait_ge(att["masked"][par], att.done("masked", r))
            dve.tensor_reduce(row_max[par], S3, AX.X, ALU.max).then_inc(att_max1[par], 1)
            dve.wait_ge(att_max1[par], done(r))
            dve.wait_ge(att["probs"][par], att.free("probs", r))
            sk = sinks[:, GQA * g:GQA * (g + 1)]
            dve.tensor_tensor(row_max[par], row_max[par], sk, ALU.max).then_inc(att["max"][par], 1)
            dve.wait_ge(att["max"][par], att.done("max", r))
            dve.tensor_scalar(neg_max[par], row_max[par], -1.0, None, ALU.mult).then_inc(att["neg_max"][par], 1)
            dve.tensor_tensor(sink_gap[par], sk, row_max[par], ALU.subtract).then_inc(sink_dve, 1)

        def q_to_place(act, i, p):
            if not isinstance(i, int) or i > 0:
                act.wait_ge(att["scores"][1], 1 + 4 * i + 2 * p - 2)
            for r in range(2):
                part = slice(HEAD * r, HEAD * (r + 1))
                last = act.activation(q_tile[p][part, :, :].rearrange("p (k r) c -> p k r c", r=2)[:, :, r, :],
                                      qo[part, bass.ds(2 * i + p, 1), :].rearrange("p a (k c) -> p (a k) c", c=P),
                                      ACT.Copy)
            last.then_inc(s_a["q_tile"][p], 1)

        def softmax_act(act, i, p, g):
            par, r = g % 2, 4 * i + 2 * p + g // 2
            act.wait_ge(att["neg_max"][par], att.done("neg_max", r))
            act.wait_ge(sink_dve, done(4 * (2 * i + p) + g))
            if g == 0:
                act.wait_ge(sums_read[p], free(i))
            act.activation(sink_exp[p][:, GQA * g:GQA * (g + 1)], sink_gap[par], ACT.Exp).then_inc(sink_act, 1)
            for m in range(GQA):
                sl = xn[par][:, m * 256:(m + 1) * 256]
                last = act.activation(sl, sl, ACT.Exp, bias=neg_max[par][:, m:m + 1],
                                      accum_out=sums[p][:, GQA * g + m:GQA * g + m + 1])
            last.then_inc(att["probs"][par], 1)

        def turn_probs(pe, i, p, g):
            par, r = g % 2, 4 * i + 2 * p + g // 2
            pe.wait_ge(att["probs"][par], att.done("probs", r))
            before = r - 1 if par == 0 else r
            pe.wait_ge(att["pt_act"][1 - par], att.done("pt_act", before))
            pe.wait_ge(att["pt_dve"][1 - par], att.done("pt_dve", before))
            for k in range(8):
                last = pe.transpose(banks(4)[:, k * P:(k + 1) * P], xn[par][:, k * P:(k + 1) * P], ident[:, :])
            last.then_inc(att["p_turned"][par], 1)

        def probs_copy(eng, i, p, g, mine):
            par, r = g % 2, 4 * i + 2 * p + g // 2
            c = 0 if mine == "pt_act" else 1
            eng.wait_ge(att["p_turned"][par], att.done("p_turned", r))
            eng.wait_ge(att["pv"][par], att.free("pv", r))
            dst, src = pt[par][:, 4 * c:4 * c + 4, :].rearrange("p a b -> p (a b)"), ps[:, 4 + c, :]
            if c == 0:
                eng.activation(dst, src, ACT.Copy).then_inc(att[mine][par], 1)
            else:
                eng.tensor_copy(dst, src).then_inc(att[mine][par], 1)

        def values(pe, i, p, g):
            par, r = g % 2, 4 * i + 2 * p + g // 2
            pe.wait_ge(att["pt_act"][par], att.done("pt_act", r))
            pe.wait_ge(att["pt_dve"][par], att.done("pt_dve", r))
            if g == 0:
                pe.wait_ge(o_out, free(2 * i + p))
            for m in range(GQA):
                h = GQA * g + m
                for b in range(2):
                    last = pe.matmul(banks(6)[:, h * HEAD:(h + 1) * HEAD], pt[par][:, 2 * m + b, :],
                                     V[:, bass.ds(2 * i + p + b, 1), g * HEAD:(g + 1) * HEAD].rearrange("p a b -> p (a b)"),
                                     start=(b == 0), stop=(b == 1))
            last.then_inc(att["pv"][par], 1)

        def att_out(dve, i, p):
            t = 2 * i + p
            dve.wait_ge(att["pv"][1], att.done("pv", 4 * i + 2 * p + 1))
            dve.wait_ge(sink_act, done(4 * t + 3))
            dve.wait_ge(att["probs"][1], att.done("probs", 4 * i + 2 * p + 1))
            dve.wait_ge(o_out, free(t))
            dve.tensor_tensor(recip[:, :], sums[p][:, :], sink_exp[p][:, :], ALU.add).then_inc(sums_read[p], 1)
            dve.wait_ge(sums_read[p], done(i))
            dve.reciprocal(recip[:, :], recip[:, :]).then_inc(recip_done, 1)
            dve.wait_ge(recip_done, t + 1)
            dve.wait_ge(s_a["q_tile"][p], s_a.done("q_tile", i))
            dve.tensor_tensor(qo[:, bass.ds(t, 1), :].rearrange("p a (h d) -> p (a h) d", d=HEAD),
                              banks(6).rearrange("p (h d) -> p h d", d=HEAD),
                              recip[:, :].unsqueeze(2).to_broadcast([P, HEADS, HEAD]), ALU.mult).then_inc(o_out, 1)

        w_o = (A["w_o_hi"], A["w_o_lo"])
        s_o = S["o"]

        def o_pe(pe, i, p):
            pe.wait_ge(s_o["lo"][p], s_o.done("lo", i))
            pe.wait_ge(s_o["scaled"][p], s_o.free("scaled", i))
            for c in range(2):
                for k in range(KD):
                    if (isinstance(i, int) or p == 0) and c == 0:
                        pe.wait_ge(w_ready, BASE["o"] + k + 1)
                    last = product(pe, ps[:, 4 + 2 * p + c, :], [x[p][:, k, :] for x in (xt_hi, xt_lo)],
                                   [x[:, k, c * HALF:(c + 1) * HALF] for x in w_o], k == 0, k == KD - 1)
            last.then_inc(s_o["used"][p], 1)

        def o_act(act, i, p):
            act.wait_ge(s_o["used"][p], s_o.done("used", i))
            act.wait_ge(s_o["mean2"][p], s_o.free("mean2", i))
            act.activation(C["o_squares"][:, p, :], banks(4 + 2 * p), ACT.Square, scale=D ** -0.5, accum_out=ssum2[p]).then_inc(s_o["ssum2"][p], 1)

        block = ctx.enter_context(nc.Block())

        @block.sync
        def _(sp):
            sp.dma_start(ident[:, :], I["identity"]).then_inc(consts_loaded, 16)
            sp.dma_start(sinks[:, :], I["sinks"][0].partition_broadcast(P)).then_inc(consts_loaded, 16)
            x_t = I["x"].rearrange("b (t p) d -> p (b t) d", p=P)
            for t in range(2):
                sp.dma_start(H[:, t * D:(t + 1) * D], x_t[:, t, :]).then_inc(x_loaded[t], 16)
            for name in ("band_first", "band_inner", "band_before"):
                sp.dma_start(C[name][:, :, :], I[name]).then_inc(pool_consts_loaded, 16)
            w = I["pool_w"][0].rearrange("g c n -> (g c) n")
            for j in range(2):
                load_unit(sp, BASE["pool"], j, quarter(w, j))
            sp.dma_start(C["scale_row"][:, :], I["pool_scale"][0].partition_broadcast(P)).then_inc(pool_consts_loaded, 16)
            for t in range(2, TILES):
                sp.dma_start(H[:, t * D:(t + 1) * D], x_t[:, t, :]).then_inc(x_loaded[t], 16)

            def ffn_loads(L):
                f, base = F, BASE[f"ffn{L}"]
                gate = I["w_ff_gate"][L].rearrange("(k p) n -> p k n", p=P)
                up = I["w_ff_up"][L].rearrange("(k p) n -> p k n", p=P)

                def group(g):
                    for j, w in enumerate((gate, gate, up, up)):
                        k = 4 * (j % 2)
                        load_unit(sp, base, j, w[:, k:k + 4, bass.ds(g * GROUP, GROUP)], g)
                    for t in range(2):
                        load_unit(sp, base, 4 + t, I["w_ff_down"][L][bass.ds((2 * g + t) * P, P), :], g)

                group(0)
                for p in range(2):
                    sp.wait_ge(S[("pool", "o")[L]]["added"][p], S[("pool", "o")[L]].done("added", PAIRS - 1))
                sp.dma_start(spill[L], H[:, :]).then_inc(f["spilled"], 16)
                with sp.Fori(1, GROUPS) as g:
                    group(g)
                for k in range(SLOTS):
                    load_unit(sp, BASE[f"ple{L}"], k, rows(I["w_ple_gate"][L], k))
                sp.wait_ge(f["spilled"], 16 * (L + 1))
                for j in range(TILES):
                    if j < 2:
                        sp.wait_ge(S[f"ffn{L}"]["lo"][j], S[f"ffn{L}"].done("lo", PAIRS - 1))
                    else:
                        sp.wait_ge(post_added[L], 1 + j - 1)
                    sp.dma_start(back[j % 2][:, :], spill[L][:, j * D:(j + 1) * D]).then_inc(f["back"][j % 2], 16)

            def ple_loads(L):
                base = BASE[f"ple{L}"]
                for k in range(SLOTS, KD):
                    load_unit(sp, base, k, rows(I["w_ple_gate"][L], k))
                for k in range(2):
                    load_unit(sp, base, KD + k, rows(I["w_ple_proj"][L], k))
                sp.wait_ge(F["down"], 1 + 16 * GROUPS * (L + 1))
                over_pairs(sp, lambda i, last: [p_load(sp, L, i, p) for p in range(2)])

            ffn_loads(0)
            ple_loads(0)
            for j in range(4):
                load_unit(sp, BASE["kv"], j, quarter(I["w_k"] if j < 2 else I["w_v"], j % 2))
            for p in range(2):
                sp.wait_ge(S["ple0"]["used"][p], S["ple0"].done("used", PAIRS - 1))
            for name, dst in (("rope_cos", C["cos"][:, :, :]), ("rope_sin", C["sin"][:, :, :])):
                sp.dma_start(dst, I[name]).then_inc(consts_loaded, 16)
            for m in range(2):
                sp.dma_start(mask[m][:, :], I["mask"][:, m, :]).then_inc(consts_loaded, 16)
            for k in range(KD):
                load_unit(sp, BASE["q"], k, rows(I["w_q"][0], k))
            for k in range(KD):
                load_unit(sp, BASE["o"], k, rows(I["w_o"][0], k))
            ffn_loads(1)
            ple_loads(1)
            o_t = out.rearrange("b (t p) d -> p (b t) d", p=P)
            for t in range(TILES):
                sp.wait_ge(ple_added[1], 1 + 2 * (t + 1))
                sp.dma_start(o_t[:, t, :], H[:, t * D:(t + 1) * D]).then_inc(stored, 16)
            sp.wait_ge(stored, 16 * TILES)

        @block.gpsimd
        def _(pool):
            for s in credited:
                pool.sem_inc(s, 1)
            pool.memset(minus_half, -0.5).then_inc(consts_set, 1)
            pool.memset(eps, EPS).then_inc(consts_set, 1)
            pool.wait_ge(consts_set, 2)

            def norm_pass(name):
                with pool.Fori(0, PAIRS) as i:
                    for p in range(2):
                        inv_rms(pool, S[name], i, p, ssum[p], mean[p], rstd[p])

            def post(i, p, s):
                inv_rms(pool, s, i, p, ssum2[p], mean2[p], rstd2[p], ("ssum2", "mean2", "rstd2"))

            def pool_body(i, last):
                inv_rms(pool, s_pool, i, 1, ssum[1], mean[1], rstd[1])
                post(i, 0, s_pool)
                if not last:
                    inv_rms(pool, s_pool, i + 1, 0, ssum[0], mean[0], rstd[0])
                post(i, 1, s_pool)

            def ffn(L):
                norm_pass(f"ffn{L}")
                f = F
                pool.wait_ge(f["spilled"], 16 * (L + 1))
                for p in range(2):
                    pool.wait_ge(S[f"ffn{L}"]["xn"][p], S[f"ffn{L}"].done("xn", PAIRS - 1))
                pool.memset(H[:, :], 0.0).then_inc(f["cleared"], 1)
                ffn_post_pool(pool, L)

            inv_rms(pool, s_pool, 0, 0, ssum[0], mean[0], rstd[0])
            over_pairs(pool, pool_body)
            ffn(0)
            norm_pass("ple0")
            for p in range(2):
                pool.wait_ge(S["ple0"]["used"][p], S["ple0"].done("used", PAIRS - 1))
            pool.memset(kT[:, 0, :, :], 0.0).then_inc(kv_zeroed, 1)
            pool.memset(V[:, 0, :], 0.0).then_inc(kv_zeroed, 1)
            norm_pass("kv")
            norm_pass("q")

            for p in range(2):
                pool.wait_ge(s_q["used"][p], s_q.done("used", PAIRS - 1))
                pool.memset(q_tile[p][:, :, :], 0.0).then_inc(q_zeroed, 1)

            def o_copy(i, p):
                pool.wait_ge(s_o["turned"][p], s_o.free("turned", i))
                pool.wait_ge(o_out, 1 + TILES)
                pool.tensor_copy(xn[p][:, :], qo[:, bass.ds(2 * i + p, 1), :].rearrange("p a b -> p (a b)")
                                 ).then_inc(s_o["xn"][p], 1)

            o_copy(0, 0)

            def o_body(i, last):
                o_copy(i, 1)
                post(i, 0, s_o)
                if not last:
                    o_copy(i + 1, 0)
                post(i, 1, s_o)

            over_pairs(pool, o_body)
            ffn(1)
            norm_pass("ple1")

        @block.scalar
        def _(act):
            def gain_row(name, src):
                row_load(act, gain, src, gain_loaded)

            gain_row("pool", I["mix_pre_g"][0])
            row_load(act, post_gain, I["mix_post_g"][0], post_gain_loaded)
            s = s_pool
            act.wait_ge(x_loaded[0], 16)
            act.wait_ge(x_loaded[1], 16)
            pool_square_sum(act, 0, 0)
            for j in range(2):
                cut_hi(act, BASE["pool"], j, w_pool[0][:, 4 * j:4 * j + 4, :])
            for t in range(2, TILES):
                act.wait_ge(x_loaded[t], 16)

            def pool_out(i, p):
                act.wait_ge(s["out_scaled"][p], s.done("out_scaled", i))
                act.wait_ge(s["mean2"][p], s.free("mean2", i))
                act.activation(A["pool_squares"][:, p, :], pool_m[p][:, :], ACT.Square, scale=D ** -0.5, accum_out=ssum2[p]).then_inc(s["ssum2"][p], 1)

            def pool_body(i, last):
                slot_hi(act, s, i, 0)
                pool_square_sum(act, i, 1)
                slot_hi(act, s, i, 1)
                pool_out(i, 0)
                if not last:
                    pool_square_sum(act, i + 1, 0)
                pool_out(i, 1)

            over_pairs(act, pool_body)

            def ffn(L, before):
                name, f, base = f"ffn{L}", F, BASE[f"ffn{L}"]
                s = S[name]
                with act.Fori(0, PAIRS) as i:
                    for p in range(2):
                        square_sum(act, s, i, p, before)
                    for p in range(2):
                        turned_hi(act, s, i, p, xT[0][:, :, bass.ds((2 * i + p) * P, P)])
                gain_row(f"ple{L}", I["ple_norm_g"][L])
                row_load(act, post_gain, I["ffn_post_g"][L], post_gain_loaded)
                for j in range(4):
                    cut_hi(act, base, j, gu_dst(j)[0])
                with act.Fori(0, GROUPS - 1) as g:
                    ffn_act(act, L, g, False)
                ffn_act(act, L, GROUPS - 1, True)
                act.wait_ge(f["up"], 1 + 4 * GROUPS * (L + 1))
                for k in range(4):
                    cut_hi(act, BASE[f"ple{L}"], k, w_pg[L][0][:, k, :])
                ffn_post_act(act, L)
                for k in range(4, KD):
                    cut_hi(act, BASE[f"ple{L}"], k, w_pg[L][0][:, k, :])
                act.wait_ge(f["down"], 1 + 16 * GROUPS * (L + 1))
                for k in range(2):
                    cut_hi(act, BASE[f"ple{L}"], KD + k, w_pp[0][:, k, :])

            def ple(L):
                name = f"ple{L}"
                s = S[name]
                ready = after_count(post_added[L], 1)

                def prepare(i, p):
                    square_sum(act, s, i, p, ready)
                    p_hi(act, L, i, p)
                    slot_hi(act, s, i, p)

                prepare(0, 0)

                def body(i, last):
                    prepare(i, 1)
                    ple_act(act, L, i, 0)
                    if not last:
                        prepare(i + 1, 0)
                    ple_act(act, L, i, 1)

                over_pairs(act, body)

            gain_row("ffn0", I["ffn_pre_g"][0])
            ffn(0, after_phase("pool"))
            ple(0)
            gain_row("kv", I["kv_norm_g"])
            for j in range(4):
                cut_hi(act, BASE["kv"], j, kv_dst(j)[0])

            ready = after_count(ple_added[0], 2)

            def kv_prepare(i, p):
                square_sum(act, s_kv, i, p, ready)
                slot_hi(act, s_kv, i, p)

            kv_prepare(0, 0)

            def kv_body(i, last):
                kv_prepare(i, 1)
                kv_act(act, i, 0)
                if not last:
                    kv_prepare(i + 1, 0)
                kv_act(act, i, 1)

            over_pairs(act, kv_body)
            for k in range(KD):
                cut_hi(act, BASE["q"], k, w_q[0][:, k, :])

            gain_row("q", I["mix_pre_g"][1])

            def q_prepare(i, p):
                square_sum(act, s_q, i, p, ready)
                slot_hi(act, s_q, i, p)

            q_prepare(0, 0)

            def q_body(i, last):
                q_prepare(i, 1)
                q_act(act, i, 0)
                if not last:
                    q_prepare(i + 1, 0)
                q_act(act, i, 1)

            over_pairs(act, q_body)
            gain_row("ffn1", I["ffn_pre_g"][1])

            act.wait_ge(q_zeroed, 2)
            act.wait_ge(q_copied, 1 + TILES)
            q_to_place(act, 0, 0)
            softmax_act(act, 0, 0, 0)
            softmax_act(act, 0, 0, 1)

            def att_tile(i, p, more, nxt):
                for g in range(KV_HEADS):
                    if g == 0 and more:
                        q_to_place(act, *nxt)
                    probs_copy(act, i, p, g, "pt_act")
                    if g < 2:
                        softmax_act(act, i, p, g + 2)
                    elif more:
                        softmax_act(act, *nxt, g - 2)

            def att_body(i, last):
                att_tile(i, 0, True, (i, 1))
                att_tile(i, 1, not last, (i + 1, 0))

            over_pairs(act, att_body)
            for k in range(KD):
                cut_hi(act, BASE["o"], k, w_o[0][:, k, :])
            row_load(act, post_gain, I["mix_post_g"][1], post_gain_loaded)

            act.wait_ge(o_out, 1 + TILES)
            slot_hi(act, s_o, 0, 0)

            def o_body(i, last):
                slot_hi(act, s_o, i, 1)
                o_act(act, i, 0)
                if not last:
                    slot_hi(act, s_o, i + 1, 0)
                o_act(act, i, 1)

            over_pairs(act, o_body)
            ffn(1, after_phase("o"))
            ple(1)

        @block.vector
        def _(dve):
            s = s_pool
            dve.wait_ge(gain_loaded, 16)
            dve.wait_ge(pool_consts_loaded, 64)
            dve.wait_ge(post_gain_loaded, 16)
            for t in range(TILES):
                dve.wait_ge(x_loaded[t], 16) if t < 2 else None
            normed(dve, s, 0, 0)
            for j in range(2):
                cut_lo(dve, BASE["pool"], j, *[w[:, 4 * j:4 * j + 4, :] for w in w_pool])
            for t in range(2, TILES):
                dve.wait_ge(x_loaded[t], 16)

            def pool_scale(i, p):
                dve.wait_ge(s["used"][p], s.done("used", i))
                dve.wait_ge(s["ssum2"][p], s.free("ssum2", i))
                dve.tensor_tensor(pool_m[p][:, :], banks(4 + 2 * p), C["scale_row"][:, :], ALU.mult
                                  ).then_inc(s["out_scaled"][p], 1)

            def pool_body(i, last):
                slot_lo(dve, s, i, 0)
                normed(dve, s, i, 1)
                slot_lo(dve, s, i, 1)
                pool_scale(i, 0)
                if not last:
                    normed(dve, s, i + 1, 0)
                add_post(dve, s, i, 0, pool_m[0][:, :])
                pool_scale(i, 1)
                add_post(dve, s, i, 1, pool_m[1][:, :])

            over_pairs(dve, pool_body)

            def ffn(L):
                name, f, base = f"ffn{L}", F, BASE[f"ffn{L}"]
                s = S[name]
                dve.wait_ge(gain_loaded, 16 * GAIN[name])
                with dve.Fori(0, PAIRS) as i:
                    for p in range(2):
                        normed(dve, s, i, p)
                    for p in range(2):
                        c = bass.ds((2 * i + p) * P, P)
                        turned_lo(dve, s, i, p, xT[0][:, :, c], xT[1][:, :, c])
                for j in range(4):
                    cut_lo(dve, base, j, *gu_dst(j))
                dve.wait_ge(f["cleared"], L + 1)
                with dve.Fori(0, GROUPS - 1) as g:
                    ffn_dve(dve, L, g, False)

                def between(n):
                    if n in (1, 3, 5, 7):
                        k = n // 2
                        cut_lo(dve, BASE[f"ple{L}"], k, *[w[:, k, :] for w in w_pg[L]])
                    if n >= 5 and n % 2:
                        ffn_post_dve(dve, L, (n - 5) // 2)

                ffn_dve(dve, L, GROUPS - 1, True, between)
                for j in range(TILES - 2, TILES):
                    ffn_post_dve(dve, L, j)
                for k in range(4, KD):
                    cut_lo(dve, BASE[f"ple{L}"], k, *[w[:, k, :] for w in w_pg[L]])
                for k in range(2):
                    cut_lo(dve, BASE[f"ple{L}"], KD + k, *[w[:, k, :] for w in w_pp])

            def ple(L):
                name = f"ple{L}"
                s = S[name]
                dve.wait_ge(gain_loaded, 16 * GAIN[name])

                def prepare(i, p):
                    normed(dve, s, i, p)
                    p_lo(dve, L, i, p)
                    slot_lo(dve, s, i, p)

                prepare(0, 0)

                def body(i, last):
                    prepare(i, 1)
                    ple_dve(dve, L, i, 0)
                    if not last:
                        prepare(i + 1, 0)
                    ple_dve(dve, L, i, 1)

                over_pairs(dve, body)

            ffn(0)
            ple(0)
            for j in range(4):
                cut_lo(dve, BASE["kv"], j, *kv_dst(j))

            dve.wait_ge(gain_loaded, 16 * GAIN["kv"])
            dve.wait_ge(consts_loaded, 16 * 6)
            dve.wait_ge(kv_zeroed, 2)

            def kv_prepare(i, p):
                normed(dve, s_kv, i, p)
                slot_lo(dve, s_kv, i, p)

            kv_prepare(0, 0)

            def kv_body(i, last):
                kv_prepare(i, 1)
                kv_dve(dve, i, 0)
                if not last:
                    kv_prepare(i + 1, 0)
                kv_dve(dve, i, 1)

            over_pairs(dve, kv_body)
            for k in range(KD):
                cut_lo(dve, BASE["q"], k, *[w[:, k, :] for w in w_q])

            dve.wait_ge(gain_loaded, 16 * GAIN["q"])

            def q_prepare(i, p):
                normed(dve, s_q, i, p)
                slot_lo(dve, s_q, i, p)

            q_prepare(0, 0)

            def q_body(i, last):
                q_prepare(i, 1)
                q_dve(dve, i, 0)
                if not last:
                    q_prepare(i + 1, 0)
                q_dve(dve, i, 1)

            over_pairs(dve, q_body)

            def att_tile(i, p, more, nxt):
                for g in range(KV_HEADS):
                    probs_copy(dve, i, p, g, "pt_dve")
                    if g < 2:
                        softmax_dve(dve, i, p, g + 2)
                    elif more:
                        softmax_dve(dve, *nxt, g - 2)
                att_out(dve, i, p)

            softmax_dve(dve, 0, 0, 0)
            softmax_dve(dve, 0, 0, 1)

            def att_body(i, last):
                att_tile(i, 0, True, (i, 1))
                att_tile(i, 1, not last, (i + 1, 0))

            over_pairs(dve, att_body)
            for k in range(KD):
                cut_lo(dve, BASE["o"], k, *[w[:, k, :] for w in w_o])

            dve.wait_ge(post_gain_loaded, 16 * POSTG["o"])
            slot_lo(dve, s_o, 0, 0)

            def o_body(i, last):
                slot_lo(dve, s_o, i, 1)
                add_post(dve, s_o, i, 0, banks(4))
                if not last:
                    slot_lo(dve, s_o, i + 1, 0)
                add_post(dve, s_o, i, 1, banks(6))

            over_pairs(dve, o_body)
            ffn(1)
            ple(1)

        @block.tensor
        def _(pe):
            pe.wait_ge(consts_loaded, 32)
            pe.wait_ge(pool_consts_loaded, 64)

            def pool_products(i, p):
                s = s_pool
                pe.wait_ge(s["lo"][p], s.done("lo", i))
                pe.wait_ge(s["out_scaled"][p], s.free("out_scaled", i))
                pe.wait_ge(w_ready, BASE["pool"] + 2)
                for g in range(len(WINDOWS)):
                    for k in range(2):
                        last = product(pe, banks(4 + 2 * p)[:, g * GROUP:(g + 1) * GROUP],
                                       [x[p][:, 2 * g + k, :] for x in (xt_hi, xt_lo)],
                                       [x[:, 2 * g + k, :] for x in w_pool], k == 0, k == 1)
                last.then_inc(s["used"][p], 1)

            pool_band(pe, 0, 0, first=True)

            def pool_body(i, last):
                pool_band(pe, i, 1)
                pool_products(i, 0)
                if not last:
                    pool_band(pe, i + 1, 0)
                pool_products(i, 1)

            over_pairs(pe, pool_body)

            def ffn(L):
                s = S[f"ffn{L}"]
                with pe.Fori(0, PAIRS) as i:
                    for p in range(2):
                        turn(pe, s, i, p)
                for p in range(2):
                    pe.wait_ge(s["lo"][p], s.done("lo", PAIRS - 1))
                with pe.Fori(0, GROUPS) as g:
                    ffn_pe(pe, L, g)

            def turn_ahead(s, products, behind=None):
                turn(pe, s, 0, 0)

                def body(i, last):
                    products(i, 0)
                    turn(pe, s, i, 1)
                    if behind:
                        behind(i, 0)
                    products(i, 1)
                    if not last:
                        turn(pe, s, i + 1, 0)
                    if behind:
                        behind(i, 1)

                def body_ahead(i, last):
                    turn(pe, s, i, 1)
                    products(i, 0)
                    if not last:
                        turn(pe, s, i + 1, 0)
                    products(i, 1)

                over_pairs(pe, body if behind else body_ahead)

            ffn(0)
            turn_ahead(S["ple0"], lambda i, p: ple_pe(pe, 0, i, p))
            pe.wait_ge(w_ready, BASE["kv"] + 4)
            turn_ahead(s_kv, lambda i, p: kv_pe(pe, i, p), lambda i, p: kv_turn(pe, i, p))
            turn_ahead(s_q, lambda i, p: q_pe(pe, i, p), lambda i, p: q_turn(pe, i, p))

            for p in range(2):
                pe.wait_ge(k_copied[p], done(PAIRS - 1))
            pe.wait_ge(v_copied, TILES)
            pe.wait_ge(q_copied, 1 + TILES)
            scores(pe, 0, 0, 0)
            scores(pe, 0, 0, 1)

            def att_tile(i, p, more, nxt):
                for g in range(KV_HEADS):
                    turn_probs(pe, i, p, g)
                    if g < 2:
                        scores(pe, i, p, g + 2)
                    elif more:
                        scores(pe, *nxt, g - 2)
                    values(pe, i, p, g)

            def att_body(i, last):
                att_tile(i, 0, True, (i, 1))
                att_tile(i, 1, not last, (i + 1, 0))

            over_pairs(pe, att_body)

            pe.wait_ge(o_out, 1 + TILES)
            turn_ahead(s_o, lambda i, p: o_pe(pe, i, p))
            ffn(1)
            turn_ahead(S["ple1"], lambda i, p: ple_pe(pe, 1, i, p))


_INS = ["x", "mix_pre_g", "mix_post_g", "ffn_pre_g", "ffn_post_g", "pool_w", "pool_scale", "kv_norm_g", "w_k", "w_v",
        "w_q", "w_o", "sinks", "w_ff_gate", "w_ff_up", "w_ff_down", "ple_norm_g", "w_ple_gate", "w_ple_proj"]


def kernel(**inputs):
    import numpy as _np
    import concourse.bacc as _bacc
    from concourse import mybir as _mybir
    from concourse.bass_utils import run_bass_kernel_spmd as _run

    nc = _bacc.Bacc("TRN2", target_bir_lowering=False, num_devices=1, dynamic_dma_scratch_size=1024)
    arrays = {name: _np.ascontiguousarray(inputs[name]) for name in _INS}
    p = inputs["p"]
    arrays["pT"] = _np.ascontiguousarray(_np.asarray(p).reshape(p.shape[0], SEQ, PLE).transpose(0, 2, 1))
    arrays.update(constants())
    I = {}
    for name, a in arrays.items():
        I[name] = nc.dram_tensor(f"in_{name}", a.shape, _mybir.dt.from_np(a.dtype), kind="ExternalInput").ap()
    out = nc.dram_tensor("out_0", (1, SEQ, D), F32, kind="ExternalOutput").ap()
    trunk(nc, I, out)
    r = _run(nc, [{f"in_{k}": v for k, v in arrays.items()}], core_ids=[0])
    return r.results[0]["out_0"]
```

```python
from contextlib import ExitStack

import numpy as np
import concourse.bass as bass
from concourse import mybir

P = 128
F32 = mybir.dt.float32
F32R = mybir.dt.float32r
BF16 = mybir.dt.bfloat16
ALU = mybir.AluOpType
ACT = mybir.ActivationFunctionType
AX = mybir.AxisListType

D = 1024
SEQ = 1024
TILES = SEQ // P
PAIRS = TILES // 2
KD = D // P
HALF = 512
HEAD = 64
HEADS = D // HEAD
KV_HEADS = 4
GQA = HEADS // KV_HEADS
WINDOWS = (2, 4, 8, 16)
LONGEST = max(WINDOWS)
D_FF = 2816
GROUP = 256
GROUPS = D_FF // GROUP
PLE = 256
EPS = 1e-6
NEG = -1e30
SLOTS = 6
STEPS = [(0, 0), (1, 0), (0, 1), (1, 1)]


def constants():
    s, t = np.arange(P)[:, None], np.arange(P)[None, :]
    first, inner, before = [], [], []
    for w in WINDOWS:
        near = (t >= s) & (t - s < w)
        first.append(near / np.minimum(t + 1, w).astype(np.float32) - (s == t))
        inner.append(near / np.float32(w) - (s == t))
        before.append(((t + P - s < w) / np.float32(w))[:, :LONGEST])
    inv = (1.0 / (10000.0 ** (np.arange(0, HEAD, 2, dtype=np.float32) / np.float32(HEAD)))).astype(np.float32)
    angle = np.arange(SEQ, dtype=np.float32)[:, None] * inv[None, :]
    angle = angle.reshape(TILES, P, HEAD // 2).transpose(1, 0, 2)
    q, k = np.arange(P)[:, None], np.arange(-P, P)[None, :]
    valid = (q - k >= 0) & (q - k < P)
    mask = np.stack([np.where(valid & (k >= 0), 0.0, NEG), np.where(valid, 0.0, NEG)], axis=1)
    out = {
        "identity": np.eye(P),
        "band_first": np.stack(first, 1), "band_inner": np.stack(inner, 1), "band_before": np.stack(before, 1),
        "rope_cos": np.cos(angle), "rope_sin": np.sin(angle), "mask": mask,
    }
    return {k: np.ascontiguousarray(v, dtype=np.float32) for k, v in out.items()}


def done(i):
    return i + 2


def free(i):
    return i + 1


def trunk(nc, I, out):
    ctx = ExitStack()
    with ctx:
        credited = []

        def sem(name):
            return ctx.enter_context(nc.semaphore(name))

        def sem_c(name):
            s = sem(name)
            credited.append(s)
            return s

        families, rounds = {}, {}

        class Phase:

            def __init__(self, *events, count=PAIRS):
                self.base = {}
                for e in events:
                    if e not in families:
                        families[e], rounds[e] = [sem_c(f"{e}{p}") for p in range(2)], 0
                    self.base[e] = rounds[e]
                    rounds[e] += count

            def __getitem__(self, e):
                return families[e]

            def done(self, e, i):
                return done(self.base[e] + i)

            def free(self, e, i):
                return free(self.base[e] + i)

        def sb(name, shape, dt=F32):
            return ctx.enter_context(nc.sbuf_tensor(name, shape, dt))

        def region(name, elements, *uses):
            views = {}
            for use in uses:
                with ExitStack() as inner:
                    for n, shape, dt in use:
                        views[n] = inner.enter_context(nc.sbuf_tensor(n, shape, dt))
            sb(name, [P, elements])
            return views

        H = sb("H", [P, TILES * D])
        raw = [sb(f"raw{i}", [P, D]) for i in range(SLOTS)]
        xn = [sb(f"xn{p}", [P, D]) for p in range(2)]
        tmp = sb("tmp", [P, D])
        gain = sb("gain", [P, D])
        ident = sb("ident", [P, P])
        small = sb("small", [P, 64])
        sinks = sb("sinks_row", [P, HEADS])

        def weights(name, shape):
            return [(name + "_hi", shape, F32R), (name + "_lo", shape, F32R)]

        A = region("A", 16 * D,
                   weights("xT", [P, KD, SEQ]),
                   weights("w_ple_gate0", [P, KD, D]), weights("w_ple_gate1", [P, KD, D]),
                   weights("w_q", [P, KD, D]), weights("w_o", [P, KD, D]), [("pool_squares", [P, 2, D], F32)])
        B = region("B", 8 * D,
                   weights("wg", [P, KD, GROUP]) + weights("wu", [P, KD, GROUP]),
                   weights("w_kv", [P, KD, 2 * GROUP]),
                   [("pool_m0", [P, D], F32), ("pool_m1", [P, D], F32)],
                   [("qo", [P, TILES, D], F32)])
        C = region("C", 8 * D,
                   weights("wd", [P, 2, D]) + weights("a", [P, 2, SEQ]),
                   weights("w_ple_proj", [P, 2, D]) + weights("pT0", [P, 2, P]) + weights("pT1", [P, 2, P])
                   + [("p_raw0", [P, 2, P], F32), ("p_raw1", [P, 2, P], F32)],
                   weights("w_pool", [P, KD, GROUP])
                   + [("band_first", [P, 4, P], F32), ("band_inner", [P, 4, P], F32),
                      ("band_before", [P, 4, LONGEST], F32), ("scale_row", [P, D], F32)],
                   [("kT", [P, TILES + 1, KV_HEADS, P], F32), ("V", [P, TILES + 1, GROUP], F32),
                    ("mask0", [P, 2 * P], F32), ("mask1", [P, 2 * P], F32),
                    ("cos", [P, TILES, 32], F32), ("sin", [P, TILES, 32], F32)],
                   [("o_squares", [P, 2, D], F32)])
        DD = region("DD", 4 * D,
                    weights("xt0", [P, KD, P]) + weights("xt1", [P, KD, P]),
                    [("sig", [P, 2, HALF], F32), ("act0", [P, HALF], F32),
                     ("act1", [P, HALF], F32), ("back0", [P, D], F32), ("back1", [P, D], F32)],
                    [("q_tile0", [P, HEADS, P], F32), ("q_tile1", [P, HEADS, P], F32)])
        E = region("E", D,
                   [("post_gain", [P, D], F32)], [("ple_sig", [P, 2, HALF], F32)],
                   [("k_rot", [P, KV_HEADS, 2, HEAD], F32), ("rope_a", [P, 256], F32), ("rope_b", [P, 256], F32)],
                   [("pt1", [P, KD, P], F32)])
        xt_hi, xt_lo = [DD["xt0_hi"], DD["xt1_hi"]], [DD["xt0_lo"], DD["xt1_lo"]]
        post_gain = E["post_gain"]
        kT, V = C["kT"], C["V"]
        qo = B["qo"]
        pool_m = [B["pool_m0"], B["pool_m1"]]

        ssum, mean, rstd = [[small[:, 2 * n + p:2 * n + p + 1] for p in range(2)] for n in range(3)]
        ssum2, mean2, rstd2 = [[small[:, 6 + 2 * n + p:7 + 2 * n + p] for p in range(2)] for n in range(3)]
        minus_half, eps = small[:, 12:13], small[:, 13:14]
        row_max = [small[:, 16 + 4 * p:20 + 4 * p] for p in range(2)]
        neg_max = [small[:, 24 + 4 * p:28 + 4 * p] for p in range(2)]
        sink_gap = [small[:, 32 + 4 * p:36 + 4 * p] for p in range(2)]
        sums = [sb(f"sums{p}", [P, HEADS]) for p in range(2)]
        sink_exp = [sb(f"sink_exp{p}", [P, HEADS]) for p in range(2)]
        recip = sb("recip", [P, HEADS])

        ps = ctx.enter_context(nc.psum_tensor("ps", [P, 8, HALF], F32))

        def banks(b, n=2):
            return ps[:, b:b + n, :].rearrange("p b c -> p (b c)")

        spill = nc.dram_tensor("residual_spill", (2, P, TILES * D), F32, kind="Internal").ap()

        units = []

        def rows(w, k):
            return w[k * P:(k + 1) * P, :]

        def quarter(w, j):
            return w.rearrange("(k p) n -> p k n", p=P)[:, 4 * j:4 * j + 4, :]

        BASE, n = {}, 0
        for name, count in (("pool", 2), ("ffn0", 6 * GROUPS), ("ple0", 10), ("kv", 4), ("q", 8), ("o", 8),
                            ("ffn1", 6 * GROUPS), ("ple1", 10)):
            BASE[name] = n
            n += count
        raw_loaded = [sem(f"raw_loaded{i}") for i in range(SLOTS)]
        hi_done = sem("weight_hi_done")
        w_ready = sem("weights_ready")

        def loaded(base, j, g=0):
            return raw_loaded[(base + j) % SLOTS], 16 * ((base + j) // SLOTS + 1 + g)

        def shape_of(dst, src):
            free_dims = dst.shape[1:]
            if len(free_dims) == 1:
                return src[:, :]
            return src[:, :].rearrange("p (k n) -> p k n", k=free_dims[0])

        def load_unit(sp, base, j, src, g=0):
            if not isinstance(g, int) or base + j + 6 * g >= SLOTS:
                sp.wait_ge(w_ready, base + j + 6 * g - SLOTS + 1)
            slot = raw[(base + j) % SLOTS]
            sp.dma_start(shape_of(src, slot), src).then_inc(loaded(base, j)[0], 16)

        def cut_hi(act, base, j, dst, g=0):
            s, value = loaded(base, j, g)
            act.wait_ge(s, value)
            act.activation(dst, shape_of(dst, raw[(base + j) % SLOTS]), ACT.Copy).then_inc(hi_done, 1)

        def cut_lo(dve, base, j, dst_hi, dst_lo, g=0):
            dve.wait_ge(hi_done, base + j + 6 * g + 1)
            dve.tensor_tensor(dst_lo, shape_of(dst_lo, raw[(base + j) % SLOTS]), dst_hi.bitcast(F32),
                              ALU.subtract).then_inc(w_ready, 1)

        def product(pe, out_, lhs, rhs, first, last):
            pe.matmul(out_, lhs[0], rhs[0], start=first, stop=False)
            pe.matmul(out_, lhs[0], rhs[1], start=False, stop=False)
            return pe.matmul(out_, lhs[1], rhs[0], start=False, stop=last)

        consts_loaded = sem("consts_loaded")
        pool_consts_loaded = sem("pool_consts_loaded")
        x_loaded = [sem(f"x_loaded{t}") for t in range(TILES)]
        gain_loaded = sem("gain_loaded")
        post_gain_loaded = sem("post_gain_loaded")
        consts_set = sem("consts_set")
        TURN = ("xn", "turned", "hi", "lo")
        MEAN = ("ssum", "mean", "rstd")
        POST = ("ssum2", "mean2", "rstd2", "scaled", "added")
        EMBED = ("p_hi", "p_lo")
        S = {}
        S["pool"] = Phase(*TURN, *MEAN, "used", *POST, "out_scaled")
        S["ffn0"] = Phase(*TURN, *MEAN)
        S["ple0"] = Phase(*TURN, *MEAN, "used", *EMBED)
        S["kv"] = Phase(*TURN, *MEAN, "used", "rotated", "k_turned")
        S["q"] = Phase(*TURN, *MEAN, "used")
        S["att"] = Phase("q_tile")
        S["o"] = Phase(*TURN, "used", *POST)
        S["ffn1"] = Phase(*TURN, *MEAN)
        S["ple1"] = Phase(*TURN, *MEAN, "used", *EMBED)
        att = Phase("scores", "masked", "max", "neg_max", "probs", "p_turned", "pt_act", "pt_dve", "pv", count=TILES * 2)
        p_loaded = [[sem(f"p_loaded{L}{p}") for p in range(2)] for L in range(2)]
        stored = sem("stored")

        def tile(i, p):
            return bass.ds((2 * i + p) * D, D)

        def square_sum(act, s, i, p, ready=None):
            act.wait_ge(s["turned"][p], s.free("turned", i))
            if ready:
                ready(act, i, p)
            act.activation(xn[p][:, :], H[:, tile(i, p)], ACT.Square, scale=D ** -0.5, accum_out=ssum[p]).then_inc(s["ssum"][p], 1)

        def inv_rms(pool, s, i, p, sums_, mean_, rstd_, names=("ssum", "mean", "rstd")):
            pool.wait_ge(s[names[0]][p], s.done(names[0], i))
            pool.tensor_tensor(mean_, sums_, eps, ALU.add).then_inc(s[names[1]][p], 1)
            pool.wait_ge(s[names[1]][p], s.done(names[1], i))
            pool.tensor_tensor(rstd_, mean_, minus_half, ALU.pow).then_inc(s[names[2]][p], 1)

        def normed(dve, s, i, p):
            dve.wait_ge(s["rstd"][p], s.done("rstd", i))
            dve.scalar_tensor_tensor(out=xn[p][:, :], in0=H[:, tile(i, p)], scalar=rstd[p], in1=gain[:, :],
                                     op0=ALU.mult, op1=ALU.mult).then_inc(s["xn"][p], 1)

        def t_banks(s, p):
            return banks(2 * p if s in (S["ffn0"], S["ffn1"]) else 0)

        def t_banks_read(pe, s, i, p):
            if s in (S["ffn0"], S["ffn1"]):
                pe.wait_ge(s["lo"][p], s.free("lo", i))
            else:
                pe.wait_ge(s["lo"][1 - p], s.done("lo", i) if p else s.free("lo", i))

        def turn(pe, s, i, p):
            pe.wait_ge(s["xn"][p], s.done("xn", i))
            t_banks_read(pe, s, i, p)
            for k in range(KD):
                last = pe.transpose(t_banks(s, p)[:, k * P:(k + 1) * P], xn[p][:, k * P:(k + 1) * P], ident[:, :])
            last.then_inc(s["turned"][p], 1)

        def turned_hi(act, s, i, p, dst):
            act.wait_ge(s["turned"][p], s.done("turned", i))
            if "used" in s.base:
                act.wait_ge(s["used"][p], s.free("used", i))
            act.activation(dst, t_banks(s, p).rearrange("p (k c) -> p k c", k=KD), ACT.Copy).then_inc(s["hi"][p], 1)

        def turned_lo(dve, s, i, p, hi, lo):
            dve.wait_ge(s["hi"][p], s.done("hi", i))
            dve.tensor_tensor(lo, t_banks(s, p).rearrange("p (k c) -> p k c", k=KD), hi.bitcast(F32),
                              ALU.subtract).then_inc(s["lo"][p], 1)

        def slot_hi(act, s, i, p):
            turned_hi(act, s, i, p, xt_hi[p][:, :, :])

        def slot_lo(dve, s, i, p):
            turned_lo(dve, s, i, p, xt_hi[p][:, :, :], xt_lo[p][:, :, :])

        def staggered(eng, *parts):
            def step(i, p):
                for d, work in parts:
                    n = p + d
                    if not isinstance(i, int) or 0 <= 2 * i + n < TILES:
                        work(i + n // 2 if n // 2 else i, n % 2)

            for t in range(-2, 2):
                step(t // 2, t % 2)
            with eng.Fori(1, PAIRS - 1) as i:
                for p in range(2):
                    step(i, p)
            for t in range(TILES - 2, TILES + 1):
                step(t // 2, t % 2)

        def over_pairs(eng, body):
            with eng.Fori(0, PAIRS - 1) as i:
                body(i, False)
            body(PAIRS - 1, True)

        def add_post(dve, s, i, p, src):
            dve.wait_ge(s["rstd2"][p], s.done("rstd2", i))
            dve.wait_ge(s["added"][1 - p], s.done("added", i) if p else s.free("added", i))
            dve.scalar_tensor_tensor(out=tmp[:, :], in0=src, scalar=rstd2[p], in1=post_gain[:, :],
                                     op0=ALU.mult, op1=ALU.mult).then_inc(s["scaled"][p], 1)
            dve.wait_ge(s["scaled"][p], s.done("scaled", i))
            dve.tensor_tensor(H[:, tile(i, p)], H[:, tile(i, p)], tmp[:, :], ALU.add).then_inc(s["added"][p], 1)

        ple_added = [sem_c(f"ple{n}_added") for n in range(2)]
        post_added = [sem_c(f"ffn{n}_post_added") for n in range(2)]

        def after_x(eng, i, p):
            pass

        def after_phase(name):
            def ready(eng, i, p):
                eng.wait_ge(S[name]["added"][p], done(PAIRS - 1))
            return ready

        def after_count(s, per_tile):
            def ready(eng, i, p):
                eng.wait_ge(s, 1 + per_tile * TILES)
            return ready

        def row_load(eng, dst, src, s):
            eng.dma_start(dst[:, :], src.partition_broadcast(P)).then_inc(s, 16)

        GAIN = {"pool": 1, "ffn0": 2, "ple0": 3, "kv": 4, "q": 5, "ffn1": 6, "ple1": 7}
        POSTG = {"pool": 1, "ffn0": 2, "o": 3, "ffn1": 4}

        w_pool = (C["w_pool_hi"], C["w_pool_lo"])
        s_pool = S["pool"]
        xn_pool_ready = s_pool["xn"]
        pool_junk = DD["xt0_hi"]

        def pool_band(pe, i, p):
            s = s_pool
            first = isinstance(i, int) and i == 0 and p == 0
            pe.wait_ge(s["xn"][p], s.done("xn", i))
            t_banks_read(pe, s, i, p)
            for c in range(KD):
                w = c // 2
                band = C["band_first"] if first else C["band_inner"]
                o = t_banks(s, p)[:, c * P:(c + 1) * P]
                last = pe.matmul(o, xn[p][:, c * P:(c + 1) * P], band[:, w, :], start=True, stop=first)
                if not first:
                    last = pe.matmul(o[:, 0:LONGEST], xn[1 - p][:, c * P:(c + 1) * P], C["band_before"][:, w, :],
                                     start=False, stop=True)
            last.then_inc(s["turned"][p], 1)

        def pool_square_sum(act, i, p):
            s = s_pool
            if p == 0:
                act.wait_ge(s["turned"][1], s.free("turned", i))
            else:
                act.wait_ge(s["turned"][0], s.done("turned", i))
            act.activation(xn[p][:, :], H[:, tile(i, p)], ACT.Square, scale=D ** -0.5, accum_out=ssum[p]).then_inc(s["ssum"][p], 1)

        xT = (A["xT_hi"], A["xT_lo"])
        wg, wu, wd = (B["wg_hi"], B["wg_lo"]), (B["wu_hi"], B["wu_lo"]), (C["wd_hi"], C["wd_lo"])
        a = (C["a_hi"], C["a_lo"])
        sig, act32 = DD["sig"], [DD["act0"], DD["act1"]]
        back = [DD["back0"], DD["back1"]]
        F = {
            "gate": sem_c("ffn_gate_ready"), "up": sem_c("ffn_up_ready"),
            "sig": sem_c("ffn_sigmoid_done"), "prod": sem_c("ffn_silu_done"),
            "act": [sem_c(f"ffn_act_done{p}") for p in range(2)],
            "a_hi": sem_c("ffn_a_hi_done"), "a_lo": sem_c("ffn_a_ready"),
            "down": sem_c("ffn_down_ready"), "summed": [sem_c(f"ffn_summed{b}") for b in range(4)],
            "spilled": sem("ffn_spilled"), "cleared": sem("ffn_cleared"),
            "back": [sem(f"ffn_back_loaded{p}") for p in range(2)],
            "ssum2": sem("ffn_out_ssum"), "mean2": sem("ffn_out_mean"), "rstd2": sem("ffn_out_rstd"),
            "scaled": sem("ffn_out_scaled"),
        }

        def gu_dst(j):
            w = wg if j < 2 else wu
            k = 4 * (j % 2)
            return w[0][:, k:k + 4, :], w[1][:, k:k + 4, :]

        def ffn_pe(pe, L, g):
            f, base, r = F, BASE[f"ffn{L}"], GROUPS * L + g
            for n, (t, h) in enumerate(STEPS):
                b = 2 * (n % 2)
                pe.wait_ge(f["act"][n % 2], free(2 * r + n // 2))
                for m, (w, ready) in enumerate(((wg, "gate"), (wu, "up"))):
                    for k in range(KD):
                        if n == 0 and k % 4 == 0:
                            pe.wait_ge(w_ready, base + 6 * g + 2 * m + k // 4 + 1)
                        last = product(pe, ps[:, b + m, :],
                                       [x[:, k, t * P:(t + 1) * P] for x in w],
                                       [x[:, k, h * HALF:(h + 1) * HALF] for x in xT], k == 0, k == KD - 1)
                    last.then_inc(f[ready], 1)
            for n in range(2 * TILES):
                j, c = n // 2, n % 2
                if n == 0:
                    pe.wait_ge(w_ready, base + 6 * g + 6)
                    pe.wait_ge(f["a_lo"], 1 + 4 * r + 2)
                if n == TILES:
                    pe.wait_ge(f["a_lo"], 1 + 4 * r + 4)
                pe.wait_ge(f["summed"][n % 4], free(4 * r + n // 4))
                for t in range(2):
                    last = product(pe, ps[:, 4 + n % 4, :], [x[:, t, j * P:(j + 1) * P] for x in a],
                                   [x[:, t, c * HALF:(c + 1) * HALF] for x in wd], t == 0, t == 1)
                last.then_inc(f["down"], 1)

        def ffn_act(act, L, g, last_group):
            f, base, r = F, BASE[f"ffn{L}"], GROUPS * L + g
            act.wait_ge(f["down"], 1 + 16 * r)
            for t in range(2):
                cut_hi(act, base, 4 + t, wd[0][:, t, :], g)
            for n, (t, h) in enumerate(STEPS):
                act.wait_ge(f["gate"], 1 + 4 * r + n + 1)
                act.wait_ge(f["act"][n % 2], free(2 * r + n // 2))
                act.activation(sig[:, n % 2, :], ps[:, 2 * (n % 2), :], ACT.Sigmoid).then_inc(f["sig"], 1)
                act.wait_ge(f["act"][n % 2], done(2 * r + n // 2))
                act.activation(a[0][:, t, h * HALF:(h + 1) * HALF], act32[n % 2][:, :], ACT.Copy).then_inc(f["a_hi"], 1)
            if not last_group:
                act.wait_ge(f["up"], 1 + 4 * r + 4)
                for j in range(4):
                    cut_hi(act, base, j, gu_dst(j)[0], g + 1)

        def ffn_dve(dve, L, g, last_group, between=None):
            f, base, r = F, BASE[f"ffn{L}"], GROUPS * L + g
            for t in range(2):
                cut_lo(dve, base, 4 + t, wd[0][:, t, :], wd[1][:, t, :], g)
            for n, (t, h) in enumerate(STEPS):
                dve.wait_ge(f["sig"], 1 + 4 * r + n + 1)
                dve.tensor_tensor(sig[:, n % 2, :], ps[:, 2 * (n % 2), :], sig[:, n % 2, :], ALU.mult).then_inc(f["prod"], 1)
                dve.wait_ge(f["prod"], 1 + 4 * r + n + 1)
                dve.wait_ge(f["up"], 1 + 4 * r + n + 1)
                dve.tensor_tensor(act32[n % 2][:, :], ps[:, 2 * (n % 2) + 1, :], sig[:, n % 2, :],
                                  ALU.mult).then_inc(f["act"][n % 2], 1)
                dve.wait_ge(f["a_hi"], 1 + 4 * r + n + 1)
                hs = slice(h * HALF, (h + 1) * HALF)
                dve.tensor_tensor(a[1][:, t, hs], act32[n % 2][:, :], a[0][:, t, hs].bitcast(F32),
                                  ALU.subtract).then_inc(f["a_lo"], 1)
            for n in range(2 * TILES):
                j, c = n // 2, n % 2
                dve.wait_ge(f["down"], 1 + 16 * r + n + 1)
                dst = H[:, j * D + c * HALF:j * D + (c + 1) * HALF]
                dve.tensor_tensor(dst, dst, ps[:, 4 + n % 4, :], ALU.add).then_inc(f["summed"][n % 4], 1)
                if not last_group and n in (4, 7, 10, 13):
                    u = (n - 4) // 3
                    cut_lo(dve, base, u, *gu_dst(u), g + 1)
                if last_group and between:
                    between(n)

        def ffn_post_act(act, L):
            f, n0 = F, TILES * L
            for j in range(TILES):
                for n in (2 * j, 2 * j + 1):
                    act.wait_ge(f["summed"][n % 4], 1 + 4 * (GROUPS * (L + 1) - 1) + n // 4 + 1)
                if n0 + j >= 1:
                    act.wait_ge(f["mean2"], n0 + j)
                act.activation(sig[:, :, :].rearrange("p a b -> p (a b)"), H[:, j * D:(j + 1) * D], ACT.Square, scale=D ** -0.5,
                               accum_out=ssum2[0]).then_inc(f["ssum2"], 1)

        def ffn_post_pool(pool, L):
            f, n0 = F, TILES * L
            for j in range(TILES):
                pool.wait_ge(f["ssum2"], n0 + j + 1)
                if n0 + j >= 1:
                    pool.wait_ge(f["rstd2"], n0 + j)
                pool.tensor_tensor(mean2[0], ssum2[0], eps, ALU.add).then_inc(f["mean2"], 1)
                pool.wait_ge(f["mean2"], n0 + j + 1)
                if n0 + j >= 1:
                    pool.wait_ge(f["scaled"], n0 + j)
                pool.tensor_tensor(rstd2[0], mean2[0], minus_half, ALU.pow).then_inc(f["rstd2"], 1)

        def ffn_post_dve(dve, L, j):
            f, n0 = F, TILES * L
            dve.wait_ge(f["rstd2"], n0 + j + 1)
            dve.wait_ge(post_gain_loaded, 16 * POSTG[f"ffn{L}"])
            Hj = H[:, j * D:(j + 1) * D]
            dve.scalar_tensor_tensor(out=Hj, in0=Hj, scalar=rstd2[0], in1=post_gain[:, :],
                                     op0=ALU.mult, op1=ALU.mult).then_inc(f["scaled"], 1)
            dve.wait_ge(f["scaled"], n0 + j + 1)
            dve.wait_ge(f["back"][j % 2], 16 * (PAIRS * L + j // 2 + 1))
            dve.tensor_tensor(Hj, Hj, back[j % 2][:, :], ALU.add).then_inc(post_added[L], 1)

        w_pg = [(A[f"w_ple_gate{L}_hi"], A[f"w_ple_gate{L}_lo"]) for L in range(2)]
        w_pp = (C["w_ple_proj_hi"], C["w_ple_proj_lo"])
        pT = [(C[f"pT{p}_hi"], C[f"pT{p}_lo"]) for p in range(2)]
        p_raw = [C["p_raw0"], C["p_raw1"]]
        ple_sig = E["ple_sig"]
        G = {
            "gate": [sem_c(f"ple_gate_ready{c}") for c in range(2)],
            "proj": sem_c("ple_proj_ready0"),
            "sig": [sem_c(f"ple_sigmoid_done{c}") for c in range(2)],
            "prod": [sem_c(f"ple_gated{c}") for c in range(2)],
        }

        def ple_pe(pe, L, i, p):
            g, s, t = G, S[f"ple{L}"], TILES * L + 2 * i + p
            pe.wait_ge(s["lo"][p], s.done("lo", i))
            for c in range(2):
                if not isinstance(i, int) or i > 0:
                    pe.wait_ge(g["sig"][c], free(t - 1))
                for k in range(KD):
                    if isinstance(i, int) and i == 0 and p == 0 and c == 0:
                        pe.wait_ge(w_ready, BASE[f"ple{L}"] + k + 1)
                    last = product(pe, ps[:, 2 + 2 * p + c, :], [x[p][:, k, :] for x in (xt_hi, xt_lo)],
                                   [x[:, k, c * HALF:(c + 1) * HALF] for x in w_pg[L]], k == 0, k == KD - 1)
                last.then_inc(g["gate"][c], 1)
            pe.wait_ge(s["p_lo"][p], s.done("p_lo", i))
            pe.wait_ge(w_ready, BASE[f"ple{L}"] + 10)
            for c in range(2):
                pe.wait_ge(g["prod"][c], free(t))
                for k in range(2):
                    last = product(pe, ps[:, 6 + c, :], [x[:, k, :] for x in pT[p]],
                                   [x[:, k, c * HALF:(c + 1) * HALF] for x in w_pp], k == 0, k == 1)
                last.then_inc(g["proj"] if c == 0 else s["used"][p], 1)

        def ple_act(act, L, i, p):
            g, t = G, TILES * L + 2 * i + p
            for c in range(2):
                act.wait_ge(g["gate"][c], done(t))
                act.wait_ge(g["prod"][c], free(t))
                act.activation(ple_sig[:, c, :], ps[:, 2 + 2 * p + c, :], ACT.Sigmoid).then_inc(g["sig"][c], 1)

        def ple_dve(dve, L, i, p):
            g, s, t = G, S[f"ple{L}"], TILES * L + 2 * i + p
            dve.wait_ge(ple_added[L], 1 + 2 * (2 * i + p))
            for c in range(2):
                dve.wait_ge(g["sig"][c], done(t))
                if c == 0:
                    dve.wait_ge(g["proj"], done(t))
                else:
                    dve.wait_ge(s["used"][p], s.done("used", i))
                dve.tensor_tensor(tmp[:, c * HALF:(c + 1) * HALF], ps[:, 6 + c, :], ple_sig[:, c, :],
                                  ALU.mult).then_inc(g["prod"][c], 1)
            for c in range(2):
                dve.wait_ge(g["prod"][c], done(t))
                dst = H[:, bass.ds((2 * i + p) * D + c * HALF, HALF)]
                dve.tensor_tensor(dst, dst, tmp[:, c * HALF:(c + 1) * HALF], ALU.add).then_inc(ple_added[L], 1)

        def p_load(sp, L, i, p):
            s = S[f"ple{L}"]
            sp.wait_ge(s["p_lo"][p], s.free("p_lo", i))
            sp.dma_start(p_raw[p][:, :, :], I["pT"][L].rearrange("(k c) t -> c k t", c=P)[:, :, bass.ds((2 * i + p) * P, P)]
                         ).then_inc(p_loaded[L][p], 16)

        def p_hi(act, L, i, p):
            s = S[f"ple{L}"]
            act.wait_ge(p_loaded[L][p], 16 * i + 16)
            act.wait_ge(s["used"][p], s.free("used", i))
            act.activation(pT[p][0][:, :, :], p_raw[p][:, :, :], ACT.Copy).then_inc(s["p_hi"][p], 1)

        def p_lo(dve, L, i, p):
            s = S[f"ple{L}"]
            dve.wait_ge(s["p_hi"][p], s.done("p_hi", i))
            dve.tensor_tensor(pT[p][1][:, :, :], p_raw[p][:, :, :], pT[p][0][:, :, :].bitcast(F32),
                              ALU.subtract).then_inc(s["p_lo"][p], 1)

        w_kv = (B["w_kv_hi"], B["w_kv_lo"])
        k_rot, rope_a, rope_b = E["k_rot"], E["rope_a"], E["rope_b"]
        s_kv = S["kv"]
        k_copied = [sem_c(f"kv_k_copied{p}") for p in range(2)]
        v_copied = sem("v_copied")
        rope_step = sem("rope_step")
        kv_zeroed = sem("kv_zeroed")
        q_zeroed = sem("q_zeroed")

        def kv_dst(j):
            k, c = 4 * (j % 2), GROUP * (j // 2)
            return [w[:, k:k + 4, c:c + GROUP] for w in w_kv]

        def kv_pe(pe, i, p):
            s = s_kv
            pe.wait_ge(s["lo"][p], s.done("lo", i))
            pe.wait_ge(s["rotated"][p], s.free("rotated", i))
            for k in range(KD):
                last = product(pe, ps[:, 2 + p, :], [x[p][:, k, :] for x in (xt_hi, xt_lo)],
                               [x[:, k, :] for x in w_kv], k == 0, k == KD - 1)
            last.then_inc(s["used"][p], 1)

        def kv_turn(pe, i, p):
            s = s_kv
            pe.wait_ge(s["rotated"][p], s.done("rotated", i))
            pe.wait_ge(k_copied[p], free(i))
            for n in range(KV_HEADS):
                last = pe.transpose(ps[:, 6 + p, n * P:(n + 1) * P], k_rot[:, n, :, :].rearrange("p a b -> p (a b)"),
                                    ident[:, :])
            last.then_inc(s["k_turned"][p], 1)

        def kv_act(act, i, p):
            act.wait_ge(s_kv["k_turned"][p], s_kv.done("k_turned", i))
            act.activation(kT[:, bass.ds(2 * i + p + 1, 1), :, :].rearrange("p a b c -> p (a b c)"),
                           ps[:, 6 + p, :], ACT.Copy).then_inc(k_copied[p], 1)

        def rope(dve, base, src1, src2, c, s, dst1, dst2, ta, tb, bank_read, n=1):
            dve.tensor_tensor(ta, src1, c, ALU.mult).then_inc(rope_step, 1)
            dve.tensor_tensor(tb, src2, s, ALU.mult).then_inc(rope_step, 1)
            dve.wait_ge(rope_step, base + 2)
            dve.tensor_tensor(dst1[0], dst1[1](ta), dst1[1](tb), ALU.subtract).then_inc(rope_step, 1)
            dve.wait_ge(rope_step, base + 3)
            dve.tensor_tensor(ta, src2, c, ALU.mult).then_inc(rope_step, 1)
            dve.tensor_tensor(tb, src1, s, ALU.mult).then_inc(rope_step, 1)
            dve.wait_ge(rope_step, base + 5)
            dve.tensor_tensor(dst2[0], dst2[1](ta), dst2[1](tb), ALU.add).then_inc(bank_read, 1)

        def table(name, i, p, heads):
            return C[name][:, bass.ds(2 * i + p, 1), :].to_broadcast([P, heads, 32])

        def kv_dve(dve, i, p):
            s = s_kv
            dve.wait_ge(s["used"][p], s.done("used", i))
            dve.tensor_copy(V[:, bass.ds(2 * i + p + 1, 1), :].rearrange("p a b -> p (a b)"),
                            ps[:, 2 + p, GROUP:2 * GROUP]).then_inc(v_copied, 1)
            dve.wait_ge(s["k_turned"][1 - p], s.done("k_turned", i) if p else s.free("k_turned", i))
            k4 = ps[:, 2 + p, 0:GROUP].rearrange("p (h d) -> p h d", d=HEAD)
            ta = rope_a[:, 0:128].rearrange("p (h d) -> p h d", d=32)
            tb = rope_b[:, 0:128].rearrange("p (h d) -> p h d", d=32)
            dve.wait_ge(s["rotated"][1 - p], s.done("rotated", i) if p else s.free("rotated", i))
            twice = lambda x: x.unsqueeze(2).to_broadcast([P, KV_HEADS, 2, 32])
            rope(dve, (2 * i + p) * 5, k4[:, :, 0:32], k4[:, :, 32:64], table("cos", i, p, KV_HEADS),
                 table("sin", i, p, KV_HEADS), (k_rot[:, :, :, 0:32], twice), (k_rot[:, :, :, 32:64], twice),
                 ta, tb, s["rotated"][p])

        w_q = (A["w_q_hi"], A["w_q_lo"])
        s_q = S["q"]
        q_out = [sem_c(f"q_out_ready{c}") for c in range(2)]
        q_rot = [sem_c(f"q_rotated{c}") for c in range(2)]
        q_turned, q_copied = sem_c("q_turned"), sem_c("q_copied")

        def q_pe(pe, i, p, halves):
            t = 2 * i + p
            pe.wait_ge(s_q["lo"][p], s_q.done("lo", i))
            for c in halves:
                if not isinstance(i, int) or i > 0:
                    pe.wait_ge(q_rot[c], free(t - 1))
                for k in range(KD):
                    if isinstance(i, int) and i == 0 and p == 0:
                        pe.wait_ge(w_ready, BASE["q"] + k + 1)
                    last = product(pe, ps[:, 2 + 2 * p + c, :], [x[p][:, k, :] for x in (xt_hi, xt_lo)],
                                   [x[:, k, c * HALF:(c + 1) * HALF] for x in w_q], k == 0, k == KD - 1)
                last.then_inc(q_out[c] if c == 0 else s_q["used"][p], 1)

        def q_turn(pe, i, p):
            t = 2 * i + p
            for c in range(2):
                pe.wait_ge(q_rot[c], done(t))
            pe.wait_ge(q_copied, free(t))
            if isinstance(i, int) and i == 0 and p == 0:
                for par in range(2):
                    pe.wait_ge(k_copied[par], done(PAIRS - 1))
            for k in range(KD):
                last = pe.transpose(banks(6)[:, k * P:(k + 1) * P], tmp[:, k * P:(k + 1) * P], ident[:, :])
            last.then_inc(q_turned, 1)

        def q_act(act, i, p):
            t = 2 * i + p
            act.wait_ge(q_turned, done(t))
            act.activation(qo[:, bass.ds(t, 1), :].rearrange("p a b -> p (a b)"), banks(6), ACT.Copy).then_inc(q_copied, 1)

        def q_dve(dve, i, p):
            t = 2 * i + p
            for c in range(2):
                if c == 0:
                    dve.wait_ge(q_out[0], done(t))
                    dve.wait_ge(q_turned, free(t))
                    dve.wait_ge(q_rot[1], free(t))
                else:
                    dve.wait_ge(s_q["used"][p], s_q.done("used", i))
                    dve.wait_ge(q_rot[0], done(t))
                h8 = ps[:, 2 + 2 * p + c, :].rearrange("p (h d) -> p h d", d=HEAD)
                o8 = tmp[:, c * HALF:(c + 1) * HALF].rearrange("p (h d) -> p h d", d=HEAD)
                ta, tb = [x[:, :].rearrange("p (h d) -> p h d", d=32) for x in (rope_a, rope_b)]
                same = lambda x: x
                rope(dve, 5 * TILES + (2 * t + c) * 5, h8[:, :, 0:32], h8[:, :, 32:64], table("cos", i, p, 8),
                     table("sin", i, p, 8), (o8[:, :, 0:32], same), (o8[:, :, 32:64], same), ta, tb, q_rot[c])

        s_a = S["att"]
        q_tile = [DD["q_tile0"], DD["q_tile1"]]
        pt = [tmp[:, :].rearrange("p (k c) -> p k c", k=KD), E["pt1"]]
        mask = [C["mask0"], C["mask1"]]
        o_ready, o_out = sem_c("o_ready"), sem_c("o_read_out")
        sink_dve, sink_act = sem_c("sink_gap_done"), sem_c("sink_exp_done")
        mask_set = sem("mask0_set")
        sums_read = [sem_c(f"sums_read{p}") for p in range(2)]
        recip_done = sem("recip_done")
        att_max1 = [sem_c(f"att_row_max{p}") for p in range(2)]

        def scores(pe, i, p, g):
            par, r = g % 2, 4 * i + 2 * p + g // 2
            if g == 0:
                pe.wait_ge(s_a["q_tile"][p], s_a.done("q_tile", i))
            pe.wait_ge(att["masked"][par], att.free("masked", r))
            for m in range(GQA):
                h = GQA * g + m
                last = pe.matmul(banks(2 * par)[:, m * 256:(m + 1) * 256].rearrange("p (b c) -> p b c", b=2),
                                 q_tile[p][:, h, :], kT[:, bass.ds(2 * i + p, 2), g, :], start=True, stop=True)
            last.then_inc(att["scores"][par], 1)

        def softmax_dve(dve, i, p, g):
            par, r = g % 2, 4 * i + 2 * p + g // 2
            dve.wait_ge(att["scores"][par], att.done("scores", r))
            dve.wait_ge(att["p_turned"][par], att.free("p_turned", r))
            if g == 0 and p == 0 and not (isinstance(i, int) and i == 0):
                dve.tensor_copy(mask[0][:, :], mask[1][:, :]).then_inc(mask_set, 1)
                dve.wait_ge(mask_set, i)
            S3 = xn[par][:, :].rearrange("p (h k) -> p h k", h=GQA)
            m3 = mask[p][:, :].unsqueeze(1).to_broadcast([P, GQA, 2 * P])
            dve.scalar_tensor_tensor(out=S3, in0=banks(2 * par).rearrange("p (h k) -> p h k", h=GQA),
                                     scalar=HEAD ** -0.5, in1=m3, op0=ALU.mult, op1=ALU.add
                                     ).then_inc(att["masked"][par], 1)
            dve.wait_ge(att["masked"][par], att.done("masked", r))
            dve.tensor_reduce(row_max[par], S3, AX.X, ALU.max).then_inc(att_max1[par], 1)
            dve.wait_ge(att_max1[par], done(r))
            dve.wait_ge(att["probs"][par], att.free("probs", r))
            sk = sinks[:, GQA * g:GQA * (g + 1)]
            dve.tensor_tensor(row_max[par], row_max[par], sk, ALU.max).then_inc(att["max"][par], 1)
            dve.wait_ge(att["max"][par], att.done("max", r))
            dve.tensor_scalar(neg_max[par], row_max[par], -1.0, None, ALU.mult).then_inc(att["neg_max"][par], 1)
            dve.tensor_tensor(sink_gap[par], sk, row_max[par], ALU.subtract).then_inc(sink_dve, 1)

        def q_to_place(act, i, p):
            if not isinstance(i, int) or i > 0:
                act.wait_ge(att["scores"][1], 1 + 4 * i + 2 * p - 2)
            for r in range(2):
                part = slice(HEAD * r, HEAD * (r + 1))
                last = act.activation(q_tile[p][part, :, :].rearrange("p (k r) c -> p k r c", r=2)[:, :, r, :],
                                      qo[part, bass.ds(2 * i + p, 1), :].rearrange("p a (k c) -> p (a k) c", c=P),
                                      ACT.Copy)
            last.then_inc(s_a["q_tile"][p], 1)

        def softmax_act(act, i, p, g):
            par, r = g % 2, 4 * i + 2 * p + g // 2
            act.wait_ge(att["neg_max"][par], att.done("neg_max", r))
            act.wait_ge(sink_dve, done(4 * (2 * i + p) + g))
            if g == 0:
                act.wait_ge(sums_read[p], free(i))
            act.activation(sink_exp[p][:, GQA * g:GQA * (g + 1)], sink_gap[par], ACT.Exp).then_inc(sink_act, 1)
            for m in range(GQA):
                sl = xn[par][:, m * 256:(m + 1) * 256]
                last = act.activation(sl, sl, ACT.Exp, bias=neg_max[par][:, m:m + 1],
                                      accum_out=sums[p][:, GQA * g + m:GQA * g + m + 1])
            last.then_inc(att["probs"][par], 1)

        def turn_probs(pe, i, p, g):
            par, r = g % 2, 4 * i + 2 * p + g // 2
            pe.wait_ge(att["probs"][par], att.done("probs", r))
            before = r - 1 if par == 0 else r
            pe.wait_ge(att["pt_act"][1 - par], att.done("pt_act", before))
            pe.wait_ge(att["pt_dve"][1 - par], att.done("pt_dve", before))
            for k in range(8):
                last = pe.transpose(banks(4)[:, k * P:(k + 1) * P], xn[par][:, k * P:(k + 1) * P], ident[:, :])
            last.then_inc(att["p_turned"][par], 1)

        def probs_copy(eng, i, p, g, mine):
            par, r = g % 2, 4 * i + 2 * p + g // 2
            c = 0 if mine == "pt_act" else 1
            eng.wait_ge(att["p_turned"][par], att.done("p_turned", r))
            eng.wait_ge(att["pv"][par], att.free("pv", r))
            dst, src = pt[par][:, 4 * c:4 * c + 4, :].rearrange("p a b -> p (a b)"), ps[:, 4 + c, :]
            if c == 0:
                eng.activation(dst, src, ACT.Copy).then_inc(att[mine][par], 1)
            else:
                eng.tensor_copy(dst, src).then_inc(att[mine][par], 1)

        def values(pe, i, p, g):
            par, r = g % 2, 4 * i + 2 * p + g // 2
            pe.wait_ge(att["pt_act"][par], att.done("pt_act", r))
            pe.wait_ge(att["pt_dve"][par], att.done("pt_dve", r))
            if g == 0:
                pe.wait_ge(o_out, free(2 * i + p))
            for m in range(GQA):
                h = GQA * g + m
                for b in range(2):
                    last = pe.matmul(banks(6)[:, h * HEAD:(h + 1) * HEAD], pt[par][:, 2 * m + b, :],
                                     V[:, bass.ds(2 * i + p + b, 1), g * HEAD:(g + 1) * HEAD].rearrange("p a b -> p (a b)"),
                                     start=(b == 0), stop=(b == 1))
            last.then_inc(att["pv"][par], 1)

        def att_out(dve, i, p):
            t = 2 * i + p
            dve.wait_ge(att["pv"][1], att.done("pv", 4 * i + 2 * p + 1))
            dve.wait_ge(sink_act, done(4 * t + 3))
            dve.wait_ge(att["probs"][1], att.done("probs", 4 * i + 2 * p + 1))
            dve.wait_ge(o_out, free(t))
            dve.tensor_tensor(recip[:, :], sums[p][:, :], sink_exp[p][:, :], ALU.add).then_inc(sums_read[p], 1)
            dve.wait_ge(sums_read[p], done(i))
            dve.reciprocal(recip[:, :], recip[:, :]).then_inc(recip_done, 1)
            dve.wait_ge(recip_done, t + 1)
            dve.wait_ge(s_a["q_tile"][p], s_a.done("q_tile", i))
            dve.tensor_tensor(qo[:, bass.ds(t, 1), :].rearrange("p a (h d) -> p (a h) d", d=HEAD),
                              banks(6).rearrange("p (h d) -> p h d", d=HEAD),
                              recip[:, :].unsqueeze(2).to_broadcast([P, HEADS, HEAD]), ALU.mult).then_inc(o_out, 1)

        w_o = (A["w_o_hi"], A["w_o_lo"])
        s_o = S["o"]

        def o_pe(pe, i, p):
            pe.wait_ge(s_o["lo"][p], s_o.done("lo", i))
            pe.wait_ge(s_o["scaled"][p], s_o.free("scaled", i))
            for c in range(2):
                for k in range(KD):
                    if isinstance(i, int) and i == 0 and p == 0 and c == 0:
                        pe.wait_ge(w_ready, BASE["o"] + k + 1)
                    last = product(pe, ps[:, 2 + 2 * p + c, :], [x[p][:, k, :] for x in (xt_hi, xt_lo)],
                                   [x[:, k, c * HALF:(c + 1) * HALF] for x in w_o], k == 0, k == KD - 1)
            last.then_inc(s_o["used"][p], 1)

        def o_act(act, i, p):
            act.wait_ge(s_o["used"][p], s_o.done("used", i))
            act.wait_ge(s_o["mean2"][p], s_o.free("mean2", i))
            act.activation(C["o_squares"][:, p, :], banks(2 + 2 * p), ACT.Square, scale=D ** -0.5, accum_out=ssum2[p]).then_inc(s_o["ssum2"][p], 1)

        block = ctx.enter_context(nc.Block())

        @block.sync
        def _(sp):
            sp.dma_start(ident[:, :], I["identity"]).then_inc(consts_loaded, 16)
            sp.dma_start(sinks[:, :], I["sinks"][0].partition_broadcast(P)).then_inc(consts_loaded, 16)
            x_t = I["x"].rearrange("b (t p) d -> p (b t) d", p=P)
            for t in range(2):
                sp.dma_start(H[:, t * D:(t + 1) * D], x_t[:, t, :]).then_inc(x_loaded[t], 16)
            for name in ("band_first", "band_inner", "band_before"):
                sp.dma_start(C[name][:, :, :], I[name]).then_inc(pool_consts_loaded, 16)
            w = I["pool_w"][0].rearrange("g c n -> (g c) n")
            for j in range(2):
                load_unit(sp, BASE["pool"], j, quarter(w, j))
            sp.dma_start(C["scale_row"][:, :], I["pool_scale"][0].partition_broadcast(P)).then_inc(pool_consts_loaded, 16)
            for t in range(2, TILES):
                sp.dma_start(H[:, t * D:(t + 1) * D], x_t[:, t, :]).then_inc(x_loaded[t], 16)

            def ffn_loads(L):
                f, base = F, BASE[f"ffn{L}"]
                gate = I["w_ff_gate"][L].rearrange("(k p) n -> p k n", p=P)
                up = I["w_ff_up"][L].rearrange("(k p) n -> p k n", p=P)

                def group(g):
                    for j, w in enumerate((gate, gate, up, up)):
                        k = 4 * (j % 2)
                        load_unit(sp, base, j, w[:, k:k + 4, bass.ds(g * GROUP, GROUP)], g)
                    for t in range(2):
                        load_unit(sp, base, 4 + t, I["w_ff_down"][L][bass.ds((2 * g + t) * P, P), :], g)

                group(0)
                for p in range(2):
                    sp.wait_ge(S[("pool", "o")[L]]["added"][p], S[("pool", "o")[L]].done("added", PAIRS - 1))
                sp.dma_start(spill[L], H[:, :]).then_inc(f["spilled"], 16)
                with sp.Fori(1, GROUPS) as g:
                    group(g)
                for k in range(SLOTS):
                    load_unit(sp, BASE[f"ple{L}"], k, rows(I["w_ple_gate"][L], k))
                sp.wait_ge(f["spilled"], 16 * (L + 1))
                for j in range(TILES):
                    if j < 2:
                        sp.wait_ge(S[f"ffn{L}"]["lo"][j], S[f"ffn{L}"].done("lo", PAIRS - 1))
                    else:
                        sp.wait_ge(post_added[L], 1 + j - 1)
                    sp.dma_start(back[j % 2][:, :], spill[L][:, j * D:(j + 1) * D]).then_inc(f["back"][j % 2], 16)

            def ple_loads(L):
                base = BASE[f"ple{L}"]
                for k in range(SLOTS, KD):
                    load_unit(sp, base, k, rows(I["w_ple_gate"][L], k))
                for k in range(2):
                    load_unit(sp, base, KD + k, rows(I["w_ple_proj"][L], k))
                sp.wait_ge(F["down"], 1 + 16 * GROUPS * (L + 1))
                over_pairs(sp, lambda i, last: [p_load(sp, L, i, p) for p in range(2)])

            ffn_loads(0)
            ple_loads(0)
            for j in range(4):
                load_unit(sp, BASE["kv"], j, quarter(I["w_k"] if j < 2 else I["w_v"], j % 2))
            for p in range(2):
                sp.wait_ge(S["ple0"]["used"][p], S["ple0"].done("used", PAIRS - 1))
            for name, dst in (("rope_cos", C["cos"][:, :, :]), ("rope_sin", C["sin"][:, :, :])):
                sp.dma_start(dst, I[name]).then_inc(consts_loaded, 16)
            for m in range(2):
                sp.dma_start(mask[m][:, :], I["mask"][:, m, :]).then_inc(consts_loaded, 16)
            for k in range(KD):
                load_unit(sp, BASE["q"], k, rows(I["w_q"][0], k))
            for k in range(KD):
                load_unit(sp, BASE["o"], k, rows(I["w_o"][0], k))
            ffn_loads(1)
            ple_loads(1)
            o_t = out.rearrange("b (t p) d -> p (b t) d", p=P)
            for t in range(TILES):
                sp.wait_ge(ple_added[1], 1 + 2 * (t + 1))
                sp.dma_start(o_t[:, t, :], H[:, t * D:(t + 1) * D]).then_inc(stored, 16)
            sp.wait_ge(stored, 16 * TILES)

        @block.gpsimd
        def _(pool):
            for s in credited:
                pool.sem_inc(s, 1)
            pool.memset(minus_half, -0.5).then_inc(consts_set, 1)
            pool.memset(eps, EPS).then_inc(consts_set, 1)
            pool.wait_ge(consts_set, 2)

            def rms(name):
                return lambda i, p: inv_rms(pool, S[name], i, p, ssum[p], mean[p], rstd[p])

            def rms_post(name):
                return lambda i, p: inv_rms(pool, S[name], i, p, ssum2[p], mean2[p], rstd2[p], ("ssum2", "mean2", "rstd2"))

            def norm_pass(name):
                with pool.Fori(0, PAIRS) as i:
                    for p in range(2):
                        rms(name)(i, p)

            def ffn(L):
                norm_pass(f"ffn{L}")
                f = F
                pool.wait_ge(f["spilled"], 16 * (L + 1))
                for p in range(2):
                    pool.wait_ge(S[f"ffn{L}"]["xn"][p], S[f"ffn{L}"].done("xn", PAIRS - 1))
                pool.memset(H[:, :], 0.0).then_inc(f["cleared"], 1)
                ffn_post_pool(pool, L)

            staggered(pool, (2, rms("pool")), (0, rms_post("pool")))
            ffn(0)
            norm_pass("ple0")
            for p in range(2):
                pool.wait_ge(S["ple0"]["used"][p], S["ple0"].done("used", PAIRS - 1))
            pool.memset(kT[:, 0, :, :], 0.0).then_inc(kv_zeroed, 1)
            pool.memset(V[:, 0, :], 0.0).then_inc(kv_zeroed, 1)
            norm_pass("kv")
            norm_pass("q")

            for p in range(2):
                pool.wait_ge(s_q["used"][p], s_q.done("used", PAIRS - 1))
                pool.memset(q_tile[p][:, :, :], 0.0).then_inc(q_zeroed, 1)

            def o_copy(i, p):
                pool.wait_ge(s_o["turned"][p], s_o.free("turned", i))
                pool.wait_ge(o_out, 1 + TILES)
                pool.tensor_copy(xn[p][:, :], qo[:, bass.ds(2 * i + p, 1), :].rearrange("p a b -> p (a b)")
                                 ).then_inc(s_o["xn"][p], 1)

            staggered(pool, (2, o_copy), (0, rms_post("o")))
            ffn(1)
            norm_pass("ple1")

        @block.scalar
        def _(act):
            def gain_row(name, src):
                row_load(act, gain, src, gain_loaded)

            gain_row("pool", I["mix_pre_g"][0])
            row_load(act, post_gain, I["mix_post_g"][0], post_gain_loaded)
            s = s_pool
            for j in range(2):
                cut_hi(act, BASE["pool"], j, w_pool[0][:, 4 * j:4 * j + 4, :])

            def pool_out(i, p):
                act.wait_ge(s["out_scaled"][p], s.done("out_scaled", i))
                act.wait_ge(s["mean2"][p], s.free("mean2", i))
                act.activation(A["pool_squares"][:, p, :], pool_m[p][:, :], ACT.Square, scale=D ** -0.5, accum_out=ssum2[p]).then_inc(s["ssum2"][p], 1)

            staggered(act, (1, lambda i, p: slot_hi(act, s, i, p)), (2, lambda i, p: pool_square_sum(act, i, p)),
                      (0, pool_out))

            def ffn(L, before):
                name, f, base = f"ffn{L}", F, BASE[f"ffn{L}"]
                s = S[name]
                with act.Fori(0, PAIRS) as i:
                    for p in range(2):
                        square_sum(act, s, i, p, before)
                    for p in range(2):
                        turned_hi(act, s, i, p, xT[0][:, :, bass.ds((2 * i + p) * P, P)])
                gain_row(f"ple{L}", I["ple_norm_g"][L])
                row_load(act, post_gain, I["ffn_post_g"][L], post_gain_loaded)
                for j in range(4):
                    cut_hi(act, base, j, gu_dst(j)[0])
                with act.Fori(0, GROUPS - 1) as g:
                    ffn_act(act, L, g, False)
                ffn_act(act, L, GROUPS - 1, True)
                act.wait_ge(f["up"], 1 + 4 * GROUPS * (L + 1))
                for k in range(4):
                    cut_hi(act, BASE[f"ple{L}"], k, w_pg[L][0][:, k, :])
                ffn_post_act(act, L)
                for k in range(4, KD):
                    cut_hi(act, BASE[f"ple{L}"], k, w_pg[L][0][:, k, :])
                act.wait_ge(f["down"], 1 + 16 * GROUPS * (L + 1))
                for k in range(2):
                    cut_hi(act, BASE[f"ple{L}"], KD + k, w_pp[0][:, k, :])

            def ple(L):
                name = f"ple{L}"
                s = S[name]
                ready = after_count(post_added[L], 1)

                staggered(act, (1, lambda i, p: slot_hi(act, s, i, p)), (1, lambda i, p: p_hi(act, L, i, p)),
                          (2, lambda i, p: square_sum(act, s, i, p, ready)), (0, lambda i, p: ple_act(act, L, i, p)))

            gain_row("ffn0", I["ffn_pre_g"][0])
            ffn(0, after_phase("pool"))
            ple(0)
            gain_row("kv", I["kv_norm_g"])
            for j in range(4):
                cut_hi(act, BASE["kv"], j, kv_dst(j)[0])

            ready = after_count(ple_added[0], 2)

            def q_cut(i, p):
                if isinstance(i, int):
                    for k in (2 * (i // 3 * 2 + p), 2 * (i // 3 * 2 + p) + 1):
                        cut_hi(act, BASE["q"], k, w_q[0][:, k, :])

            staggered(act, (1, lambda i, p: slot_hi(act, s_kv, i, p)), (2, lambda i, p: square_sum(act, s_kv, i, p, ready)),
                      (0, q_cut), (-1, lambda i, p: kv_act(act, i, p)))

            gain_row("q", I["mix_pre_g"][1])
            staggered(act, (1, lambda i, p: slot_hi(act, s_q, i, p)), (2, lambda i, p: square_sum(act, s_q, i, p, ready)),
                      (-1, lambda i, p: q_act(act, i, p)))
            gain_row("ffn1", I["ffn_pre_g"][1])

            act.wait_ge(q_zeroed, 2)
            act.wait_ge(q_copied, 1 + TILES)
            q_to_place(act, 0, 0)
            softmax_act(act, 0, 0, 0)
            softmax_act(act, 0, 0, 1)

            def att_tile(i, p, more, nxt):
                for g in range(KV_HEADS):
                    if g == 0 and more:
                        q_to_place(act, *nxt)
                    probs_copy(act, i, p, g, "pt_act")
                    if g < 2:
                        softmax_act(act, i, p, g + 2)
                    elif more:
                        softmax_act(act, *nxt, g - 2)

            def att_body(i, last):
                att_tile(i, 0, True, (i, 1))
                att_tile(i, 1, not last, (i + 1, 0))

            over_pairs(act, att_body)
            for k in range(KD):
                cut_hi(act, BASE["o"], k, w_o[0][:, k, :])
            row_load(act, post_gain, I["mix_post_g"][1], post_gain_loaded)

            act.wait_ge(o_out, 1 + TILES)
            staggered(act, (1, lambda i, p: slot_hi(act, s_o, i, p)), (0, lambda i, p: o_act(act, i, p)))
            ffn(1, after_phase("o"))
            ple(1)

        @block.vector
        def _(dve):
            s = s_pool
            dve.wait_ge(gain_loaded, 16)
            dve.wait_ge(pool_consts_loaded, 64)
            dve.wait_ge(post_gain_loaded, 16)
            for t in range(TILES):
                dve.wait_ge(x_loaded[t], 16)
            for j in range(2):
                cut_lo(dve, BASE["pool"], j, *[w[:, 4 * j:4 * j + 4, :] for w in w_pool])

            def pool_scale(i, p):
                dve.wait_ge(s["used"][p], s.done("used", i))
                dve.wait_ge(s["ssum2"][p], s.free("ssum2", i))
                dve.tensor_tensor(pool_m[p][:, :], banks(2 + 2 * p), C["scale_row"][:, :], ALU.mult
                                  ).then_inc(s["out_scaled"][p], 1)

            staggered(dve, (1, lambda i, p: slot_lo(dve, s, i, p)), (-1, lambda i, p: add_post(dve, s, i, p, pool_m[p][:, :])),
                      (2, lambda i, p: normed(dve, s, i, p)), (0, pool_scale))

            def ffn(L):
                name, f, base = f"ffn{L}", F, BASE[f"ffn{L}"]
                s = S[name]
                dve.wait_ge(gain_loaded, 16 * GAIN[name])
                with dve.Fori(0, PAIRS) as i:
                    for p in range(2):
                        normed(dve, s, i, p)
                    for p in range(2):
                        c = bass.ds((2 * i + p) * P, P)
                        turned_lo(dve, s, i, p, xT[0][:, :, c], xT[1][:, :, c])
                for j in range(4):
                    cut_lo(dve, base, j, *gu_dst(j))
                dve.wait_ge(f["cleared"], L + 1)
                with dve.Fori(0, GROUPS - 1) as g:
                    ffn_dve(dve, L, g, False)

                def between(n):
                    if n in (1, 3, 5, 7):
                        k = n // 2
                        cut_lo(dve, BASE[f"ple{L}"], k, *[w[:, k, :] for w in w_pg[L]])
                    if n >= 5 and n % 2:
                        ffn_post_dve(dve, L, (n - 5) // 2)

                ffn_dve(dve, L, GROUPS - 1, True, between)
                for j in range(TILES - 2, TILES):
                    ffn_post_dve(dve, L, j)
                for k in range(4, KD):
                    cut_lo(dve, BASE[f"ple{L}"], k, *[w[:, k, :] for w in w_pg[L]])
                for k in range(2):
                    cut_lo(dve, BASE[f"ple{L}"], KD + k, *[w[:, k, :] for w in w_pp])

            def ple(L):
                name = f"ple{L}"
                s = S[name]
                dve.wait_ge(gain_loaded, 16 * GAIN[name])

                staggered(dve, (1, lambda i, p: slot_lo(dve, s, i, p)), (1, lambda i, p: p_lo(dve, L, i, p)),
                          (2, lambda i, p: normed(dve, s, i, p)), (0, lambda i, p: ple_dve(dve, L, i, p)))

            ffn(0)
            ple(0)
            for j in range(4):
                cut_lo(dve, BASE["kv"], j, *kv_dst(j))

            dve.wait_ge(gain_loaded, 16 * GAIN["kv"])
            dve.wait_ge(consts_loaded, 16 * 6)
            dve.wait_ge(kv_zeroed, 2)

            def q_cut(i, p):
                if isinstance(i, int):
                    for k in (2 * (i // 3 * 2 + p), 2 * (i // 3 * 2 + p) + 1):
                        cut_lo(dve, BASE["q"], k, *[w[:, k, :] for w in w_q])

            staggered(dve, (1, lambda i, p: slot_lo(dve, s_kv, i, p)), (2, lambda i, p: normed(dve, s_kv, i, p)),
                      (0, q_cut), (0, lambda i, p: kv_dve(dve, i, p)))

            dve.wait_ge(gain_loaded, 16 * GAIN["q"])
            staggered(dve, (1, lambda i, p: slot_lo(dve, s_q, i, p)), (2, lambda i, p: normed(dve, s_q, i, p)),
                      (0, lambda i, p: q_dve(dve, i, p)))

            def att_tile(i, p, more, nxt):
                for g in range(KV_HEADS):
                    probs_copy(dve, i, p, g, "pt_dve")
                    if g < 2:
                        softmax_dve(dve, i, p, g + 2)
                    elif more:
                        softmax_dve(dve, *nxt, g - 2)
                att_out(dve, i, p)

            softmax_dve(dve, 0, 0, 0)
            softmax_dve(dve, 0, 0, 1)

            def att_body(i, last):
                att_tile(i, 0, True, (i, 1))
                att_tile(i, 1, not last, (i + 1, 0))

            over_pairs(dve, att_body)
            for k in range(KD):
                cut_lo(dve, BASE["o"], k, *[w[:, k, :] for w in w_o])

            dve.wait_ge(post_gain_loaded, 16 * POSTG["o"])
            staggered(dve, (1, lambda i, p: slot_lo(dve, s_o, i, p)),
                      (0, lambda i, p: add_post(dve, s_o, i, p, banks(2 + 2 * p))))
            ffn(1)
            ple(1)

        @block.tensor
        def _(pe):
            pe.wait_ge(consts_loaded, 32)
            pe.wait_ge(pool_consts_loaded, 64)

            def pool_products(i, p):
                s = s_pool
                pe.wait_ge(s["lo"][p], s.done("lo", i))
                pe.wait_ge(s["out_scaled"][p], s.free("out_scaled", i))
                pe.wait_ge(w_ready, BASE["pool"] + 2)
                for g in range(len(WINDOWS)):
                    for k in range(2):
                        last = product(pe, banks(2 + 2 * p)[:, g * GROUP:(g + 1) * GROUP],
                                       [x[p][:, 2 * g + k, :] for x in (xt_hi, xt_lo)],
                                       [x[:, 2 * g + k, :] for x in w_pool], k == 0, k == 1)
                last.then_inc(s["used"][p], 1)

            staggered(pe, (1, lambda i, p: pool_band(pe, i, p)), (0, pool_products))

            def ffn(L):
                s = S[f"ffn{L}"]
                with pe.Fori(0, PAIRS) as i:
                    for p in range(2):
                        turn(pe, s, i, p)
                for p in range(2):
                    pe.wait_ge(s["lo"][p], s.done("lo", PAIRS - 1))
                with pe.Fori(0, GROUPS) as g:
                    ffn_pe(pe, L, g)

            def turned(s):
                return lambda i, p: turn(pe, s, i, p)

            ffn(0)
            staggered(pe, (1, turned(S["ple0"])), (0, lambda i, p: ple_pe(pe, 0, i, p)))
            pe.wait_ge(w_ready, BASE["kv"] + 4)
            staggered(pe, (1, turned(s_kv)), (0, lambda i, p: kv_pe(pe, i, p)), (-1, lambda i, p: kv_turn(pe, i, p)))
            staggered(pe, (1, turned(s_q)), (0, lambda i, p: q_pe(pe, i, p, [0])), (-1, lambda i, p: q_turn(pe, i, p)),
                      (0, lambda i, p: q_pe(pe, i, p, [1])))

            for p in range(2):
                pe.wait_ge(k_copied[p], done(PAIRS - 1))
            pe.wait_ge(v_copied, TILES)
            pe.wait_ge(q_copied, 1 + TILES)
            scores(pe, 0, 0, 0)
            scores(pe, 0, 0, 1)

            def att_tile(i, p, more, nxt):
                for g in range(KV_HEADS):
                    turn_probs(pe, i, p, g)
                    if g < 2:
                        scores(pe, i, p, g + 2)
                    elif more:
                        scores(pe, *nxt, g - 2)
                    values(pe, i, p, g)

            def att_body(i, last):
                att_tile(i, 0, True, (i, 1))
                att_tile(i, 1, not last, (i + 1, 0))

            over_pairs(pe, att_body)

            pe.wait_ge(o_out, 1 + TILES)
            staggered(pe, (1, turned(s_o)), (0, lambda i, p: o_pe(pe, i, p)))
            ffn(1)
            staggered(pe, (1, turned(S["ple1"])), (0, lambda i, p: ple_pe(pe, 1, i, p)))


_INS = ["x", "mix_pre_g", "mix_post_g", "ffn_pre_g", "ffn_post_g", "pool_w", "pool_scale", "kv_norm_g", "w_k", "w_v",
        "w_q", "w_o", "sinks", "w_ff_gate", "w_ff_up", "w_ff_down", "ple_norm_g", "w_ple_gate", "w_ple_proj"]


def kernel(**inputs):
    import numpy as _np
    import concourse.bacc as _bacc
    from concourse import mybir as _mybir
    from concourse.bass_utils import run_bass_kernel_spmd as _run

    nc = _bacc.Bacc("TRN2", target_bir_lowering=False, num_devices=1, dynamic_dma_scratch_size=1024)
    arrays = {name: _np.ascontiguousarray(inputs[name]) for name in _INS}
    p = inputs["p"]
    arrays["pT"] = _np.ascontiguousarray(_np.asarray(p).reshape(p.shape[0], SEQ, PLE).transpose(0, 2, 1))
    arrays.update(constants())
    I = {}
    for name, a in arrays.items():
        I[name] = nc.dram_tensor(f"in_{name}", a.shape, _mybir.dt.from_np(a.dtype), kind="ExternalInput").ap()
    out = nc.dram_tensor("out_0", (1, SEQ, D), F32, kind="ExternalOutput").ap()
    trunk(nc, I, out)
    r = _run(nc, [{f"in_{k}": v for k, v in arrays.items()}], core_ids=[0])
    return r.results[0]["out_0"]
```

```python
from contextlib import ExitStack

import numpy as np
import concourse.bass as bass
from concourse import mybir

P = 128
F32 = mybir.dt.float32
F32R = mybir.dt.float32r
BF16 = mybir.dt.bfloat16
ALU = mybir.AluOpType
ACT = mybir.ActivationFunctionType
AX = mybir.AxisListType

D = 1024
SEQ = 1024
TILES = SEQ // P
PAIRS = TILES // 2
KD = D // P
HALF = 512
HEAD = 64
HEADS = D // HEAD
KV_HEADS = 4
GQA = HEADS // KV_HEADS
WINDOWS = (2, 4, 8, 16)
LONGEST = max(WINDOWS)
D_FF = 2816
GROUP = 256
GROUPS = D_FF // GROUP
PLE = 256
EPS = 1e-6
NEG = -2.0 ** 103
SLOTS = 6
STEPS = [(0, 0), (1, 0), (0, 1), (1, 1)]


def constants():
    s, t = np.arange(P)[:, None], np.arange(P)[None, :]
    first, inner, before = [], [], []
    for w in WINDOWS:
        near = (t >= s) & (t - s < w)
        first.append(near / np.minimum(t + 1, w).astype(np.float32) - (s == t))
        inner.append(near / np.float32(w) - (s == t))
        before.append(((t + P - s < w) / np.float32(w))[:, :LONGEST])
    inv = (1.0 / (10000.0 ** (np.arange(0, HEAD, 2, dtype=np.float32) / np.float32(HEAD)))).astype(np.float32)
    angle = np.arange(SEQ, dtype=np.float32)[:, None] * inv[None, :]
    angle = angle.reshape(TILES, P, HEAD // 2).transpose(1, 0, 2)
    q, k = np.arange(P)[:, None], np.arange(-P, P)[None, :]
    valid = (q - k >= 0) & (q - k < P)
    mask = np.stack([np.where(valid & (k >= 0), 0.0, NEG), np.where(valid, 0.0, NEG)], axis=1)
    out = {
        "identity": np.eye(P),
        "band_first": np.stack(first, 1), "band_inner": np.stack(inner, 1), "band_before": np.stack(before, 1),
        "rope_cos": np.cos(angle), "rope_sin": np.sin(angle),
        "mask_unit": np.concatenate([mask[:, 0], mask[:, 1], np.eye(P), np.zeros((P, D - 5 * P))], axis=1),
    }
    return {k: np.ascontiguousarray(v, dtype=np.float32) for k, v in out.items()}


def done(i):
    return i + 2


def free(i):
    return i + 1


def trunk(nc, I, out):
    ctx = ExitStack()
    with ctx:
        credited = []

        def sem(name):
            return ctx.enter_context(nc.semaphore(name))

        def sem_c(name):
            s = sem(name)
            credited.append(s)
            return s

        families, rounds = {}, {}

        class Phase:

            def __init__(self, *events, count=PAIRS):
                self.base = {}
                for e in events:
                    if e not in families:
                        families[e], rounds[e] = [sem_c(f"{e}{p}") for p in range(2)], 0
                    self.base[e] = rounds[e]
                    rounds[e] += count

            def __getitem__(self, e):
                return families[e]

            def done(self, e, i):
                return done(self.base[e] + i)

            def free(self, e, i):
                return free(self.base[e] + i)

        def sb(name, shape, dt=F32):
            return ctx.enter_context(nc.sbuf_tensor(name, shape, dt))

        def region(name, elements, *uses):
            views = {}
            for use in uses:
                with ExitStack() as inner:
                    for n, shape, dt in use:
                        views[n] = inner.enter_context(nc.sbuf_tensor(n, shape, dt))
            sb(name, [P, elements])
            return views

        H = sb("H", [P, TILES * D])
        raw = [sb(f"raw{i}", [P, D]) for i in range(SLOTS)]
        xn = [sb(f"xn{p}", [P, D]) for p in range(2)]
        tmp = sb("tmp", [P, D])
        gain = sb("gain", [P, D])
        ident = sb("ident", [P, P])
        small = sb("small", [P, 64])
        sinks = sb("sinks_row", [P, HEADS])

        def weights(name, shape):
            return [(name + "_hi", shape, F32R), (name + "_lo", shape, F32R)]

        def ffn_weights(L):
            return (weights(f"wg{L}", [P, KD, GROUP]) + weights(f"wu{L}", [P, KD, GROUP])
                    + weights(f"wd{L}", [P, 2, D]) + weights(f"ffn_a{L}", [P, 2, SEQ]))

        def embed_weights(L):
            return (weights(f"w_ple_proj{L}", [P, 2, D]) + weights(f"pT0_{L}", [P, 2, P]) + weights(f"pT1_{L}", [P, 2, P])
                    + [(f"p_raw0_{L}", [P, 2, P], F32), (f"p_raw1_{L}", [P, 2, P], F32)])

        def pad(name, elements):
            return [(name, [P, elements], F32)]

        A = region("A", 16 * D,
                   weights("xT0", [P, TILES, KD, P]), weights("w_ple_gate0", [P, KD, D]),
                   weights("w_q", [P, KD, D]), weights("w_o", [P, KD, D]),
                   ffn_weights(1), embed_weights(1))
        B = region("B", 16 * D,
                   ffn_weights(0), embed_weights(0),
                   pad("below_junk", 6 * D) + [("squares", [P, 2, D], F32)] + weights("w_pool", [P, KD, GROUP])
                   + [("band_first", [P, 4, P], F32), ("band_inner", [P, 4, P], F32),
                      ("band_before", [P, 4, LONGEST], F32), ("scale_row", [P, D], F32), ("pool_gain", [P, D], F32)],
                   pad("below_w_kv", 8 * D) + weights("w_kv", [P, KD, 2 * GROUP]),
                   [("kT", [P, TILES + 1, KV_HEADS, P], F32), ("V", [P, TILES + 1, GROUP], F32),
                    ("mask_r", [P, 2, 2 * P], F32R), ("ident_r", [P, P], F32R),
                    ("cos", [P, TILES, 32], F32), ("sin", [P, TILES, 32], F32)],
                   pad("below_qo", 8 * D) + [("qo", [P, TILES, D], F32)],
                   [("xT1_lo", [P, TILES, KD, P], F32R), ("xT1_hi", [P, TILES, KD, P], F32R)],
                   weights("w_ple_gate1", [P, KD, D]))
        DD = region("DD", 4 * D,
                    weights("xt0", [P, KD, P]) + weights("xt1", [P, KD, P]),
                    [("sig", [P, 2, HALF], F32), ("act0", [P, HALF], F32),
                     ("act1", [P, HALF], F32), ("back0", [P, D], F32), ("back1", [P, D], F32)],
                    [("q_tile0", [P, HEADS, P], F32), ("q_tile1", [P, HEADS, P], F32)])
        E = region("E", D,
                   [("post_gain", [P, D], F32)], [("ple_sig", [P, 2, HALF], F32)],
                   [("k_rot", [P, KV_HEADS, 2, HEAD], F32), ("rope_a", [P, 256], F32), ("rope_b", [P, 256], F32)],
                   [("pt1", [P, KD, P], F32)])
        xt_hi, xt_lo = [DD["xt0_hi"], DD["xt1_hi"]], [DD["xt0_lo"], DD["xt1_lo"]]
        post_gain = E["post_gain"]
        kT, V = B["kT"], B["V"]
        qo = B["qo"]

        ssum, mean, rstd = [[small[:, 2 * n + p:2 * n + p + 1] for p in range(2)] for n in range(3)]
        ssum2, mean2, rstd2 = [[small[:, 6 + 2 * n + p:7 + 2 * n + p] for p in range(2)] for n in range(3)]
        minus_half, eps = small[:, 12:13], small[:, 13:14]
        neg_row_max = [small[:, 16 + 4 * p:20 + 4 * p] for p in range(2)]
        neg_sinks = small[:, 44:60]
        neg_max = [small[:, 24 + 4 * p:28 + 4 * p] for p in range(2)]
        sink_gap = [small[:, 32 + 4 * p:36 + 4 * p] for p in range(2)]
        sums = [sb(f"sums{p}", [P, HEADS]) for p in range(2)]
        sink_exp = [sb(f"sink_exp{p}", [P, HEADS]) for p in range(2)]
        recip = sb("recip", [P, HEADS])

        ps = ctx.enter_context(nc.psum_tensor("ps", [P, 8, HALF], F32))

        def banks(b, n=2):
            return ps[:, b:b + n, :].rearrange("p b c -> p (b c)")

        spill = nc.dram_tensor("residual_spill", (2, P, TILES * D), F32, kind="Internal").ap()

        units = []

        def rows(w, k):
            return w[k * P:(k + 1) * P, :]

        def quarter(w, j):
            return w.rearrange("(k p) n -> p k n", p=P)[:, 4 * j:4 * j + 4, :]

        BASE, n = {}, 0
        for name, count in (("pool", 2), ("ffn0", 6 * GROUPS), ("ple0", 10), ("kv", 4), ("mask", 1), ("q", 8), ("o", 8),
                            ("ffn1", 6 * GROUPS), ("ple1", 10)):
            BASE[name] = n
            n += count
        raw_loaded = [sem(f"raw_loaded{i}") for i in range(SLOTS)]
        hi_done = sem("weight_hi_done")
        w_ready = sem("weights_ready")

        def loaded(base, j, g=0):
            return raw_loaded[(base + j) % SLOTS], 16 * ((base + j) // SLOTS + 1 + g)

        def shape_of(dst, src):
            free_dims = dst.shape[1:]
            if len(free_dims) == 1:
                return src[:, :]
            return src[:, :].rearrange("p (k n) -> p k n", k=free_dims[0])

        def load_unit(sp, base, j, src, g=0):
            if not isinstance(g, int) or base + j + 6 * g >= SLOTS:
                sp.wait_ge(w_ready, base + j + 6 * g - SLOTS + 1)
            slot = raw[(base + j) % SLOTS]
            sp.dma_start(shape_of(src, slot), src).then_inc(loaded(base, j)[0], 16)

        def cut_hi(act, base, j, dst, g=0, columns=slice(0, D)):
            s, value = loaded(base, j, g)
            act.wait_ge(s, value)
            act.activation(dst, shape_of(dst, raw[(base + j) % SLOTS][:, columns]), ACT.Copy).then_inc(hi_done, 1)

        def cut_lo(dve, base, j, dst_hi, dst_lo, g=0):
            dve.wait_ge(hi_done, base + j + 6 * g + 1)
            dve.tensor_tensor(dst_lo, shape_of(dst_lo, raw[(base + j) % SLOTS]), dst_hi.bitcast(F32),
                              ALU.subtract).then_inc(w_ready, 1)

        def product(pe, out_, lhs, rhs, first, last):
            pe.matmul(out_, lhs[0], rhs[0], start=first, stop=False)
            pe.matmul(out_, lhs[0], rhs[1], start=False, stop=False)
            return pe.matmul(out_, lhs[1], rhs[0], start=False, stop=last)

        consts_loaded = sem("consts_loaded")
        first_consts_loaded = sem("first_consts_loaded")
        pool_consts_loaded = sem("pool_consts_loaded")
        w_pool_scaled = sem("w_pool_scaled")
        x_loaded = [sem(f"x_loaded{t}") for t in range(TILES)]
        x_arrived = sem_c("x_arrived")
        gain_loaded = sem("gain_loaded")
        post_gain_loaded = sem("post_gain_loaded")
        consts_set = sem("consts_set")
        TURN = ("xn", "turned", "hi", "lo")
        MEAN = ("ssum", "mean", "rstd")
        POST = ("ssum2", "mean2", "rstd2", "scaled", "added")
        EMBED = ("p_hi", "p_lo")
        S = {}
        S["pool"] = Phase(*TURN, *MEAN, "used", *POST)
        S["ple0"] = Phase(*TURN, *MEAN, "used", *EMBED)
        S["kv"] = Phase(*TURN, *MEAN, "used", "rotated", "k_turned")
        S["q"] = Phase(*TURN, *MEAN, "used")
        S["att"] = Phase("q_tile")
        S["o"] = Phase(*TURN, "used", *POST)
        S["ple1"] = Phase(*TURN, *MEAN, "used", *EMBED)
        att = Phase("scores", "max", "neg_max", "probs", "p_turned", "pt", "pv", count=TILES * 2)
        p_loaded = [[sem(f"p_loaded{L}{p}") for p in range(2)] for L in range(2)]
        stored = sem("stored")

        def tile(i, p):
            return bass.ds((2 * i + p) * D, D)

        def square_sum(act, s, i, p, ready=None):
            act.wait_ge(s["turned"][p], s.free("turned", i))
            if ready:
                ready(act, i, p)
            act.activation(xn[p][:, :], H[:, tile(i, p)], ACT.Square, scale=D ** -0.5, accum_out=ssum[p]).then_inc(s["ssum"][p], 1)

        def inv_rms(pool, s, i, p, sums_, mean_, rstd_, names=("ssum", "mean", "rstd")):
            pool.wait_ge(s[names[0]][p], s.done(names[0], i))
            pool.tensor_tensor(mean_, sums_, eps, ALU.add).then_inc(s[names[1]][p], 1)
            pool.wait_ge(s[names[1]][p], s.done(names[1], i))
            pool.tensor_tensor(rstd_, mean_, minus_half, ALU.pow).then_inc(s[names[2]][p], 1)

        def normed(dve, s, i, p, row=gain):
            dve.wait_ge(s["rstd"][p], s.done("rstd", i))
            dve.scalar_tensor_tensor(out=xn[p][:, :], in0=H[:, tile(i, p)], scalar=rstd[p], in1=row[:, :],
                                     op0=ALU.mult, op1=ALU.mult).then_inc(s["xn"][p], 1)

        def t_banks_read(pe, s, i, p):
            pe.wait_ge(s["lo"][1 - p], s.done("lo", i) if p else s.free("lo", i))

        def turn(pe, s, i, p):
            pe.wait_ge(s["xn"][p], s.done("xn", i))
            t_banks_read(pe, s, i, p)
            for k in range(KD):
                last = pe.transpose(banks(0)[:, k * P:(k + 1) * P], xn[p][:, k * P:(k + 1) * P], ident[:, :])
            last.then_inc(s["turned"][p], 1)

        def turned_hi(act, s, i, p, dst):
            act.wait_ge(s["turned"][p], s.done("turned", i))
            if "used" in s.base:
                act.wait_ge(s["used"][p], s.free("used", i))
            act.activation(dst, banks(0).rearrange("p (k c) -> p k c", k=KD), ACT.Copy).then_inc(s["hi"][p], 1)

        def turned_lo(dve, s, i, p, hi, lo):
            dve.wait_ge(s["hi"][p], s.done("hi", i))
            dve.tensor_tensor(lo, banks(0).rearrange("p (k c) -> p k c", k=KD), hi.bitcast(F32),
                              ALU.subtract).then_inc(s["lo"][p], 1)

        def slot_hi(act, s, i, p):
            turned_hi(act, s, i, p, xt_hi[p][:, :, :])

        def slot_lo(dve, s, i, p):
            turned_lo(dve, s, i, p, xt_hi[p][:, :, :], xt_lo[p][:, :, :])

        def staggered(eng, parts, before=(), after=(), head=True, tail=True):
            def run(parts, i, p, which=lambda d: True):
                for d, work in parts:
                    n = p + d
                    if which(d) and (not isinstance(i, int) or 0 <= 2 * i + n < TILES):
                        work(i + n // 2 if n // 2 else i, n % 2)

            if head:
                for t in range(-2, 0):
                    run(parts, t // 2, t % 2)
            for p in range(2):
                run(parts, 0, p)
                if p == 0:
                    run(before, PAIRS, 0)
            with eng.Fori(1, PAIRS - 1) as i:
                for p in range(2):
                    run(parts, i, p)
            for p in range(2):
                run(parts, PAIRS - 1, p, lambda d: d > 0)
                run(after, -1, p)
                run(parts, PAIRS - 1, p, lambda d: d <= 0)
            if tail:
                run(parts, PAIRS, 0)

        def at_last(work):
            return lambda i, p: work(i, p) if isinstance(i, int) and i == PAIRS - 1 and p == 1 else None

        def at_first(work):
            return lambda i, p: work(i, p) if isinstance(i, int) and i == 0 and p == 0 else None

        def over_pairs(eng, body):
            body(0, False)
            with eng.Fori(1, PAIRS - 1) as i:
                body(i, False)
            body(PAIRS - 1, True)

        def add_post(dve, s, i, p):
            src = banks(2 + 2 * p)
            dve.wait_ge(s["rstd2"][p], s.done("rstd2", i))
            dve.scalar_tensor_tensor(out=src, in0=src, scalar=rstd2[p], in1=post_gain[:, :],
                                     op0=ALU.mult, op1=ALU.mult).then_inc(s["scaled"][p], 1)
            dve.wait_ge(s["scaled"][p], s.done("scaled", i))
            dve.tensor_tensor(H[:, tile(i, p)], H[:, tile(i, p)], src, ALU.add).then_inc(s["added"][p], 1)

        FN = {e: sem_c(f"ffn_norm_{e}") for e in ("ssum", "mean", "rstd", "xn", "turned", "hi", "lo")}
        ssum_f, mean_f, rstd_f = [small[:, 40 + n:41 + n] for n in range(3)]

        def squares(L, p):
            return xT[L][1][:, TILES - 2 + p, :, :].rearrange("p k c -> p (k c)")

        def fn_squares(act, L, i, p):
            n, s = TILES * L + 2 * i + p, S[("pool", "o")[L]]
            act.wait_ge(FN["mean"], free(n))
            act.wait_ge(s["added"][p], s.done("added", i))
            act.activation(squares(L, p), H[:, tile(i, p)], ACT.Square, scale=D ** -0.5, accum_out=ssum_f).then_inc(FN["ssum"], 1)

        def fn_rms(pool, L, i, p):
            n = TILES * L + 2 * i + p
            pool.wait_ge(FN["ssum"], done(n))
            pool.tensor_tensor(mean_f, ssum_f, eps, ALU.add).then_inc(FN["mean"], 1)
            pool.wait_ge(FN["mean"], done(n))
            pool.tensor_tensor(rstd_f, mean_f, minus_half, ALU.pow).then_inc(FN["rstd"], 1)

        def fn_normed(dve, L, i, p):
            n = TILES * L + 2 * i + p
            dve.wait_ge(FN["rstd"], done(n))
            dve.wait_ge(FN["turned"], free(n))
            dve.scalar_tensor_tensor(out=tmp[:, :], in0=H[:, tile(i, p)], scalar=rstd_f, in1=gain[:, :],
                                     op0=ALU.mult, op1=ALU.mult).then_inc(FN["xn"], 1)

        def fn_turn(pe, L, i, p):
            n = TILES * L + 2 * i + p
            pe.wait_ge(FN["xn"], done(n))
            pe.wait_ge(FN["lo"], free(n))
            for k in range(KD):
                last = pe.transpose(banks(6)[:, k * P:(k + 1) * P], tmp[:, k * P:(k + 1) * P], ident[:, :])
            last.then_inc(FN["turned"], 1)

        def fn_hi(act, L, i, p):
            act.wait_ge(FN["turned"], done(TILES * L + 2 * i + p))
            act.activation(xT[L][0][:, bass.ds(2 * i + p, 1), :, :].rearrange("p a k c -> p (a k c)"), banks(6),
                           ACT.Copy).then_inc(FN["hi"], 1)

        def fn_lo(dve, L, i, p):
            hi, lo = [x[:, bass.ds(2 * i + p, 1), :, :].rearrange("p a k c -> p (a k c)") for x in xT[L]]
            dve.wait_ge(FN["hi"], done(TILES * L + 2 * i + p))
            dve.tensor_tensor(lo, banks(6), hi.bitcast(F32), ALU.subtract).then_inc(FN["lo"], 1)

        def output_squares(act, s, i, p):
            act.wait_ge(s["used"][p], s.done("used", i))
            act.wait_ge(s["mean2"][p], s.free("mean2", i))
            act.activation(squares(int(s is not S["pool"]), p), banks(2 + 2 * p), ACT.Square, scale=D ** -0.5,
                           accum_out=ssum2[p]).then_inc(s["ssum2"][p], 1)

        ple_added = [sem_c(f"ple{n}_added") for n in range(2)]
        post_added = [sem_c(f"ffn{n}_post_added") for n in range(2)]

        def row_load(eng, dst, src, s):
            eng.dma_start(dst[:, :], src.partition_broadcast(P)).then_inc(s, 16)

        GAIN = {"ffn0": 1, "ple0": 2, "kv": 3, "q": 4, "ffn1": 5, "ple1": 6}
        POSTG = {"pool": 1, "ffn0": 2, "o": 3, "ffn1": 4}

        w_pool = (B["w_pool_hi"], B["w_pool_lo"])
        s_pool = S["pool"]

        def pool_band(pe, i, p):
            s = s_pool
            first = isinstance(i, int) and i == 0 and p == 0
            if isinstance(i, int) and i == 0 and p == 1:
                pe.wait_ge(pool_consts_loaded, 48)
            pe.wait_ge(s["xn"][p], s.done("xn", i))
            t_banks_read(pe, s, i, p)
            for c in range(KD):
                w = c // 2
                band = B["band_first"] if first else B["band_inner"]
                o = banks(0)[:, c * P:(c + 1) * P]
                last = pe.matmul(o, xn[p][:, c * P:(c + 1) * P], band[:, w, :], start=True, stop=first)
                if not first:
                    last = pe.matmul(o[:, 0:LONGEST], xn[1 - p][:, c * P:(c + 1) * P], B["band_before"][:, w, :],
                                     start=False, stop=True)
            last.then_inc(s["turned"][p], 1)

        def pool_square_sum(act, i, p):
            s = s_pool
            if isinstance(i, int):
                act.wait_ge(x_arrived, done(2 * i + p))
            else:
                act.wait_ge(x_arrived, 2 + 2 * i + p)
            act.wait_ge(s["mean"][p], s.free("mean", i))
            act.activation(B["squares"][:, p, :], H[:, tile(i, p)], ACT.Square, scale=D ** -0.5, accum_out=ssum[p]
                           ).then_inc(s["ssum"][p], 1)

        def pool_normed(dve, i, p):
            s = s_pool
            if p == 0:
                dve.wait_ge(s["turned"][1], s.free("turned", i))
            else:
                dve.wait_ge(s["turned"][0], s.done("turned", i))
            normed(dve, s, i, p, B["pool_gain"])

        xT = [(A["xT0_hi"], A["xT0_lo"]), (B["xT1_hi"], B["xT1_lo"])]
        FW = [{n: (X[f"{n}{L}_hi"], X[f"{n}{L}_lo"]) for n in ("wg", "wu", "wd", "ffn_a")} for L, X in enumerate((B, A))]
        sig, act32 = DD["sig"], [DD["act0"], DD["act1"]]
        back = [xn[0], xn[1], DD["back0"], DD["back1"], tmp, DD["back0"], DD["back1"], tmp]
        F = {
            "gate": sem_c("ffn_gate_ready"), "up": sem_c("ffn_up_ready"),
            "sig": sem_c("ffn_sigmoid_done"), "prod": sem_c("ffn_silu_done"),
            "act": [sem_c(f"ffn_act_done{p}") for p in range(2)],
            "a_hi": sem_c("ffn_a_hi_done"), "a_lo": sem_c("ffn_a_ready"),
            "down": sem_c("ffn_down_ready"), "summed": [sem_c(f"ffn_summed{b}") for b in range(4)],
            "spilled": sem("ffn_spilled"), "back": [sem(f"ffn_back_loaded{j}") for j in range(TILES)],
            "ssum2": sem("ffn_out_ssum"), "mean2": sem("ffn_out_mean"), "rstd2": sem("ffn_out_rstd"),
            "scaled": sem("ffn_out_scaled"),
        }

        def gu_dst(L, j):
            w = FW[L]["wg" if j < 2 else "wu"]
            k = 4 * (j % 2)
            return w[0][:, k:k + 4, :], w[1][:, k:k + 4, :]

        def ffn_pe(pe, L, g, first_group=False, during_down=None):
            f, base, r = F, BASE[f"ffn{L}"], GROUPS * L + g
            wg, wu, wd, a = [FW[L][x] for x in ("wg", "wu", "wd", "ffn_a")]
            for n, (t, h) in enumerate(STEPS):
                b = 2 * (n % 2)
                if first_group:
                    if n == 0:
                        pe.wait_ge(FN["lo"], done(TILES * L + TILES // 2 - 1))
                    if n == 1:
                        fn_turn(pe, L, PAIRS - 1, 0)
                    if n == 2:
                        pe.wait_ge(FN["lo"], done(TILES * L + TILES - 1))
                pe.wait_ge(f["act"][n % 2], free(2 * r + n // 2))
                for m, (w, ready) in enumerate(((wg, "gate"), (wu, "up"))):
                    if first_group and n == 1 and m == 1:
                        fn_turn(pe, L, PAIRS - 1, 1)
                    for k in range(KD):
                        if n == 0 and k % 4 == 0:
                            pe.wait_ge(w_ready, base + 6 * g + 2 * m + k // 4 + 1)
                        last = product(pe, ps[:, b + m, :],
                                       [x[:, k, t * P:(t + 1) * P] for x in w],
                                       [x[:, 4 * h:4 * h + 4, k, :] for x in xT[L]], k == 0, k == KD - 1)
                    last.then_inc(f[ready], 1)
            for n in range(2 * TILES):
                j, c = n // 2, n % 2
                if n == 0:
                    pe.wait_ge(w_ready, base + 6 * g + 6)
                    pe.wait_ge(f["a_lo"], 1 + 4 * r + 2)
                if n == TILES:
                    pe.wait_ge(f["a_lo"], 1 + 4 * r + 4)
                pe.wait_ge(f["summed"][n % 4], free(4 * r + n // 4))
                for t in range(2):
                    last = product(pe, ps[:, 4 + n % 4, :], [x[:, t, j * P:(j + 1) * P] for x in a],
                                   [x[:, t, c * HALF:(c + 1) * HALF] for x in wd], t == 0, t == 1)
                last.then_inc(f["down"], 1)
                if during_down:
                    during_down(n)

        def ffn_act(act, L, g, last_group, first_group=False):
            f, base, r = F, BASE[f"ffn{L}"], GROUPS * L + g
            wd, a = FW[L]["wd"], FW[L]["ffn_a"]
            if not first_group:
                act.wait_ge(f["down"], 1 + 16 * r)
            for t in range(2):
                cut_hi(act, base, 4 + t, wd[0][:, t, :], g)
            for n, (t, h) in enumerate(STEPS):
                act.wait_ge(f["gate"], 1 + 4 * r + n + 1)
                act.wait_ge(f["act"][n % 2], free(2 * r + n // 2))
                act.activation(sig[:, n % 2, :], ps[:, 2 * (n % 2), :], ACT.Sigmoid).then_inc(f["sig"], 1)
                if first_group and n == 1:
                    fn_hi(act, L, PAIRS - 1, 1)
                act.wait_ge(f["act"][n % 2], done(2 * r + n // 2))
                act.activation(a[0][:, t, h * HALF:(h + 1) * HALF], act32[n % 2][:, :], ACT.Copy).then_inc(f["a_hi"], 1)
            if not last_group:
                act.wait_ge(f["up"], 1 + 4 * r + 4)
                for j in range(4):
                    cut_hi(act, base, j, gu_dst(L, j)[0], g + 1)

        def ffn_dve(dve, L, g, last_group, between=None, first_group=False):
            f, base, r = F, BASE[f"ffn{L}"], GROUPS * L + g
            wd, a = FW[L]["wd"], FW[L]["ffn_a"]
            for t in range(2):
                cut_lo(dve, base, 4 + t, wd[0][:, t, :], wd[1][:, t, :], g)
            for n, (t, h) in enumerate(STEPS):
                dve.wait_ge(f["sig"], 1 + 4 * r + n + 1)
                dve.tensor_tensor(sig[:, n % 2, :], ps[:, 2 * (n % 2), :], sig[:, n % 2, :], ALU.mult).then_inc(f["prod"], 1)
                if first_group and n == 1:
                    fn_lo(dve, L, PAIRS - 1, 1)
                dve.wait_ge(f["prod"], 1 + 4 * r + n + 1)
                dve.wait_ge(f["up"], 1 + 4 * r + n + 1)
                dve.tensor_tensor(act32[n % 2][:, :], ps[:, 2 * (n % 2) + 1, :], sig[:, n % 2, :],
                                  ALU.mult).then_inc(f["act"][n % 2], 1)
                dve.wait_ge(f["a_hi"], 1 + 4 * r + n + 1)
                hs = slice(h * HALF, (h + 1) * HALF)
                dve.tensor_tensor(a[1][:, t, hs], act32[n % 2][:, :], a[0][:, t, hs].bitcast(F32),
                                  ALU.subtract).then_inc(f["a_lo"], 1)
            if first_group:
                dve.wait_ge(f["spilled"], 16 * TILES * (L + 1))
            for n in range(2 * TILES):
                j, c = n // 2, n % 2
                dve.wait_ge(f["down"], 1 + 16 * r + n + 1)
                dst = H[:, j * D + c * HALF:j * D + (c + 1) * HALF]
                if first_group:
                    dve.tensor_copy(dst, ps[:, 4 + n % 4, :]).then_inc(f["summed"][n % 4], 1)
                else:
                    dve.tensor_tensor(dst, dst, ps[:, 4 + n % 4, :], ALU.add).then_inc(f["summed"][n % 4], 1)
                if not last_group and n in (4, 7, 10, 13):
                    u = (n - 4) // 3
                    cut_lo(dve, base, u, *gu_dst(L, u), g + 1)
                if last_group and between:
                    between(n)

        def ffn_post_act(act, L, j):
            f, n0 = F, TILES * L
            for n in (2 * j, 2 * j + 1):
                act.wait_ge(f["summed"][n % 4], 1 + 4 * (GROUPS * (L + 1) - 1) + n // 4 + 1)
            if n0 + j >= 1:
                act.wait_ge(f["mean2"], n0 + j)
            junk = FW[L]["wu"][1][:, KD // 2:, :].rearrange("p k n -> p (k n)")
            act.activation(junk, H[:, j * D:(j + 1) * D], ACT.Square, scale=D ** -0.5,
                           accum_out=ssum2[0]).then_inc(f["ssum2"], 1)

        def ffn_post_rms(pool, L, j):
            f, n0 = F, TILES * L
            pool.wait_ge(f["ssum2"], n0 + j + 1)
            if n0 + j >= 1:
                pool.wait_ge(f["rstd2"], n0 + j)
            pool.tensor_tensor(mean2[0], ssum2[0], eps, ALU.add).then_inc(f["mean2"], 1)
            pool.wait_ge(f["mean2"], n0 + j + 1)
            if n0 + j >= 1:
                pool.wait_ge(f["scaled"], n0 + j)
            pool.tensor_tensor(rstd2[0], mean2[0], minus_half, ALU.pow).then_inc(f["rstd2"], 1)

        def ffn_post_scale(dve, L, j):
            f, n0 = F, TILES * L
            dve.wait_ge(f["rstd2"], n0 + j + 1)
            dve.wait_ge(post_gain_loaded, 16 * POSTG[f"ffn{L}"])
            Hj = H[:, j * D:(j + 1) * D]
            dve.scalar_tensor_tensor(out=Hj, in0=Hj, scalar=rstd2[0], in1=post_gain[:, :],
                                     op0=ALU.mult, op1=ALU.mult).then_inc(f["scaled"], 1)

        def ffn_post_add(pool, L, j):
            f, n0 = F, TILES * L
            Hj = H[:, j * D:(j + 1) * D]
            pool.wait_ge(f["back"][j], 16 * (L + 1))
            pool.wait_ge(f["scaled"], n0 + j + 1)
            pool.tensor_tensor(Hj, Hj, back[j][:, :], ALU.add).then_inc(post_added[L], 1)

        w_pg = [(X[f"w_ple_gate{L}_hi"], X[f"w_ple_gate{L}_lo"]) for L, X in enumerate((A, B))]
        w_pp = [(X[f"w_ple_proj{L}_hi"], X[f"w_ple_proj{L}_lo"]) for L, X in enumerate((B, A))]
        pT = [[(X[f"pT{p}_{L}_hi"], X[f"pT{p}_{L}_lo"]) for p in range(2)] for L, X in enumerate((B, A))]
        p_raw = [[X[f"p_raw{p}_{L}"] for p in range(2)] for L, X in enumerate((B, A))]
        ple_sig = E["ple_sig"]
        G = {
            "gate": [sem_c(f"ple_gate_ready{c}") for c in range(2)],
            "proj": sem_c("ple_proj_ready0"),
            "sig": [sem_c(f"ple_sigmoid_done{c}") for c in range(2)],
            "prod": [sem_c(f"ple_gated{c}") for c in range(2)],
        }

        def ple_pe(pe, L, i, p):
            g, s, t = G, S[f"ple{L}"], TILES * L + 2 * i + p
            pe.wait_ge(s["lo"][p], s.done("lo", i))
            first_tile = isinstance(i, int) and i == 0 and p == 0

            def gate(c, k):
                return product(pe, ps[:, 2 + 2 * p + c, :], [x[p][:, k, :] for x in (xt_hi, xt_lo)],
                               [x[:, k, c * HALF:(c + 1) * HALF] for x in w_pg[L]], k == 0, k == KD - 1)

            if first_tile:
                for k in range(KD):
                    pe.wait_ge(w_ready, BASE[f"ple{L}"] + k + 1)
                    for c in range(2):
                        last = gate(c, k)
                        if k == KD - 1:
                            last.then_inc(g["gate"][c], 1)
            else:
                for c in range(2):
                    if not isinstance(i, int) or i > 0:
                        pe.wait_ge(g["sig"][c], free(t - 1))
                    for k in range(KD):
                        last = gate(c, k)
                    last.then_inc(g["gate"][c], 1)
            pe.wait_ge(s["p_lo"][p], s.done("p_lo", i))
            pe.wait_ge(w_ready, BASE[f"ple{L}"] + 10)
            for c in range(2):
                pe.wait_ge(g["prod"][c], free(t))
                for k in range(2):
                    last = product(pe, ps[:, 6 + c, :], [x[:, k, :] for x in pT[L][p]],
                                   [x[:, k, c * HALF:(c + 1) * HALF] for x in w_pp[L]], k == 0, k == 1)
                last.then_inc(g["proj"] if c == 0 else s["used"][p], 1)

        def ple_act(act, L, i, p):
            g, t = G, TILES * L + 2 * i + p
            if isinstance(i, int) and i == 0 and p == 0:
                act.wait_ge(post_added[L], 1 + TILES)
            for c in range(2):
                act.wait_ge(g["gate"][c], done(t))
                act.wait_ge(g["prod"][c], free(t))
                act.activation(ple_sig[:, c, :], ps[:, 2 + 2 * p + c, :], ACT.Sigmoid).then_inc(g["sig"][c], 1)

        def ple_dve(dve, L, i, p):
            g, s, t = G, S[f"ple{L}"], TILES * L + 2 * i + p
            if isinstance(i, int) and i == 0 and p == 0:
                dve.wait_ge(post_added[L], 1 + TILES)
            dve.wait_ge(ple_added[L], 1 + 2 * (2 * i + p))
            for c in range(2):
                dve.wait_ge(g["sig"][c], done(t))
                if c == 0:
                    dve.wait_ge(g["proj"], done(t))
                else:
                    dve.wait_ge(s["used"][p], s.done("used", i))
                dve.tensor_tensor(tmp[:, c * HALF:(c + 1) * HALF], ps[:, 6 + c, :], ple_sig[:, c, :],
                                  ALU.mult).then_inc(g["prod"][c], 1)
            for c in range(2):
                dve.wait_ge(g["prod"][c], done(t))
                dst = H[:, bass.ds((2 * i + p) * D + c * HALF, HALF)]
                dve.tensor_tensor(dst, dst, tmp[:, c * HALF:(c + 1) * HALF], ALU.add).then_inc(ple_added[L], 1)

        def p_load(sp, L, i, p):
            s = S[f"ple{L}"]
            sp.wait_ge(s["p_lo"][p], s.free("p_lo", i))
            sp.dma_start(p_raw[L][p][:, :, :], I["pT"][L].rearrange("(k c) t -> c k t", c=P)[:, :, bass.ds((2 * i + p) * P, P)]
                         ).then_inc(p_loaded[L][p], 16)

        def p_hi(act, L, i, p):
            s = S[f"ple{L}"]
            act.wait_ge(p_loaded[L][p], 16 * i + 16)
            act.wait_ge(s["used"][p], s.free("used", i))
            act.activation(pT[L][p][0][:, :, :], p_raw[L][p][:, :, :], ACT.Copy).then_inc(s["p_hi"][p], 1)

        def p_lo(dve, L, i, p):
            s = S[f"ple{L}"]
            dve.wait_ge(s["p_hi"][p], s.done("p_hi", i))
            dve.tensor_tensor(pT[L][p][1][:, :, :], p_raw[L][p][:, :, :], pT[L][p][0][:, :, :].bitcast(F32),
                              ALU.subtract).then_inc(s["p_lo"][p], 1)

        w_kv = (B["w_kv_hi"], B["w_kv_lo"])
        k_rot, rope_a, rope_b = E["k_rot"], E["rope_a"], E["rope_b"]
        s_kv = S["kv"]
        k_copied = [sem_c(f"kv_k_copied{p}") for p in range(2)]
        v_copied = sem("v_copied")
        rope_step = sem("rope_step")
        kv_zeroed = sem("kv_zeroed")
        q_zeroed = sem("q_zeroed")

        def kv_dst(j):
            k, c = 4 * (j % 2), GROUP * (j // 2)
            return [w[:, k:k + 4, c:c + GROUP] for w in w_kv]

        def kv_pe(pe, i, p):
            s = s_kv
            pe.wait_ge(s["lo"][p], s.done("lo", i))
            pe.wait_ge(s["rotated"][p], s.free("rotated", i))
            for k in range(KD):
                last = product(pe, ps[:, 2 + p, :], [x[p][:, k, :] for x in (xt_hi, xt_lo)],
                               [x[:, k, :] for x in w_kv], k == 0, k == KD - 1)
            last.then_inc(s["used"][p], 1)

        def kv_turn(pe, i, p):
            s = s_kv
            pe.wait_ge(s["rotated"][p], s.done("rotated", i))
            pe.wait_ge(k_copied[p], free(i))
            for n in range(KV_HEADS):
                last = pe.transpose(ps[:, 6 + p, n * P:(n + 1) * P], k_rot[:, n, :, :].rearrange("p a b -> p (a b)"),
                                    ident[:, :])
            last.then_inc(s["k_turned"][p], 1)

        def kv_act(act, i, p):
            act.wait_ge(s_kv["k_turned"][p], s_kv.done("k_turned", i))
            act.activation(kT[:, bass.ds(2 * i + p + 1, 1), :, :].rearrange("p a b c -> p (a b c)"),
                           ps[:, 6 + p, :], ACT.Copy).then_inc(k_copied[p], 1)

        def rope(dve, base, src1, src2, c, s, dst1, dst2, ta, tb, bank_read, n=1):
            dve.tensor_tensor(ta, src1, c, ALU.mult).then_inc(rope_step, 1)
            dve.tensor_tensor(tb, src2, s, ALU.mult).then_inc(rope_step, 1)
            dve.wait_ge(rope_step, base + 2)
            dve.tensor_tensor(dst1[0], dst1[1](ta), dst1[1](tb), ALU.subtract).then_inc(rope_step, 1)
            dve.wait_ge(rope_step, base + 3)
            dve.tensor_tensor(ta, src2, c, ALU.mult).then_inc(rope_step, 1)
            dve.tensor_tensor(tb, src1, s, ALU.mult).then_inc(rope_step, 1)
            dve.wait_ge(rope_step, base + 5)
            dve.tensor_tensor(dst2[0], dst2[1](ta), dst2[1](tb), ALU.add).then_inc(bank_read, 1)

        def table(name, i, p, heads):
            return B[name][:, bass.ds(2 * i + p, 1), :].to_broadcast([P, heads, 32])

        def kv_dve(dve, i, p):
            s = s_kv
            dve.wait_ge(s["used"][p], s.done("used", i))
            dve.tensor_copy(V[:, bass.ds(2 * i + p + 1, 1), :].rearrange("p a b -> p (a b)"),
                            ps[:, 2 + p, GROUP:2 * GROUP]).then_inc(v_copied, 1)
            dve.wait_ge(s["k_turned"][1 - p], s.done("k_turned", i) if p else s.free("k_turned", i))
            k4 = ps[:, 2 + p, 0:GROUP].rearrange("p (h d) -> p h d", d=HEAD)
            ta = rope_a[:, 0:128].rearrange("p (h d) -> p h d", d=32)
            tb = rope_b[:, 0:128].rearrange("p (h d) -> p h d", d=32)
            dve.wait_ge(s["rotated"][1 - p], s.done("rotated", i) if p else s.free("rotated", i))
            twice = lambda x: x.unsqueeze(2).to_broadcast([P, KV_HEADS, 2, 32])
            rope(dve, (2 * i + p) * 5, k4[:, :, 0:32], k4[:, :, 32:64], table("cos", i, p, KV_HEADS),
                 table("sin", i, p, KV_HEADS), (k_rot[:, :, :, 0:32], twice), (k_rot[:, :, :, 32:64], twice),
                 ta, tb, s["rotated"][p])

        w_q = (A["w_q_hi"], A["w_q_lo"])
        s_q = S["q"]
        q_out = [sem_c(f"q_out_ready{c}") for c in range(2)]
        q_rot = [sem_c(f"q_rotated{c}") for c in range(2)]
        q_turned, q_copied = sem_c("q_turned"), sem_c("q_copied")

        def q_pe(pe, i, p, halves):
            t = 2 * i + p
            pe.wait_ge(s_q["lo"][p], s_q.done("lo", i))
            for c in halves:
                if not isinstance(i, int) or i > 0:
                    pe.wait_ge(q_rot[c], free(t - 1))
                elif p == 0:
                    pe.wait_ge(s_kv["rotated"][c], s_kv.done("rotated", PAIRS - 1))
                for k in range(KD):
                    if isinstance(i, int) and i == 0 and p == 0:
                        pe.wait_ge(w_ready, BASE["q"] + k + 1)
                    last = product(pe, ps[:, 2 + 2 * p + c, :], [x[p][:, k, :] for x in (xt_hi, xt_lo)],
                                   [x[:, k, c * HALF:(c + 1) * HALF] for x in w_q], k == 0, k == KD - 1)
                last.then_inc(q_out[c] if c == 0 else s_q["used"][p], 1)

        def q_turn(pe, i, p):
            t = 2 * i + p
            for c in range(2):
                pe.wait_ge(q_rot[c], done(t))
            pe.wait_ge(q_copied, free(t))
            if isinstance(i, int) and i == 0 and p == 0:
                for par in range(2):
                    pe.wait_ge(k_copied[par], done(PAIRS - 1))
            for k in range(KD):
                last = pe.transpose(banks(6)[:, k * P:(k + 1) * P], tmp[:, k * P:(k + 1) * P], ident[:, :])
            last.then_inc(q_turned, 1)

        def q_act(act, i, p):
            t = 2 * i + p
            act.wait_ge(q_turned, done(t))
            act.activation(qo[:, bass.ds(t, 1), :].rearrange("p a b -> p (a b)"), banks(6), ACT.Copy).then_inc(q_copied, 1)

        def q_dve(dve, i, p):
            t = 2 * i + p
            for c in range(2):
                if c == 0:
                    dve.wait_ge(q_out[0], done(t))
                    if isinstance(i, int) and i == 0 and p == 0:
                        dve.wait_ge(s_kv["rotated"][1], s_kv.done("rotated", PAIRS - 1))
                    dve.wait_ge(q_turned, free(t))
                    dve.wait_ge(q_rot[1], free(t))
                else:
                    dve.wait_ge(s_q["used"][p], s_q.done("used", i))
                    dve.wait_ge(q_rot[0], done(t))
                h8 = ps[:, 2 + 2 * p + c, :].rearrange("p (h d) -> p h d", d=HEAD)
                o8 = tmp[:, c * HALF:(c + 1) * HALF].rearrange("p (h d) -> p h d", d=HEAD)
                ta, tb = [x[:, :].rearrange("p (h d) -> p h d", d=32) for x in (rope_a, rope_b)]
                same = lambda x: x
                rope(dve, 5 * TILES + (2 * t + c) * 5, h8[:, :, 0:32], h8[:, :, 32:64], table("cos", i, p, 8),
                     table("sin", i, p, 8), (o8[:, :, 0:32], same), (o8[:, :, 32:64], same), ta, tb, q_rot[c])

        s_a = S["att"]
        q_tile = [DD["q_tile0"], DD["q_tile1"]]
        pt = [tmp[:, :].rearrange("p (k c) -> p k c", k=KD), E["pt1"]]
        mask_r, ident_r = B["mask_r"], B["ident_r"]
        o_ready, o_out = sem_c("o_ready"), sem_c("o_read_out")
        sink_dve, sink_act = sem_c("sink_gap_done"), sem_c("sink_exp_done")
        neg_sinks_set = sem("neg_sinks_set")
        sums_read = [sem_c(f"sums_read{p}") for p in range(2)]
        recip_done = sem("recip_done")

        def scores(pe, i, p, g):
            par, r = g % 2, 4 * i + 2 * p + g // 2
            if g == 0:
                pe.wait_ge(s_a["q_tile"][p], s_a.done("q_tile", i))
            pe.wait_ge(att["probs"][par], att.free("probs", r))
            m2 = mask_r[:, 0 if isinstance(i, int) and i == 0 and p == 0 else 1, :].unsqueeze(1).to_broadcast([P, 2, 2 * P])
            for c in range(2):
                pe.matmul(banks(2 * par)[:, c * HALF:(c + 1) * HALF].rearrange("p (h k) -> p h k", h=2),
                          ident_r[:, :], m2, start=True, stop=False)
            for m in range(GQA):
                h = GQA * g + m
                last = pe.matmul(banks(2 * par)[:, m * 256:(m + 1) * 256].rearrange("p (b c) -> p b c", b=2),
                                 q_tile[p][:, h, :], kT[:, bass.ds(2 * i + p, 2), g, :], start=False, stop=m % 2 == 1)
            last.then_inc(att["scores"][par], 1)

        def softmax_dve(dve, i, p, g):
            par, r = g % 2, 4 * i + 2 * p + g // 2
            dve.wait_ge(att["scores"][par], att.done("scores", r))
            dve.tensor_reduce(neg_row_max[par], banks(2 * par).rearrange("p (h k) -> p h k", h=GQA), AX.X, ALU.max,
                              negate=True).then_inc(att["max"][par], 1)
            dve.wait_ge(att["max"][par], att.done("max", r))
            dve.wait_ge(att["probs"][par], att.free("probs", r))
            gs = slice(GQA * g, GQA * (g + 1))
            dve.scalar_tensor_tensor(out=neg_max[par], in0=neg_row_max[par], scalar=HEAD ** -0.5, in1=neg_sinks[:, gs],
                                     op0=ALU.mult, op1=ALU.min).then_inc(att["neg_max"][par], 1)
            dve.wait_ge(att["neg_max"][par], att.done("neg_max", r))
            dve.tensor_tensor(sink_gap[par], sinks[:, gs], neg_max[par], ALU.add).then_inc(sink_dve, 1)

        def q_to_place(act, i, p, halves=(0, 1)):
            if isinstance(i, int) and i == 0:
                act.wait_ge(q_zeroed, p + 1)
                act.wait_ge(q_copied, done(p))
            else:
                act.wait_ge(att["scores"][1], 1 + 4 * i + 2 * p - 2)
            for r in halves:
                part = slice(HEAD * r, HEAD * (r + 1))
                last = act.activation(q_tile[p][part, :, :].rearrange("p (k r) c -> p k r c", r=2)[:, :, r, :],
                                      qo[part, bass.ds(2 * i + p, 1), :].rearrange("p a (k c) -> p (a k) c", c=P),
                                      ACT.Copy)
            if 1 in halves:
                last.then_inc(s_a["q_tile"][p], 1)

        def softmax_act(act, i, p, g):
            par, r = g % 2, 4 * i + 2 * p + g // 2
            act.wait_ge(att["neg_max"][par], att.done("neg_max", r))
            act.wait_ge(att["p_turned"][par], att.free("p_turned", r))
            if g == 0:
                act.wait_ge(sums_read[p], free(i))
            act.wait_ge(sink_dve, done(4 * (2 * i + p) + g))
            act.activation(sink_exp[p][:, GQA * g:GQA * (g + 1)], sink_gap[par], ACT.Exp).then_inc(sink_act, 1)
            for m in range(GQA):
                sl = slice(m * 256, (m + 1) * 256)
                last = act.activation(xn[par][:, sl], banks(2 * par)[:, sl], ACT.Exp, scale=HEAD ** -0.5,
                                      bias=neg_max[par][:, m:m + 1],
                                      accum_out=sums[p][:, GQA * g + m:GQA * g + m + 1])
            last.then_inc(att["probs"][par], 1)

        def turn_probs(pe, i, p, g):
            par, r = g % 2, 4 * i + 2 * p + g // 2
            pe.wait_ge(att["probs"][par], att.done("probs", r))
            before = r - 1 if par == 0 else r
            pe.wait_ge(att["pt"][1 - par], att.done("pt", before))
            for k in range(8):
                last = pe.transpose(banks(4)[:, k * P:(k + 1) * P], xn[par][:, k * P:(k + 1) * P], ident[:, :])
            last.then_inc(att["p_turned"][par], 1)

        def probs_copy(dve, i, p, g):
            par, r = g % 2, 4 * i + 2 * p + g // 2
            dve.wait_ge(att["p_turned"][par], att.done("p_turned", r))
            dve.wait_ge(att["pv"][par], att.free("pv", r))
            dve.tensor_copy(pt[par][:, :, :].rearrange("p a b -> p (a b)"), banks(4)).then_inc(att["pt"][par], 1)

        def values(pe, i, p, g):
            par, r = g % 2, 4 * i + 2 * p + g // 2
            pe.wait_ge(att["pt"][par], att.done("pt", r))
            if isinstance(i, int) and i == 0 and p == 0 and g == 0:
                pe.wait_ge(q_copied, 1 + TILES)
            if g == 0:
                pe.wait_ge(o_out, free(2 * i + p))
            for m in range(GQA):
                h = GQA * g + m
                for b in range(2):
                    last = pe.matmul(banks(6)[:, h * HEAD:(h + 1) * HEAD], pt[par][:, 2 * m + b, :],
                                     V[:, bass.ds(2 * i + p + b, 1), g * HEAD:(g + 1) * HEAD].rearrange("p a b -> p (a b)"),
                                     start=(b == 0), stop=(b == 1))
            last.then_inc(att["pv"][par], 1)

        def att_recip(dve, i, p):
            t = 2 * i + p
            dve.wait_ge(sink_act, done(4 * t + 3))
            dve.wait_ge(att["probs"][1], att.done("probs", 4 * i + 2 * p + 1))
            dve.wait_ge(o_out, free(t))
            dve.tensor_tensor(recip[:, :], sums[p][:, :], sink_exp[p][:, :], ALU.add).then_inc(sums_read[p], 1)
            dve.wait_ge(sums_read[p], done(i))
            dve.reciprocal(recip[:, :], recip[:, :]).then_inc(recip_done, 1)

        def att_out(dve, i, p):
            t = 2 * i + p
            dve.wait_ge(att["pv"][1], att.done("pv", 4 * i + 2 * p + 1))
            dve.wait_ge(recip_done, t + 1)
            dve.wait_ge(s_a["q_tile"][p], s_a.done("q_tile", i))
            dve.tensor_tensor(qo[:, bass.ds(t, 1), :].rearrange("p a (h d) -> p (a h) d", d=HEAD),
                              banks(6).rearrange("p (h d) -> p h d", d=HEAD),
                              recip[:, :].unsqueeze(2).to_broadcast([P, HEADS, HEAD]), ALU.mult).then_inc(o_out, 1)

        w_o = (A["w_o_hi"], A["w_o_lo"])
        s_o = S["o"]

        def o_pe(pe, i, p):
            pe.wait_ge(s_o["lo"][p], s_o.done("lo", i))
            pe.wait_ge(s_o["added"][p], s_o.free("added", i))
            for c in range(2):
                for k in range(KD):
                    if isinstance(i, int) and i == 0 and p == 0 and c == 0:
                        pe.wait_ge(w_ready, BASE["o"] + k + 1)
                    last = product(pe, ps[:, 2 + 2 * p + c, :], [x[p][:, k, :] for x in (xt_hi, xt_lo)],
                                   [x[:, k, c * HALF:(c + 1) * HALF] for x in w_o], k == 0, k == KD - 1)
            last.then_inc(s_o["used"][p], 1)

        block = ctx.enter_context(nc.Block())

        @block.sync
        def _(sp):
            x_t = I["x"].rearrange("b (t p) d -> p (b t) d", p=P)

            def x_load(t):
                sp.dma_start(H[:, t * D:(t + 1) * D], x_t[:, t, :]).then_inc(x_loaded[t], 16)

            x_load(0)
            sp.dma_start(B["band_first"][:, :, :], I["band_first"]).then_inc(first_consts_loaded, 16)
            w = I["pool_w"][0].rearrange("g c n -> (g c) n")
            for j in range(2):
                load_unit(sp, BASE["pool"], j, quarter(w, j))
            x_load(1)
            for name in ("band_inner", "band_before"):
                sp.dma_start(B[name][:, :, :], I[name]).then_inc(pool_consts_loaded, 16)
            x_load(2)
            sp.dma_start(ident[:, :], I["identity"]).then_inc(pool_consts_loaded, 16)
            for t in range(3, TILES):
                x_load(t)
            sp.dma_start(sinks[:, :], I["sinks"][0].partition_broadcast(P)).then_inc(consts_loaded, 16)
            for t in range(TILES):
                sp.wait_ge(x_loaded[t], 16)
                sp.sem_inc(x_arrived, 1)

            def ffn_loads(L):
                f, base = F, BASE[f"ffn{L}"]
                gate = I["w_ff_gate"][L].rearrange("(k p) n -> p k n", p=P)
                up = I["w_ff_up"][L].rearrange("(k p) n -> p k n", p=P)

                def group(g):
                    for j, w in enumerate((gate, gate, up, up)):
                        k = 4 * (j % 2)
                        load_unit(sp, base, j, w[:, k:k + 4, bass.ds(g * GROUP, GROUP)], g)
                    for t in range(2):
                        load_unit(sp, base, 4 + t, I["w_ff_down"][L][bass.ds((2 * g + t) * P, P), :], g)

                group(0)
                s = S[("pool", "o")[L]]
                for j in range(TILES):
                    sp.wait_ge(s["added"][j % 2], s.done("added", j // 2))
                    sp.dma_start(spill[L][:, j * D:(j + 1) * D], H[:, j * D:(j + 1) * D]).then_inc(f["spilled"], 16)
                with sp.Fori(1, GROUPS) as g:
                    group(g)
                for k in range(SLOTS):
                    load_unit(sp, BASE[f"ple{L}"], k, rows(I["w_ple_gate"][L], k))
                sp.wait_ge(f["spilled"], 16 * TILES * (L + 1))
                sp.wait_ge(FN["turned"], 1 + TILES * (L + 1))
                for j in range(5):
                    load_back(L, j)

            def load_back(L, j):
                if j >= 5:
                    sp.wait_ge(post_added[L], 1 + (j - 3 + 1))
                sp.dma_start(back[j][:, :], spill[L][:, j * D:(j + 1) * D]).then_inc(F["back"][j], 16)

            def ple_loads(L):
                base = BASE[f"ple{L}"]
                sp.wait_ge(F["up"], 1 + 4 * GROUPS * (L + 1))
                for p in range(2):
                    p_load(sp, L, 0, p)
                for k in range(SLOTS, KD):
                    load_unit(sp, base, k, rows(I["w_ple_gate"][L], k))
                load_back(L, 5)
                load_unit(sp, base, KD, rows(I["w_ple_proj"][L], 0))
                load_back(L, 6)
                load_unit(sp, base, KD + 1, rows(I["w_ple_proj"][L], 1))
                load_back(L, 7)
                with sp.Fori(1, PAIRS) as i:
                    for p in range(2):
                        p_load(sp, L, i, p)

            ffn_loads(0)
            ple_loads(0)
            for j in range(4):
                load_unit(sp, BASE["kv"], j, quarter(I["w_k"] if j < 2 else I["w_v"], j % 2))
            load_unit(sp, BASE["mask"], 0, I["mask_unit"])
            for p in range(2):
                sp.wait_ge(S["ple0"]["used"][p], S["ple0"].done("used", PAIRS - 1))
            for name, dst in (("rope_cos", B["cos"][:, :, :]), ("rope_sin", B["sin"][:, :, :])):
                sp.dma_start(dst, I[name]).then_inc(consts_loaded, 16)
            for k in range(KD):
                load_unit(sp, BASE["q"], k, rows(I["w_q"][0], k))
            for k in range(KD):
                load_unit(sp, BASE["o"], k, rows(I["w_o"][0], k))
            ffn_loads(1)
            ple_loads(1)
            o_t = out.rearrange("b (t p) d -> p (b t) d", p=P)
            for t in range(TILES):
                sp.wait_ge(ple_added[1], 1 + 2 * (t + 1))
                sp.dma_start(o_t[:, t, :], H[:, t * D:(t + 1) * D]).then_inc(stored, 16)
            sp.wait_ge(stored, 16 * TILES)

        @block.gpsimd
        def _(pool):
            for s in credited:
                pool.sem_inc(s, 1)
            pool.memset(minus_half, -0.5).then_inc(consts_set, 1)
            pool.memset(eps, EPS).then_inc(consts_set, 1)
            pool.wait_ge(consts_set, 2)

            def rms(name):
                return lambda i, p: inv_rms(pool, S[name], i, p, ssum[p], mean[p], rstd[p])

            def rms_post(name):
                return lambda i, p: inv_rms(pool, S[name], i, p, ssum2[p], mean2[p], rstd2[p], ("ssum2", "mean2", "rstd2"))

            def fn(L):
                return lambda i, p: fn_rms(pool, L, i, p)

            def ffn(L):
                fn_rms(pool, L, PAIRS - 1, 1)
                ffn_post_rms(pool, L, 0)
                for j in range(1, TILES):
                    ffn_post_rms(pool, L, j)
                    ffn_post_add(pool, L, j - 1)
                    if j in (3, 4):
                        rms(f"ple{L}")(0, j - 3)
                ffn_post_add(pool, L, TILES - 1)

            staggered(pool, [(2, rms("pool")), (-1, fn(0)), (0, rms_post("pool"))], tail=False)
            ffn(0)
            staggered(pool, [(2, rms("ple0"))], after=[(2, rms("kv"))], head=False)
            for p in range(2):
                pool.wait_ge(S["ple0"]["used"][p], S["ple0"].done("used", PAIRS - 1))
            pool.memset(kT[:, 0, :, :], 0.0).then_inc(kv_zeroed, 1)
            pool.memset(V[:, 0, :], 0.0).then_inc(kv_zeroed, 1)
            staggered(pool, [(2, rms("kv"))], after=[(2, rms("q"))], head=False)
            staggered(pool, [(2, rms("q"))], head=False)

            for p in range(2):
                pool.wait_ge(s_q["used"][p], s_q.done("used", PAIRS - 1))
                pool.memset(q_tile[p][:, :, :], 0.0).then_inc(q_zeroed, 1)

            def o_copy(i, p):
                if isinstance(i, int) and i == 0:
                    return
                pool.wait_ge(s_o["turned"][p], s_o.free("turned", i))
                pool.wait_ge(o_out, 1 + TILES)
                pool.tensor_copy(xn[p][:, :], qo[:, bass.ds(2 * i + p, 1), :].rearrange("p a b -> p (a b)")
                                 ).then_inc(s_o["xn"][p], 1)

            staggered(pool, [(2, o_copy), (-1, fn(1)), (0, rms_post("o"))], tail=False)
            ffn(1)
            staggered(pool, [(2, rms("ple1"))], head=False)

        @block.scalar
        def _(act):
            def gain_row(name, src):
                row_load(act, gain, src, gain_loaded)

            row_load(act, B["pool_gain"], I["mix_pre_g"][0], first_consts_loaded)
            row_load(act, B["scale_row"], I["pool_scale"][0], first_consts_loaded)
            def gate_cut(L):
                def cut(i, p):
                    if L == 1:
                        act.wait_ge(s_o["used"][1], s_o.done("used", PAIRS - 1))
                    for j in range((4, 2)[L]):
                        cut_hi(act, BASE[f"ffn{L}"], j, gu_dst(L, j)[0])
                return at_last(cut)

            s = s_pool

            def pool_cut(i, p):
                for j in range(2):
                    act.wait_ge(w_pool_scaled, j + 1)
                    cut_hi(act, BASE["pool"], j, w_pool[0][:, 4 * j:4 * j + 4, :])
                row_load(act, post_gain, I["mix_post_g"][0], post_gain_loaded)
                gain_row("ffn0", I["ffn_pre_g"][0])

            staggered(act, [(2, lambda i, p: pool_square_sum(act, i, p)), (2, at_first(pool_cut)),
                            (1, lambda i, p: slot_hi(act, s, i, p)),
                            (0, gate_cut(0)), (-2, lambda i, p: fn_hi(act, 0, i, p)),
                            (-1, lambda i, p: fn_squares(act, 0, i, p)),
                            (0, lambda i, p: output_squares(act, s, i, p))], tail=False)

            def ffn(L):
                f, base, s_before, s_ple = F, BASE[f"ffn{L}"], S[("pool", "o")[L]], S[f"ple{L}"]
                if L == 1:
                    for j in range(2, 4):
                        cut_hi(act, base, j, gu_dst(L, j)[0])
                fn_squares(act, L, PAIRS - 1, 1)
                fn_hi(act, L, PAIRS - 1, 0)
                ffn_act(act, L, 0, False, first_group=True)
                gain_row(f"ple{L}", I["ple_norm_g"][L])
                row_load(act, post_gain, I["ffn_post_g"][L], post_gain_loaded)
                with act.Fori(1, GROUPS - 1) as g:
                    ffn_act(act, L, g, False)
                ffn_act(act, L, GROUPS - 1, True)
                act.wait_ge(f["up"], 1 + 4 * GROUPS * (L + 1))
                for k in range(4):
                    cut_hi(act, BASE[f"ple{L}"], k, w_pg[L][0][:, k, :])
                for j in range(TILES):
                    ffn_post_act(act, L, j)
                    if j in (3, 4):
                        t = j - 3
                        act.wait_ge(post_added[L], 1 + t + 1)
                        square_sum(act, s_ple, 0, t)
                    if j == 6:
                        slot_hi(act, s_ple, 0, 0)
                for k in range(4, KD):
                    cut_hi(act, BASE[f"ple{L}"], k, w_pg[L][0][:, k, :])
                for k in range(2):
                    cut_hi(act, BASE[f"ple{L}"], KD + k, w_pp[L][0][:, k, :])
                p_hi(act, L, 0, 0)

            def ple(L):
                name = f"ple{L}"
                s = S[name]

                def ready(act, i, p):
                    act.wait_ge(post_added[L], 1 + TILES)

                def cuts(i, p):
                    if L == 0 and isinstance(i, int) and i == PAIRS - 1:
                        for j in (2 * p, 2 * p + 1):
                            cut_hi(act, BASE["kv"], j, kv_dst(j)[0])

                def second_slot(i, p):
                    if isinstance(i, int) and i == 0 and p == 1:
                        act.wait_ge(post_added[L], 1 + TILES)
                    slot_hi(act, s, i, p)

                staggered(act, [(1, second_slot), (1, lambda i, p: p_hi(act, L, i, p)),
                                (2, lambda i, p: square_sum(act, s, i, p, ready)), (0, cuts),
                                (0, lambda i, p: ple_act(act, L, i, p))],
                          after=kv_parts if L == 0 else (), head=False)

            def next_gain(name, row, s_before):
                def load(i, p):
                    for par in range(2):
                        act.wait_ge(s_before["xn"][par], s_before.done("xn", PAIRS - 1))
                    gain_row(name, row)
                return at_first(load)

            def ready(act, i, p):
                act.wait_ge(ple_added[0], 3 + 2 * (2 * i + p))

            def q_cut(i, p):
                if isinstance(i, int) and i == 0 and p == 0:
                    cut_hi(act, BASE["mask"], 0, mask_r[:, :, :].rearrange("p m k -> p (m k)"), columns=slice(0, 4 * P))
                if isinstance(i, int):
                    for k in (2 * (i // 3 * 2 + p), 2 * (i // 3 * 2 + p) + 1):
                        cut_hi(act, BASE["q"], k, w_q[0][:, k, :])

            kv_parts = [(1, lambda i, p: slot_hi(act, s_kv, i, p)), (2, next_gain("kv", I["kv_norm_g"], S["ple0"])),
                        (2, lambda i, p: square_sum(act, s_kv, i, p, ready)),
                        (0, q_cut), (-1, lambda i, p: kv_act(act, i, p))]
            q_parts = [(1, lambda i, p: slot_hi(act, s_q, i, p)), (2, next_gain("q", I["mix_pre_g"][1], s_kv)),
                       (2, lambda i, p: square_sum(act, s_q, i, p, ready)), (-1, lambda i, p: q_act(act, i, p))]
            ffn(0)
            ple(0)
            staggered(act, kv_parts, after=q_parts, head=False, tail=False)

            staggered(act, q_parts, before=kv_parts, head=False, tail=False)
            for par in range(2):
                act.wait_ge(s_q["xn"][par], s_q.done("xn", PAIRS - 1))
            gain_row("ffn1", I["ffn_pre_g"][1])

            q_to_place(act, 0, 0)
            softmax_act(act, 0, 0, 0)
            q_act(act, PAIRS - 1, 1)
            softmax_act(act, 0, 0, 1)
            q_to_place(act, 0, 1)

            def att_tile(i, p, more, nxt):
                for g in range(KV_HEADS):
                    if g >= 2 and not (isinstance(i, int) and i == PAIRS - 1):
                        q_to_place(act, i + 1, p, halves=[g - 2])
                    if isinstance(i, int) and g < 2:
                        k = 4 * (i // 3) + 2 * p + g
                        cut_hi(act, BASE["o"], k, w_o[0][:, k, :])
                    if g < 2:
                        softmax_act(act, i, p, g + 2)
                    elif more:
                        softmax_act(act, *nxt, g - 2)

            def att_body(i, last):
                att_tile(i, 0, True, (i, 1))
                att_tile(i, 1, not last, (i + 1, 0))

            over_pairs(act, att_body)

            def o_first_copies(i, p):
                if isinstance(i, int) and i == 0:
                    act.wait_ge(att["p_turned"][p], att.done("p_turned", 2 * TILES - 1))
                    act.wait_ge(o_out, done(p))
                    act.activation(xn[p][:, :], qo[:, p, :], ACT.Copy).then_inc(s_o["xn"][p], 1)

            def o_gain(i, p):
                act.wait_ge(o_out, 1 + TILES)
                row_load(act, post_gain, I["mix_post_g"][1], post_gain_loaded)

            staggered(act, [(2, o_first_copies), (1, lambda i, p: slot_hi(act, s_o, i, p)),
                            (-1, lambda i, p: fn_squares(act, 1, i, p)), (0, at_first(o_gain)),
                            (0, gate_cut(1)), (0, lambda i, p: output_squares(act, s_o, i, p)),
                            (-2, lambda i, p: fn_hi(act, 1, i, p))], tail=False)
            ffn(1)
            ple(1)

        @block.vector
        def _(dve):
            def gate_cut(L):
                return at_last(lambda i, p: [cut_lo(dve, BASE[f"ffn{L}"], j, *gu_dst(L, j)) for j in range((4, 2)[L])])

            s = s_pool
            dve.wait_ge(first_consts_loaded, 48)

            def pool_cut(i, p):
                for j in range(2):
                    dve.wait_ge(*loaded(BASE["pool"], j))
                    w = raw[(BASE["pool"] + j) % SLOTS][:, :].rearrange("p (g k n) -> p g k n", g=2, k=2)
                    scale = B["scale_row"][:, j * HALF:(j + 1) * HALF].rearrange("p (g n) -> p g n", g=2)
                    dve.tensor_tensor(w, w, scale.unsqueeze(2).to_broadcast([P, 2, 2, GROUP]), ALU.mult
                                      ).then_inc(w_pool_scaled, 1)
                for j in range(2):
                    cut_lo(dve, BASE["pool"], j, *[w[:, 4 * j:4 * j + 4, :] for w in w_pool])

            def rows_ready(i, p):
                dve.wait_ge(post_gain_loaded, 16 * POSTG["pool"])
                dve.wait_ge(gain_loaded, 16 * GAIN["ffn0"])

            staggered(dve, [(2, lambda i, p: pool_normed(dve, i, p)), (2, at_first(pool_cut)),
                            (1, lambda i, p: slot_lo(dve, s, i, p)),
                            (0, gate_cut(0)), (-1, at_first(rows_ready)), (-1, lambda i, p: add_post(dve, s, i, p)),
                            (-2, lambda i, p: fn_lo(dve, 0, i, p)),
                            (-1, lambda i, p: fn_normed(dve, 0, i, p))], tail=False)

            def ffn(L):
                f, base, s_before, s_ple = F, BASE[f"ffn{L}"], S[("pool", "o")[L]], S[f"ple{L}"]
                if L == 1:
                    for j in range(2, 4):
                        cut_lo(dve, base, j, *gu_dst(L, j))
                add_post(dve, s_before, PAIRS - 1, 1)
                fn_normed(dve, L, PAIRS - 1, 1)
                fn_lo(dve, L, PAIRS - 1, 0)
                ffn_dve(dve, L, 0, False, first_group=True)
                with dve.Fori(1, GROUPS - 1) as g:
                    ffn_dve(dve, L, g, False)

                def between(n):
                    if n in (1, 3):
                        for k in (n - 1, n):
                            cut_lo(dve, BASE[f"ple{L}"], k, *[w[:, k, :] for w in w_pg[L]])
                    if n >= 3 and n % 2:
                        ffn_post_scale(dve, L, (n - 3) // 2)
                    if n == 11:
                        dve.wait_ge(gain_loaded, 16 * GAIN[f"ple{L}"])
                        normed(dve, s_ple, 0, 0)
                    if n == 13:
                        normed(dve, s_ple, 0, 1)
                        slot_lo(dve, s_ple, 0, 0)

                ffn_dve(dve, L, GROUPS - 1, True, between)
                ffn_post_scale(dve, L, TILES - 1)
                for k in range(4, KD):
                    cut_lo(dve, BASE[f"ple{L}"], k, *[w[:, k, :] for w in w_pg[L]])
                for k in range(2):
                    cut_lo(dve, BASE[f"ple{L}"], KD + k, *[w[:, k, :] for w in w_pp[L]])
                p_lo(dve, L, 0, 0)

            def ple(L):
                s = S[f"ple{L}"]

                def cuts(i, p):
                    if L == 0 and isinstance(i, int) and i == PAIRS - 1:
                        for j in (2 * p, 2 * p + 1):
                            cut_lo(dve, BASE["kv"], j, *kv_dst(j))

                staggered(dve, [(1, lambda i, p: slot_lo(dve, s, i, p)), (1, lambda i, p: p_lo(dve, L, i, p)),
                                (2, lambda i, p: normed(dve, s, i, p)), (0, cuts), (0, lambda i, p: ple_dve(dve, L, i, p))],
                          after=kv_parts if L == 0 else (), head=False)

            def q_cut(i, p):
                if isinstance(i, int) and i == 0 and p == 0:
                    dve.wait_ge(hi_done, BASE["mask"] + 1)
                    dve.tensor_copy(ident_r[:, :], raw[BASE["mask"] % SLOTS][:, 4 * P:5 * P]).then_inc(w_ready, 1)
                if isinstance(i, int):
                    for k in (2 * (i // 3 * 2 + p), 2 * (i // 3 * 2 + p) + 1):
                        cut_lo(dve, BASE["q"], k, *[w[:, k, :] for w in w_q])

            def tables_ready(i, p):
                dve.wait_ge(consts_loaded, 16 * 3)
                dve.wait_ge(kv_zeroed, 2)

            kv_parts = [(1, lambda i, p: slot_lo(dve, s_kv, i, p)),
                        (2, at_first(lambda i, p: dve.wait_ge(gain_loaded, 16 * GAIN["kv"]))),
                        (2, lambda i, p: normed(dve, s_kv, i, p)), (0, q_cut),
                        (0, at_first(tables_ready)), (0, lambda i, p: kv_dve(dve, i, p))]
            q_parts = [(1, lambda i, p: slot_lo(dve, s_q, i, p)),
                       (2, at_first(lambda i, p: dve.wait_ge(gain_loaded, 16 * GAIN["q"]))),
                       (2, lambda i, p: normed(dve, s_q, i, p)), (0, lambda i, p: q_dve(dve, i, p))]
            ffn(0)
            ple(0)
            staggered(dve, kv_parts, after=q_parts, head=False)
            staggered(dve, q_parts, head=False)

            def att_tile(i, p, more, nxt):
                for g in range(KV_HEADS):
                    if g == 0 and p == 1:
                        before = (i, 0)
                    elif g == 0 and not (isinstance(i, int) and i == 0):
                        before = (i - 1, 1)
                    else:
                        before = None
                    if before:
                        att_recip(dve, *before)
                    probs_copy(dve, i, p, g)
                    if before:
                        att_out(dve, *before)
                    if g < 2:
                        softmax_dve(dve, i, p, g + 2)
                    elif more:
                        softmax_dve(dve, *nxt, g - 2)
                    if isinstance(i, int) and g < 2:
                        k = 4 * (i // 3) + 2 * p + g
                        cut_lo(dve, BASE["o"], k, *[w[:, k, :] for w in w_o])

            dve.tensor_scalar(neg_sinks, sinks[:, :], -1.0, None, ALU.mult).then_inc(neg_sinks_set, 1)
            dve.wait_ge(neg_sinks_set, 1)
            softmax_dve(dve, 0, 0, 0)
            softmax_dve(dve, 0, 0, 1)

            def att_body(i, last):
                att_tile(i, 0, True, (i, 1))
                att_tile(i, 1, not last, (i + 1, 0))

            over_pairs(dve, att_body)
            att_recip(dve, PAIRS - 1, 1)
            slot_lo(dve, s_o, 0, 0)
            att_out(dve, PAIRS - 1, 1)

            def rows_ready(i, p):
                dve.wait_ge(post_gain_loaded, 16 * POSTG["o"])
                dve.wait_ge(gain_loaded, 16 * GAIN["ffn1"])

            staggered(dve, [(1, lambda i, p: slot_lo(dve, s_o, i, p)),
                            (-1, at_first(rows_ready)), (-1, lambda i, p: add_post(dve, s_o, i, p)),
                            (0, gate_cut(1)), (-1, lambda i, p: fn_normed(dve, 1, i, p)),
                            (-2, lambda i, p: fn_lo(dve, 1, i, p))], head=False, tail=False)
            ffn(1)
            ple(1)

        @block.tensor
        def _(pe):
            pe.wait_ge(first_consts_loaded, 48)

            def pool_products(i, p):
                s = s_pool
                pe.wait_ge(s["lo"][p], s.done("lo", i))
                pe.wait_ge(s["added"][p], s.free("added", i))
                pe.wait_ge(w_ready, BASE["pool"] + 2)
                for g in range(len(WINDOWS)):
                    for k in range(2):
                        last = product(pe, banks(2 + 2 * p)[:, g * GROUP:(g + 1) * GROUP],
                                       [x[p][:, 2 * g + k, :] for x in (xt_hi, xt_lo)],
                                       [x[:, 2 * g + k, :] for x in w_pool], k == 0, k == 1)
                last.then_inc(s["used"][p], 1)

            staggered(pe, [(1, lambda i, p: pool_band(pe, i, p)), (-2, lambda i, p: fn_turn(pe, 0, i, p)),
                           (0, pool_products)], tail=False)

            def ffn(L):
                ffn_pe(pe, L, 0, first_group=True)
                with pe.Fori(1, GROUPS - 1) as g:
                    ffn_pe(pe, L, g)
                ffn_pe(pe, L, GROUPS - 1, during_down=lambda n: turn(pe, S[f"ple{L}"], 0, 0) if n == 14 else None)

            def turned(s):
                return lambda i, p: turn(pe, s, i, p)

            ffn(0)
            ple_parts = [[(1, turned(S[f"ple{L}"])), (0, lambda i, p, L=L: ple_pe(pe, L, i, p))] for L in range(2)]
            kv_parts = [(1, turned(s_kv)), (0, lambda i, p: kv_pe(pe, i, p)), (-1, lambda i, p: kv_turn(pe, i, p))]
            q_parts = [(1, turned(s_q)), (0, lambda i, p: q_pe(pe, i, p, [0])), (-1, lambda i, p: q_turn(pe, i, p)),
                       (0, lambda i, p: q_pe(pe, i, p, [1]))]
            staggered(pe, ple_parts[0], after=kv_parts, head=False)
            pe.wait_ge(w_ready, BASE["kv"] + 4)
            staggered(pe, kv_parts, after=q_parts, head=False, tail=False)
            staggered(pe, q_parts, before=kv_parts, head=False, tail=False)

            pe.wait_ge(v_copied, TILES)
            pe.wait_ge(w_ready, BASE["mask"] + 1)
            for c in range(2):
                pe.wait_ge(q_rot[c], done(TILES - 2))
            scores(pe, 0, 0, 0)
            scores(pe, 0, 0, 1)
            q_turn(pe, PAIRS - 1, 1)

            def att_tile(i, p, more, nxt):
                for g in range(KV_HEADS):
                    turn_probs(pe, i, p, g)
                    if g < 2:
                        scores(pe, i, p, g + 2)
                    elif more:
                        scores(pe, *nxt, g - 2)
                    elif g == 3:
                        turn(pe, s_o, 0, 0)
                    values(pe, i, p, g)

            def att_body(i, last):
                att_tile(i, 0, True, (i, 1))
                att_tile(i, 1, not last, (i + 1, 0))

            over_pairs(pe, att_body)

            staggered(pe, [(1, turned(s_o)), (0, lambda i, p: o_pe(pe, i, p)),
                           (-2, lambda i, p: fn_turn(pe, 1, i, p))], head=False, tail=False)
            ffn(1)
            staggered(pe, ple_parts[1], head=False)


_INS = ["x", "mix_pre_g", "mix_post_g", "ffn_pre_g", "ffn_post_g", "pool_w", "pool_scale", "kv_norm_g", "w_k", "w_v",
        "w_q", "w_o", "sinks", "w_ff_gate", "w_ff_up", "w_ff_down", "ple_norm_g", "w_ple_gate", "w_ple_proj"]


def kernel(**inputs):
    import numpy as _np
    import concourse.bacc as _bacc
    from concourse import mybir as _mybir
    from concourse.bass_utils import run_bass_kernel_spmd as _run

    nc = _bacc.Bacc("TRN2", target_bir_lowering=False, num_devices=1, dynamic_dma_scratch_size=1024)
    arrays = {name: _np.ascontiguousarray(inputs[name]) for name in _INS}
    p = inputs["p"]
    arrays["pT"] = _np.ascontiguousarray(_np.asarray(p).reshape(p.shape[0], SEQ, PLE).transpose(0, 2, 1))
    arrays.update(constants())
    I = {}
    for name, a in arrays.items():
        I[name] = nc.dram_tensor(f"in_{name}", a.shape, _mybir.dt.from_np(a.dtype), kind="ExternalInput").ap()
    out = nc.dram_tensor("out_0", (1, SEQ, D), F32, kind="ExternalOutput").ap()
    trunk(nc, I, out)
    r = _run(nc, [{f"in_{k}": v for k, v in arrays.items()}], core_ids=[0])
    return r.results[0]["out_0"]
```
